# Optimizing a Trainium2 kernel written in Bass

```python
import jax
import jax.numpy as jnp
from jax import lax
import numpy as np

D_MODEL = 1024
BATCH = 1
SEQ = 128
DEPTH = 2
DEC_BATCH = 1
DEC_SEQ = 512
PAST_LEN = 128

GRID_W = 64
NORM_EPS = 1e-6
D_FF = 4 * D_MODEL
N_EVEN = (DEPTH + 1) // 2
N_ODD = DEPTH // 2

HEAD_DIM = 64
A_HEADS = 8
A_KV_HEADS = 2
A_WIDTH = A_HEADS * HEAD_DIM
A_KV_WIDTH = A_KV_HEADS * HEAD_DIM
Q_BLOCK = 128
ROPE_THETA = 10000.0
ATTN_SCALE = HEAD_DIM ** -0.5

B_HEADS = 8
B_DK = 64
B_DV = 64
B_FDIM = B_HEADS * B_DK
B_VDIM = B_HEADS * B_DV
B_CHUNK = 64

AB_SIZES = (A_WIDTH, A_KV_WIDTH, A_KV_WIDTH, B_FDIM, B_FDIM, B_FDIM, B_VDIM, B_VDIM)
AB_IN = A_WIDTH + 2 * A_KV_WIDTH + 3 * B_FDIM + 2 * B_VDIM
AB_OUT = A_WIDTH + B_VDIM

C_N = 64
C_HEADS = D_MODEL // C_N
DECAY_LORA = 64
AAA_LORA = 64
GATE_LORA = 128
LN_X_EPS = 64e-5

kernel_name = 'hybrid_dit_gqa_hgrn2_rwkv7_step'

def rms_norm(x, w):
    xf = x.astype(jnp.float32)
    y = xf * lax.rsqrt(jnp.mean(xf * xf, axis=-1, keepdims=True) + NORM_EPS)
    return (y * w.astype(jnp.float32)).astype(x.dtype)

def adaln_vectors(cvec, w, b):
    m = jax.nn.silu(cvec) @ w + b
    return jnp.split(m[:, None, :], 6, axis=-1)

def modulate(h, shift, scale):
    return h * (1 + scale) + shift

def axial_rope_tables(n_tok):
    rows = n_tok // GRID_W
    row = jnp.repeat(jnp.arange(rows), GRID_W).astype(jnp.float32)
    col = jnp.tile(jnp.arange(GRID_W), rows).astype(jnp.float32)
    ax = HEAD_DIM // 2
    inv = ROPE_THETA ** (-jnp.arange(0, ax, 2, dtype=jnp.float32) / ax)
    ang = jnp.concatenate([row[:, None] * inv, col[:, None] * inv], axis=-1)
    return jnp.cos(ang), jnp.sin(ang)

def apply_rope(x, cos, sin):
    xf = x.astype(jnp.float32).reshape(x.shape[:-1] + (HEAD_DIM // 2, 2))
    x0, x1 = xf[..., 0], xf[..., 1]
    c = cos[None, :, None, :]
    s = sin[None, :, None, :]
    out = jnp.stack([x0 * c - x1 * s, x0 * s + x1 * c], axis=-1).reshape(x.shape)
    return out.astype(x.dtype)

def block_attention(q, k, v):
    bsz, n_q, n_h, hd = q.shape
    n_kv = k.shape[2]
    grp = n_h // n_kv
    n_blk = n_q // Q_BLOCK
    qb = jnp.moveaxis(q.reshape(bsz, n_blk, Q_BLOCK, n_kv, grp, hd), 1, 0)

    def one_block(q_blk):
        s = jnp.einsum('bqkgd,btkd->bkgqt', q_blk, k, preferred_element_type=jnp.float32) * ATTN_SCALE
        p = jax.nn.softmax(s, axis=-1).astype(v.dtype)
        return jnp.einsum('bkgqt,btkd->bqkgd', p, v)

    out = lax.map(one_block, qb)
    return jnp.moveaxis(out, 0, 1).reshape(bsz, n_q, n_h * hd)

def gla_chunkwise(q, log_f, k, v, s0):
    bsz, n_tok, n_h, dk = q.shape
    dv = v.shape[-1]
    n_c = n_tok // B_CHUNK
    q, log_f, k = (t.reshape(bsz, n_c, B_CHUNK, n_h, dk) for t in (q, log_f, k))
    v = v.reshape(bsz, n_c, B_CHUNK, n_h, dv)
    b = jnp.cumsum(log_f, axis=2)
    b_end = b[:, :, -1]
    q_dec = q * jnp.exp(b)
    k_inv = k * jnp.exp(-b)
    mask = jnp.tril(jnp.ones((B_CHUNK, B_CHUNK), dtype=bool))
    att = jnp.where(mask, jnp.einsum('bnchk,bnshk->bnhcs', q_dec, k_inv), 0.0)
    o_intra = jnp.einsum('bnhcs,bnshv->bnchv', att, v)
    k_end = k * jnp.exp(b_end[:, :, None] - b)
    ds = jnp.einsum('bnchk,bnchv->bnhkv', k_end, v)
    decay = jnp.exp(b_end)

    def step(s, inp):
        dec, d = inp
        return dec[..., None] * s + d, s

    s_final, s_start = lax.scan(step, s0.astype(jnp.float32), (jnp.moveaxis(decay, 1, 0), jnp.moveaxis(ds, 1, 0)))
    s_start = jnp.moveaxis(s_start, 0, 1)
    o_inter = jnp.einsum('bnchk,bnhkv->bnchv', q_dec, s_start)
    return (o_intra + o_inter).reshape(bsz, n_tok, n_h, dv), s_final

def even_mixer(h, w_in, w_out, q_norm, k_norm, lb, g_norm, ctx):
    bsz, n_tok, _ = h.shape
    offs = []
    acc = 0
    for size in AB_SIZES[:-1]:
        acc += size
        offs.append(acc)
    qa, ka, va, qb, fa, fb, vb, gb = jnp.split(h @ w_in, offs, axis=-1)
    qa = rms_norm(qa.reshape(bsz, n_tok, A_HEADS, HEAD_DIM), q_norm)
    ka = rms_norm(ka.reshape(bsz, n_tok, A_KV_HEADS, HEAD_DIM), k_norm)
    va = va.reshape(bsz, n_tok, A_KV_HEADS, HEAD_DIM)
    if ctx is None:
        keys, vals = ka, va
        s0_f = jnp.zeros((bsz, B_HEADS, B_DK, B_DV), jnp.float32)
        s0_b = s0_f
    else:
        ctx_k, ctx_v, s0_f, s0_b = ctx
        cos, sin = axial_rope_tables(n_tok)
        qa = apply_rope(qa, cos, sin)
        keys = jnp.concatenate([apply_rope(ka, cos, sin), ctx_k.astype(ka.dtype)], axis=1)
        vals = jnp.concatenate([va, ctx_v.astype(va.dtype)], axis=1)
    oa = block_attention(qa, keys, vals)
    lb = lb.reshape(B_HEADS, B_DK)

    def heads_b(t, d):
        return t.astype(jnp.float32).reshape(bsz, n_tok, B_HEADS, d)

    q = jax.nn.silu(heads_b(qb, B_DK))
    v = heads_b(vb, B_DV)
    f_f = lb + (1 - lb) * jax.nn.sigmoid(heads_b(fa, B_DK))
    f_b = lb + (1 - lb) * jax.nn.sigmoid(heads_b(fb, B_DK))
    o_f, s_f = gla_chunkwise(q, jnp.log(f_f), 1 - f_f, v, s0_f)
    o_b, s_b = gla_chunkwise(q[:, ::-1], jnp.log(f_b)[:, ::-1], (1 - f_b)[:, ::-1], v[:, ::-1], s0_b)
    o = rms_norm(o_f + o_b[:, ::-1], g_norm) * jax.nn.silu(heads_b(gb, B_DV))
    ob = o.reshape(bsz, n_tok, B_VDIM).astype(h.dtype)
    y = jnp.concatenate([oa, ob], axis=-1) @ w_out
    return y, (ka, va, s_f, s_b)

def token_shift(x):
    half = x.shape[-1] // 2
    xp = jnp.pad(x, ((0, 0), (1, 1), (0, 0)))
    shifted = jnp.concatenate([xp[:, :-2, :half], xp[:, 2:, half:]], axis=-1)
    return shifted - x

def rwkv7_scan(r, w, k, v, kk, a, s0):
    def step(s, inp):
        r_t, w_t, k_t, v_t, kk_t, a_t = inp
        sa = jnp.einsum('bhvk,bhk->bhv', s, -kk_t)
        s = s * w_t[:, :, None, :] + sa[..., None] * (kk_t * a_t)[:, :, None, :] + v_t[..., None] * k_t[:, :, None, :]
        return s, jnp.einsum('bhvk,bhk->bhv', s, r_t)

    xs = tuple(jnp.moveaxis(t, 1, 0) for t in (r, w, k, v, kk, a))
    s_fin, ys = lax.scan(step, s0.astype(jnp.float32), xs)
    return jnp.moveaxis(ys, 0, 1), s_fin

def odd_mixer(h, mix, wr, wk, wv, wo, w0, w1, w2, a0, a1, a2, g1, g2, k_k, k_a, r_k, ln_w, ln_b, ctx):
    bsz, n_tok, _ = h.shape

    def heads(t):
        return t.astype(jnp.float32).reshape(bsz, n_tok, C_HEADS, C_N)

    xx = token_shift(h)
    xr, xw, xk, xv, xa, xg = [h + xx * mix[i] for i in range(6)]
    r = heads(xr @ wr)
    k = heads(xk @ wk)
    v = heads(xv @ wv)
    g = jax.nn.sigmoid(xg @ g1) @ g2
    kk = k * k_k.astype(jnp.float32).reshape(C_HEADS, C_N)
    kk = kk * lax.rsqrt(jnp.maximum(jnp.sum(kk * kk, axis=-1, keepdims=True), 1e-24))
    k_a_h = k_a.astype(jnp.float32).reshape(C_HEADS, C_N)
    r_k_f = r_k.astype(jnp.float32)
    if ctx is None:
        s0_f = jnp.zeros((bsz, C_HEADS, C_N, C_N), jnp.float32)
        s0_b = s0_f
    else:
        s0_f, s0_b = ctx

    def direction(d, s0):
        w_log = -jax.nn.softplus(-(w0[d] + jnp.tanh(xw @ w1[d]) @ w2[d]).astype(jnp.float32)) - 0.5
        decay = heads(jnp.exp(-jnp.exp(w_log)))
        a = heads(jax.nn.sigmoid((a0[d] + (xa @ a1[d]) @ a2[d]).astype(jnp.float32)))
        kd = k * (1 + (a - 1) * k_a_h)
        seq = (r, decay, kd, v, kk, a)
        if d == 1:
            seq = tuple(t[:, ::-1] for t in seq)
        y, s_fin = rwkv7_scan(*seq, s0)
        if d == 1:
            y = y[:, ::-1]
        bonus = jnp.sum(r * kd * r_k_f, axis=-1, keepdims=True) * v
        return y, bonus, s_fin

    y_f, bonus_f, s_f = direction(0, s0_f)
    y_b, bonus_b, s_b = direction(1, s0_b)
    y = y_f + y_b
    mu = jnp.mean(y, axis=-1, keepdims=True)
    var = jnp.mean(jnp.square(y - mu), axis=-1, keepdims=True)
    yn = ((y - mu) * lax.rsqrt(var + LN_X_EPS)).reshape(bsz, n_tok, D_MODEL) * ln_w + ln_b
    out = (yn + (bonus_f + bonus_b).reshape(bsz, n_tok, D_MODEL)) * g
    return out.astype(h.dtype) @ wo, (s_f, s_b)

def sq_relu_mlp(h, w1, w2):
    return jnp.square(jax.nn.relu(h @ w1)) @ w2

def run_trunk(x, cvec, W, lb_all, cache):
    attn_k, attn_v, hg_f, hg_b, rw_f, rw_b = [], [], [], [], [], []
    for l in range(DEPTH):
        j = l // 2
        sh1, sc1, gt1, sh2, sc2, gt2 = adaln_vectors(cvec, W['ada_w'][l], W['ada_b'][l])
        h = modulate(rms_norm(x, W['norm1_w'][l]), sh1, sc1)
        if l % 2 == 0:
            ctx = None if cache is None else (cache['attn_k'][:, j], cache['attn_v'][:, j], cache['hgrn_fwd'][:, j], cache['hgrn_bwd'][:, j])
            y, (k_c, v_c, s_f, s_b) = even_mixer(h, W['ab_w_in'][j], W['ab_w_out'][j], W['attn_q_norm'][j], W['attn_k_norm'][j], lb_all[j], W['hgrn_g_norm'][j], ctx)
            attn_k.append(k_c)
            attn_v.append(v_c)
            hg_f.append(s_f)
            hg_b.append(s_b)
        else:
            ctx = None if cache is None else (cache['rwkv_fwd'][:, j], cache['rwkv_bwd'][:, j])
            y, (s_f, s_b) = odd_mixer(h, W['rwkv_mix'][j], W['rwkv_wr'][j], W['rwkv_wk'][j], W['rwkv_wv'][j], W['rwkv_wo'][j], W['rwkv_w0'][j], W['rwkv_w1'][j], W['rwkv_w2'][j], W['rwkv_a0'][j], W['rwkv_a1'][j], W['rwkv_a2'][j], W['rwkv_g1'][j], W['rwkv_g2'][j], W['rwkv_k_k'][j], W['rwkv_k_a'][j], W['rwkv_r_k'][j], W['rwkv_ln_w'][j], W['rwkv_ln_b'][j], ctx)
            rw_f.append(s_f)
            rw_b.append(s_b)
        x = x + gt1 * y
        h = modulate(rms_norm(x, W['norm2_w'][l]), sh2, sc2)
        x = x + gt2 * sq_relu_mlp(h, W['mlp_w1'][l], W['mlp_w2'][l])
    if cache is not None:
        return x, None
    return x, (jnp.stack(attn_k, axis=1), jnp.stack(attn_v, axis=1), jnp.stack(hg_f, axis=1), jnp.stack(hg_b, axis=1), jnp.stack(rw_f, axis=1), jnp.stack(rw_b, axis=1))

def setup_inputs(seed: int = 0) -> dict:
    key = jax.random.key(seed)
    keys = jax.random.split(key, 64)
    counter = [0]

    def nxt():
        kk = keys[counter[0]]
        counter[0] += 1
        return kk

    def nrm(shape, scale):
        return scale * jax.random.normal(nxt(), shape, jnp.float32)

    def unif(shape, lo, hi):
        return jax.random.uniform(nxt(), shape, jnp.float32, lo, hi)

    D = D_MODEL
    E, O, L = N_EVEN, N_ODD, DEPTH
    return {
        'x_prompt': nrm((BATCH, SEQ, D), 1.0),
        'x_sample': nrm((DEC_BATCH, DEC_SEQ, D), 1.0),
        'cache_attn_k': nrm((DEC_BATCH, E, PAST_LEN, A_KV_HEADS, HEAD_DIM), 1.0),
        'cache_attn_v': nrm((DEC_BATCH, E, PAST_LEN, A_KV_HEADS, HEAD_DIM), 1.0),
        'state_hgrn_fwd': nrm((DEC_BATCH, E, B_HEADS, B_DK, B_DV), 0.5),
        'state_hgrn_bwd': nrm((DEC_BATCH, E, B_HEADS, B_DK, B_DV), 0.5),
        'state_rwkv_fwd': nrm((DEC_BATCH, O, C_HEADS, C_N, C_N), 0.3),
        'state_rwkv_bwd': nrm((DEC_BATCH, O, C_HEADS, C_N, C_N), 0.3),
        'c': nrm((DEC_BATCH, D), 1.0),
        'c_ctx': nrm((D,), 1.0),
        'ada_w': nrm((L, D, 6 * D), 0.5 * D ** -0.5),
        'ada_b': nrm((L, 6 * D), 0.02),
        'norm1_w': 1.0 + nrm((L, D), 0.02),
        'norm2_w': 1.0 + nrm((L, D), 0.02),
        'ab_w_in': nrm((E, D, AB_IN), D ** -0.5),
        'ab_w_out': nrm((E, AB_OUT, D), AB_OUT ** -0.5),
        'attn_q_norm': 1.0 + nrm((E, HEAD_DIM), 0.02),
        'attn_k_norm': 1.0 + nrm((E, HEAD_DIM), 0.02),
        'hgrn_lb': nrm((E + 1, B_FDIM), 0.1),
        'hgrn_g_norm': 1.0 + nrm((E, B_DV), 0.02),
        'rwkv_mix': unif((O, 6, D), 0.0, 1.0),
        'rwkv_wr': nrm((O, D, D), D ** -0.5),
        'rwkv_wk': nrm((O, D, D), D ** -0.5),
        'rwkv_wv': nrm((O, D, D), D ** -0.5),
        'rwkv_wo': nrm((O, D, D), D ** -0.5),
        'rwkv_w0': unif((O, 2, D), -4.0, -1.0),
        'rwkv_w1': nrm((O, 2, D, DECAY_LORA), D ** -0.5),
        'rwkv_w2': nrm((O, 2, DECAY_LORA, D), 0.1 * DECAY_LORA ** -0.5),
        'rwkv_a0': nrm((O, 2, D), 0.1),
        'rwkv_a1': nrm((O, 2, D, AAA_LORA), D ** -0.5),
        'rwkv_a2': nrm((O, 2, AAA_LORA, D), AAA_LORA ** -0.5),
        'rwkv_g1': nrm((O, D, GATE_LORA), D ** -0.5),
        'rwkv_g2': nrm((O, GATE_LORA, D), GATE_LORA ** -0.5),
        'rwkv_k_k': 0.85 + nrm((O, D), 0.05),
        'rwkv_k_a': 1.0 + nrm((O, D), 0.05),
        'rwkv_r_k': nrm((O, C_HEADS, C_N), 0.1),
        'rwkv_ln_w': 1.0 + nrm((O, D), 0.02),
        'rwkv_ln_b': nrm((O, D), 0.02),
        'mlp_w1': nrm((L, D, D_FF), D ** -0.5),
        'mlp_w2': nrm((L, D_FF, D), D_FF ** -0.5),
    }

def reference(x_prompt, x_sample, cache_attn_k, cache_attn_v, state_hgrn_fwd, state_hgrn_bwd, state_rwkv_fwd, state_rwkv_bwd, c, c_ctx, ada_w, ada_b, norm1_w, norm2_w, ab_w_in, ab_w_out, attn_q_norm, attn_k_norm, hgrn_lb, hgrn_g_norm, rwkv_mix, rwkv_wr, rwkv_wk, rwkv_wv, rwkv_wo, rwkv_w0, rwkv_w1, rwkv_w2, rwkv_a0, rwkv_a1, rwkv_a2, rwkv_g1, rwkv_g2, rwkv_k_k, rwkv_k_a, rwkv_r_k, rwkv_ln_w, rwkv_ln_b, mlp_w1, mlp_w2):
    W = dict(ada_w=ada_w, ada_b=ada_b, norm1_w=norm1_w, norm2_w=norm2_w, ab_w_in=ab_w_in, ab_w_out=ab_w_out, attn_q_norm=attn_q_norm, attn_k_norm=attn_k_norm, hgrn_g_norm=hgrn_g_norm, rwkv_mix=rwkv_mix, rwkv_wr=rwkv_wr, rwkv_wk=rwkv_wk, rwkv_wv=rwkv_wv, rwkv_wo=rwkv_wo, rwkv_w0=rwkv_w0, rwkv_w1=rwkv_w1, rwkv_w2=rwkv_w2, rwkv_a0=rwkv_a0, rwkv_a1=rwkv_a1, rwkv_a2=rwkv_a2, rwkv_g1=rwkv_g1, rwkv_g2=rwkv_g2, rwkv_k_k=rwkv_k_k, rwkv_k_a=rwkv_k_a, rwkv_r_k=rwkv_r_k, rwkv_ln_w=rwkv_ln_w, rwkv_ln_b=rwkv_ln_b, mlp_w1=mlp_w1, mlp_w2=mlp_w2)
    lb_all = jnp.cumsum(jax.nn.softmax(hgrn_lb.astype(jnp.float32), axis=0), axis=0)
    y_prompt, ctx_new = run_trunk(x_prompt, c_ctx[None, :], W, lb_all, None)
    new_attn_k, new_attn_v, new_hgrn_fwd, new_hgrn_bwd, new_rwkv_fwd, new_rwkv_bwd = ctx_new
    cache = dict(attn_k=cache_attn_k, attn_v=cache_attn_v, hgrn_fwd=state_hgrn_fwd, hgrn_bwd=state_hgrn_bwd, rwkv_fwd=state_rwkv_fwd, rwkv_bwd=state_rwkv_bwd)
    y_sample, _ = run_trunk(x_sample, c, W, lb_all, cache)
    return (y_prompt, y_sample, new_attn_k, new_attn_v, new_hgrn_fwd, new_hgrn_bwd, new_rwkv_fwd, new_rwkv_bwd)


_drawn_inputs = setup_inputs


def setup_inputs(seed=0):
    import zlib

    import numpy as np

    out = dict(_drawn_inputs(seed))
    spreads = {}
    factors = {'cache_attn_k': 8.0,
     'cache_attn_v': 8.0,
     'state_hgrn_fwd': 8.0,
     'state_hgrn_bwd': 8.0,
     'state_rwkv_fwd': 8.0,
     'state_rwkv_bwd': 8.0,
     'norm2_w': 4.664,
     'attn_q_norm': 8.0,
     'attn_k_norm': 8.127,
     'hgrn_g_norm': 21.54,
     'rwkv_w1': 4.241,
     'rwkv_w2': 4.099,
     'rwkv_ln_w': 64.0,
     'rwkv_ln_b': 64.0,
     'rwkv_r_k': 4.055}
    for name, (base, spread) in spreads.items():
        noise = np.random.default_rng([zlib.crc32(name.encode()), seed]).standard_normal(out[name].shape)
        drawn = base * np.exp(spread * noise) if base else spread * noise
        out[name] = jnp.asarray(drawn.astype(out[name].dtype))
    for name, factor in factors.items():
        out[name] = (out[name] * factor).astype(out[name].dtype)
    return out
```

```python
from contextlib import ExitStack

import numpy as np

import concourse.bass as bass
from concourse import mybir

F32 = mybir.dt.float32
ALU = mybir.AluOpType
ACT = mybir.ActivationFunctionType
AXX = mybir.AxisListType.X

P = 128
D = 1024
KT = D // P
NS, NP_ = 512, 128
T = NS + NP_
TT_ = T // P
DFF = 4096
HD = 64
CH = 64
NCH = T // CH
EPS = 1e-6
LN_X_EPS = 64e-5
DECAY = float(np.exp(-0.5))
ATTN_SCALE = HD ** -0.5
LAYERS = 2

C_ID, C_MEAN, C_BD64, C_BD16, C_ROPE, C_RWKV, C_HGRN, C_SCAN, C_END = (
    0, 128, 256, 384, 512, 640, 896, 1152, 1152 + T + 1)


def constants():
    c = np.zeros((P, C_END), np.float32)
    i, j = np.arange(P)[:, None], np.arange(P)[None, :]
    c[:, C_ID:C_ID + P] = i == j
    c[:, C_MEAN:C_MEAN + P] = 1.0 / D
    c[:, C_BD64:C_BD64 + P] = (i // 64 == j // 64) / 64.0
    c[:, C_BD16:C_BD16 + P] = i // 16 == j // 16
    c[:, C_ROPE:C_ROPE + P] = (i == j - 1) * (j % 2 == 1) - 1.0 * (i == j + 1) * (j % 2 == 0)
    s, t = i % 64, j % 64
    c[:, C_RWKV:C_RWKV + P] = np.where(j < 64, s < t, s <= t)
    c[:, C_RWKV + P:C_RWKV + 2 * P] = np.where(j < 64, s > t, s >= t)
    same = i // 64 == j // 64
    c[:, C_HGRN:C_HGRN + P] = same & (i <= j)
    c[:, C_HGRN + P:C_HGRN + 2 * P] = same & (i >= j)
    c[:, C_SCAN:] = np.arange(T + 1)[None, :] % CH != 0
    return c


def rope_tables():
    tok = np.arange(NS)
    inv = (np.float32(10000.0) ** (-np.arange(0, 32, 2, dtype=np.float32) / np.float32(32))).astype(np.float32)
    ang = np.concatenate([(tok // 64).astype(np.float32)[:, None] * inv,
                          (tok % 64).astype(np.float32)[:, None] * inv], axis=-1)
    both = np.stack([np.cos(ang), np.sin(ang)]).astype(np.float32)
    both = np.repeat(both, 2, axis=2)
    both = np.concatenate([both, both], axis=2)
    return np.ascontiguousarray(both.transpose(2, 0, 1)).reshape(P, 2 * NS)


R_ADAB, R_N1, R_N2 = 0, 96, 112
R_MIX, R_W0, R_A0, R_KK, R_KA, R_RK, R_LNW, R_LNB, R1 = 0, 48, 64, 80, 88, 96, 104, 112, 120
R_C, R_LB, R_QN, R_KN, R_GN, R2 = 0, 16, 24, 25, 26, 27

U_X, U_H = 0, 8
U_Q, U_K, U_VA, U_QB, U_F, U_VB, U_GB = 16, 20, 21, 22, 26, 34, 38
U_MIX = 42
U_S = 50
U_H1 = 16
U_R, U_RK, U_RV, U_MID, U_XI = 16, 24, 32, 40, 43
RING = 65 * T
SLOT = 4096
ARENA = RING + 2 * SLOT


def program(nc, a, o):
    with ExitStack() as ctx:
        def sb(name, shape):
            return ctx.enter_context(nc.sbuf_tensor(name, shape, F32))

        AR = sb("arena", [P, ARENA])[:, :]
        CON = sb("constants", [P, C_END + 1])[:, :]
        PC = sb("param_cols", [P, 3, P])
        ADA = sb("ada", [P, 48, 2])
        SC = sb("silu_c", [P, 2, KT])[:, :, :]
        GAIN = sb("gain", [P, 2, KT, 2])
        LB = sb("lower_bound", [P, 6, 4])
        SML = sb("small", [P, 32])
        EPSC = sb("eps_cols", [P, 4])
        PS = ctx.enter_context(nc.psum_tensor("psum", [P, 8, 512], F32))

        sems = {}

        def S(name):
            if name not in sems:
                sems[name] = ctx.enter_context(nc.semaphore(name))
            return sems[name]

        def unit(u, n=1):
            return AR[:, u * T:(u + n) * T] if n == 1 else AR[:, u * T:(u + n) * T].rearrange("p (u t) -> p u t", u=n)

        def flat(off, n):
            return AR[:, off:off + n]

        def pair(b, n=T):
            return PS[:, b:b + 2, :].rearrange("p b n -> p (b n)")[:, 0:n]

        def con(c, n=P):
            return CON[:, c:c + n]

        ident = con(C_ID)
        bd64 = con(C_BD64)
        GROUPS = ((0, NS), (NS, NP_))

        stage = {}

        def stage_end(eng, key):
            eng.drain().then_inc(S("stage_done"), 1)
            stage[key] = stage.get(key, 0) + 1
            eng.wait_ge(S("stage_done"), 4 * stage[key])

        def mm(out, lhsT, rhs, start=True, stop=True):
            return nc.tensor.matmul(out, lhsT, rhs, start=start, stop=stop)

        class Steps:

            def __init__(self, eng, name):
                self.eng, self.sem, self.n = eng, S(name), 0

            def __call__(self, ins):
                self.n += 1
                ins.then_inc(self.sem, 1)
                self.eng.wait_ge(self.sem, self.n)

        V, A, G = nc.vector, nc.scalar, nc.gpsimd

        def cols(w, c0, n):
            return w[:, c0:c0 + n].rearrange("(k p) n -> p k n", p=P)

        def cm_tiles(m0, n):
            return [("cm", j, m0 + j) for j in range(n)]

        stages = {}
        order = []

        def add_stage(name, blocks):
            stages[name] = blocks
            order.append(name)

        for l in range(LAYERS):
            aw = a["ada_w"][l]
            add_stage(f"ada{l}", [(cols(aw, 512 * b, 512), 8, 512, [("ada", j, 4 * b + j) for j in range(4)])
                                  for b in range(12)])
            if l == 0:
                w = a["ab_w_in"][0]
                tm = [("tm", 0, t) for t in range(TT_)]
                add_stage("in", [(cols(w, 0, 512), 8, 512, cm_tiles(U_Q, 4)),
                                 (cols(w, 512, 256), 8, 256, [("cm", 0, U_K)] + [("tmk", 1, t) for t in range(TT_)]),
                                 (cols(w, 768, 512), 8, 512, cm_tiles(U_QB, 4)),
                                 (cols(w, 1280, 512), 8, 512, cm_tiles(U_F, 4)),
                                 (cols(w, 1792, 512), 8, 512, cm_tiles(U_F + 4, 4)),
                                 (cols(w, 2304, 512), 8, 512, tm),
                                 (cols(w, 2816, 512), 8, 512, cm_tiles(U_GB, 4))])
                add_stage("out0", [(cols(a["ab_w_out"][0], 512 * b, 512), 8, 512, cm_tiles(4 * b, 4)) for b in range(2)])
            else:
                bl = []
                for u, n in ((U_R, "rwkv_wr"), (U_RK, "rwkv_wk")):
                    bl += [(cols(a[n][0], 512 * b, 512), 8, 512, cm_tiles(u + 4 * b, 4)) for b in range(2)]
                bl += [(cols(a["rwkv_wv"][0], 512 * b, 512), 8, 512, [("tm", b, t) for t in range(TT_)]) for b in range(2)]
                bl += [("lora_w1", 8, 128, cm_tiles(U_MID, 1)), ("lora_a1", 8, 128, cm_tiles(U_MID + 1, 1)),
                       (cols(a["rwkv_g1"][0], 0, 128), 8, 128, cm_tiles(U_MID + 2, 1))]
                add_stage("proj", bl)
                add_stage("out1", [(cols(a["rwkv_wo"][0], 512 * b, 512), 8, 512, cm_tiles(4 * b, 4)) for b in range(2)])
            add_stage(f"up{l}", [(cols(a["mlp_w1"][l], 512 * b, 512), 8, 512, cm_tiles(U_H1 + 4 * b, 4)) for b in range(8)])
            add_stage(f"down{l}", [(a["mlp_w2"][l][:, 128 * m:128 * m + 128].rearrange("(k p) n -> p k n", p=P),
                                    32, 128, cm_tiles(m, 1)) for m in range(8)])

        first_block, first_tile, tiles_upto, nb, nt = {}, {}, [0], 0, 0
        for name in order:
            first_block[name], first_tile[name] = nb, nt
            for b in stages[name]:
                nb, nt = nb + 1, nt + len(b[3])
                tiles_upto.append(nt)

        def slot(b, kt, n):
            s = RING + (b % 2) * SLOT
            return flat(s, kt * n).rearrange("p (k n) -> p k n", k=kt)

        loads = [0, 0]
        loaded_at = {}

        def load_blocks(sp, name):
            for i, (w, kt, n, _) in enumerate(stages[name]):
                b = first_block[name] + i
                if b >= 2:
                    sp.wait_ge(S("tile_product"), tiles_upto[b - 1])
                dst = slot(b, kt, n)
                if w in ("lora_w1", "lora_a1"):
                    src = a["rwkv_w1" if w == "lora_w1" else "rwkv_a1"][0]
                    parts = [(dst[:, :, 64 * d:64 * d + 64], src[d].rearrange("(k p) n -> p k n", p=P)) for d in range(2)]
                else:
                    parts = [(dst, w)]
                for x, y in parts:
                    sp.dma_start(x, y).then_inc(S(f"ring_loaded{b % 2}"), 16)

        per = [0, 0]
        b = 0
        for name in order:
            for blk in stages[name]:
                per[b % 2] += 2 if isinstance(blk[0], str) else 1
                loaded_at[b] = 16 * per[b % 2]
                b += 1

        def products(pe, name, act, before=None):
            n = first_tile[name]
            for i, (_, kt, cn, tiles) in enumerate(stages[name]):
                b = first_block[name] + i
                pe.wait_ge(S(f"ring_loaded{b % 2}"), loaded_at[b])
                w = slot(b, kt, cn)
                if before:
                    before(i)
                for kind, j, _x in tiles:
                    pb = 2 * (n % 2)
                    if n - first_tile[name] >= 2:
                        pe.wait_ge(S("tile_evacuated"), n - 1)
                    for k in range(kt):
                        se = dict(start=k == 0, stop=k == kt - 1)
                        if kind == "cm":
                            lw = w[:, k, 128 * j:128 * j + 128]
                            mm(PS[:, pb, 0:NS], lw, act(i, k)[:, 0:NS], **se)
                            last = mm(PS[:, pb + 1, 0:NP_], lw, act(i, k)[:, NS:T], **se)
                        elif kind == "tm":
                            last = mm(PS[:, pb, 0:cn], act(i, k)[:, 128 * _x:128 * _x + 128], w[:, k, :], **se)
                        else:
                            last = mm(PS[:, pb, 0:128], act(i, k)[:, 128 * _x:128 * _x + 128], w[:, k, 128:256], **se)
                    last.then_inc(S("tile_product"), 1)
                    n += 1

        def tile_list(name):
            n = first_tile[name]
            for i, (_, kt, cn, tiles) in enumerate(stages[name]):
                for t in tiles:
                    yield n, i, t
                    n += 1

        def ada_pe(pe, l):
            name = f"ada{l}"
            for i, (_, kt, cn, tiles) in enumerate(stages[name]):
                b = first_block[name] + i
                pe.wait_ge(S(f"ring_loaded{b % 2}"), loaded_at[b])
                w = slot(b, kt, cn)
                for _, j, m in tiles:
                    for k in range(KT):
                        last = mm(PS[:, 0, 2 * m:2 * m + 2], w[:, k, 128 * j:128 * j + 128], SC[:, :, k],
                                  start=k == 0, stop=k == KT - 1)
                    last.then_inc(S("tile_product"), 1)

        def ada_dve(dve, step, l):
            name = f"ada{l}"
            dve.wait_ge(S("tile_product"), first_tile[name] + 48)
            ps = PS[:, 0, 0:96].rearrange("p (m g) -> p m g", g=2)
            bias = PC[:, 0, R_ADAB + 48 * l:R_ADAB + 48 * l + 48]
            for g in range(2):
                step(V.tensor_tensor(ADA[:, :, g], ps[:, :, g], bias, ALU.add))
            for w, (row, q) in enumerate(((R_N1, 8), (R_N2, 32))):
                for g in range(2):
                    step(V.scalar_tensor_tensor(GAIN[:, w, :, g], ADA[:, q:q + 8, g], 1.0,
                                                PC[:, 0, row + 8 * l:row + 8 * l + 8], ALU.add, ALU.mult))

        norms = [0]

        def norm_act(act, step, i, w):
            X = unit(U_X, 8)
            for k in range(KT):
                if k >= 2:
                    act.wait_ge(S("norm_sum"), 8 * i + k - 1)
                A.activation(unit(U_S + k % 2), X[:, k, :], ACT.Square).then_inc(S("norm_square"), 1)
            act.wait_ge(S("norm_sum"), 8 * i + 8)
            r = unit(U_S + 2)
            step(A.activation(r, pair(0), ACT.Ln, bias=EPSC[:, 0:1]))
            A.activation(r, r, ACT.Exp, scale=-0.5).then_inc(S("norm_rms"), 1)
            H = unit(U_H, 8)
            sh = 0 if w == 0 else 24
            for k in range(KT):
                act.wait_ge(S("norm_scaled"), 8 * i + k + 1)
                for g, (t0, n) in enumerate(GROUPS):
                    ins = A.activation(H[:, k, t0:t0 + n], unit(U_S + 3 + k % 2)[:, t0:t0 + n], ACT.Identity,
                                       scale=GAIN[:, w, k, g:g + 1], bias=ADA[:, sh + k, g:g + 1])
                ins.then_inc(S("norm_out"), 1)

        def norm_pe(pe, i):
            for k in range(KT):
                pe.wait_ge(S("norm_square"), 8 * i + k + 1)
                sq = unit(U_S + k % 2)
                mm(PS[:, 0, 0:NS], con(C_MEAN), sq[:, 0:NS], start=k == 0, stop=k == 7)
                mm(PS[:, 1, 0:NP_], con(C_MEAN), sq[:, NS:T], start=k == 0, stop=k == 7).then_inc(S("norm_sum"), 1)

        def norm_dve(dve, i):
            X = unit(U_X, 8)
            dve.wait_ge(S("norm_rms"), i + 1)
            for k in range(KT):
                if k >= 2:
                    dve.wait_ge(S("norm_out"), 8 * i + k - 1)
                V.tensor_tensor(unit(U_S + 3 + k % 2), X[:, k, :], unit(U_S + 2), ALU.mult).then_inc(S("norm_scaled"), 1)

        def residual_dve(dve, name, gate):
            X = unit(U_X, 8)
            for n, _, (_, j, m) in tile_list(name):
                dve.wait_ge(S("tile_product"), n + 1)
                pb = 2 * (n % 2)
                for g, (t0, c) in enumerate(GROUPS):
                    x = X[:, m, t0:t0 + c]
                    ins = V.scalar_tensor_tensor(x, PS[:, pb + g, 0:c], ADA[:, gate + m, g:g + 1], x, ALU.mult, ALU.add)
                ins.then_inc(S("tile_evacuated"), 1)

        def up_act(act, l):
            for n, _, (_, j, u) in tile_list(f"up{l}"):
                act.wait_ge(S("tile_product"), n + 1)
                A.activation(unit(u), pair(2 * (n % 2)), ACT.Relu).then_inc(S("tile_evacuated"), 1)

        def up_dve(dve, l):
            for n, _, (_, j, u) in tile_list(f"up{l}"):
                dve.wait_ge(S("tile_evacuated"), n + 1)
                V.tensor_tensor(unit(u), unit(u), unit(u), ALU.mult)

        def evac_act(act, name, func, tm_dst):
            for n, i, (kind, j, x) in tile_list(name):
                act.wait_ge(S("tile_product"), n + 1)
                pb = 2 * (n % 2)
                if kind == "cm":
                    ins = A.activation(unit(x), pair(pb), func(x))
                else:
                    dst, c = tm_dst(kind, j, x)
                    ins = A.activation(dst, PS[:, pb, 0:c], ACT.Copy)
                ins.then_inc(S("tile_evacuated"), 1)

        VA = unit(U_VA).rearrange("p (t c) -> p t c", t=TT_)
        COS = flat((U_S + 4) * T, NS)
        SIN = flat((U_S + 4) * T + NS, NS)
        KD = flat((U_S + 6) * T, 2 * 768).rearrange("p (k t) -> p k t", k=2)
        CK = flat((U_S + 9) * T, 256).rearrange("p (a c) -> p a c", a=2)
        KOUT = flat((U_S + 9) * T + 256, 128)
        PR = unit(U_S + 10, 2)
        PT = unit(U_S + 12, 2)

        def attn_prep_act(act, step):
            for t in range(5):
                u = unit(U_Q + t)
                if t >= 2:
                    act.wait_ge(S("qk_sum"), t - 1)
                A.activation(unit(U_S + t % 2), u, ACT.Square).then_inc(S("qk_square"), 1)
                act.wait_ge(S("qk_sum"), t + 1)
                r = unit(U_S + 2 + t % 2)
                if t >= 2:
                    act.wait_ge(S("qk_normed"), t - 1)
                step(A.activation(r, pair(2 * (t % 2)), ACT.Ln, bias=EPSC[:, 0:1]))
                A.activation(r, r, ACT.Exp, scale=-0.5).then_inc(S("qk_rms"), 1)
            act.wait_ge(S("key_out_psum"), 1)
            A.activation(KOUT, PS[:, 6, 0:128], ACT.Copy).then_inc(S("key_out"), 1)
            act.wait_ge(S("qk_roped"), 5)
            act.wait_ge(S("cache_key"), 1)
            K = unit(U_K)
            for kv in range(2):
                r0 = 64 * kv
                for half in range(2):
                    h = slice(64 * half, 64 * half + 64)
                    A.activation(KD[h, kv, 0:NS], K[r0:r0 + 64, 0:NS], ACT.Copy)
                    A.activation(KD[h, kv, NS:T], PS[r0:r0 + 64, 7, 0:128], ACT.Copy)
                    A.activation(KD[h, kv, T:768], K[r0:r0 + 64, NS:T], ACT.Copy)

        def attn_prep_pe(pe):
            for t in range(5):
                pe.wait_ge(S("qk_square"), t + 1)
                if t >= 2:
                    pe.wait_ge(S("qk_rms"), t - 1)
                sq, b = unit(U_S + t % 2), 2 * (t % 2)
                mm(PS[:, b, 0:NS], bd64, sq[:, 0:NS])
                mm(PS[:, b + 1, 0:NP_], bd64, sq[:, NS:T]).then_inc(S("qk_sum"), 1)
                if t >= 1:
                    rope_pe(pe, t - 1)
            rope_pe(pe, 4)
            nc.tensor.transpose(PS[:, 6, 0:128], unit(U_K)[:, NS:T], ident).then_inc(S("key_out_psum"), 1)
            pe.wait_ge(S("cache_loaded"), 32)
            nc.tensor.transpose(PS[:, 7, 0:128], CK[:, 0, :], ident).then_inc(S("cache_key"), 1)

        def rope_pe(pe, t):
            pe.wait_ge(S("qk_normed"), t + 1)
            if t >= 2:
                pe.wait_ge(S("qk_roped"), t - 1)
            mm(PS[:, 4 + t % 2, 0:NS], con(C_ROPE), unit(U_Q + t)[:, 0:NS]).then_inc(S("qk_swapped"), 1)

        def attn_prep_dve(dve, step):
            dve.wait_ge(S("rope_loaded"), 16)
            for t in range(5):
                u = unit(U_Q + t)
                col = PC[:, 2, R_QN:R_QN + 1] if t < 4 else PC[:, 2, R_KN:R_KN + 1]
                dve.wait_ge(S("qk_rms"), t + 1)
                V.scalar_tensor_tensor(u, u, col, unit(U_S + 2 + t % 2), ALU.mult, ALU.mult).then_inc(S("qk_normed"), 1)
                dve.wait_ge(S("qk_swapped"), t + 1)
                tmp = unit(U_S + 14)[:, 0:NS]
                step(V.tensor_tensor(tmp, PS[:, 4 + t % 2, 0:NS], SIN, ALU.mult))
                step(V.tensor_tensor(u[:, 0:NS], u[:, 0:NS], COS, ALU.mult))
                V.tensor_tensor(u[:, 0:NS], u[:, 0:NS], tmp, ALU.add).then_inc(S("qk_roped"), 1)
                dve.wait_ge(S("qk_roped"), t + 1)

        ATT = [(h, t) for h in range(8) for t in range(TT_)]
        NA = len(ATT)

        def keys_of(t):
            return T if t < 4 else 128

        def att_scores(n):
            h, t = ATT[n]
            r = slice(64 * (h % 2), 64 * (h % 2) + 64)
            q = unit(U_Q + h // 2)[r, 128 * t:128 * t + 128]
            kd = KD[r, h // 4, :]
            b = 2 * (n % 2)
            if t < 4:
                mm(PS[:, b, 0:NS], q, kd[:, 0:NS])
                return mm(PS[:, b + 1, 0:128], q, kd[:, NS:T])
            return mm(PS[:, b, 0:128], q, kd[:, T:768])

        def attn_pe(pe):
            def scores(n):
                if n >= 2:
                    pe.wait_ge(S("att_exp"), n - 1)
                att_scores(n).then_inc(S("att_scores"), 1)

            scores(0)
            for n, (h, t) in enumerate(ATT):
                if n + 1 < NA:
                    scores(n + 1)
                pe.wait_ge(S("att_probs"), n + 1)
                if n >= 1:
                    pe.wait_ge(S("att_pt"), n)
                kt = keys_of(t) // 128
                for j in range(kt):
                    ins = nc.tensor.transpose(pair(4)[:, 128 * j:128 * j + 128], PR[:, n % 2, 128 * j:128 * j + 128], ident)
                ins.then_inc(S("att_turned"), 1)
                pe.wait_ge(S("att_pt"), n + 1)
                if n >= 2:
                    pe.wait_ge(S("att_out"), n - 1)
                r = slice(64 * (h % 2), 64 * (h % 2) + 64)
                vc = slice(64 * (h // 4), 64 * (h // 4) + 64)
                for j in range(kt):
                    v = VA[:, 4, vc] if t == 4 else (VA[:, j, vc] if j < 4 else CK[:, 1, vc])
                    ins = mm(PS[r, 6 + n % 2, 0:128], v, PT[:, n % 2, 128 * j:128 * j + 128], start=j == 0, stop=j == kt - 1)
                ins.then_inc(S("att_values"), 1)

        def attn_dve(dve, step):
            def row_max(n):
                k = keys_of(ATT[n][1])
                dve.wait_ge(S("att_scores"), n + 1)
                if n >= 2:
                    dve.wait_ge(S("att_exp"), n - 1)
                st = SML[:, 4 * (n % 2):4 * (n % 2) + 4]
                step(V.tensor_reduce(st[:, 0:1], pair(2 * (n % 2), k), AXX, ALU.max))
                V.tensor_scalar(st[:, 1:2], st[:, 0:1], -ATTN_SCALE, None, ALU.mult).then_inc(S("att_max"), 1)

            row_max(0)
            for n in range(NA):
                if n + 1 < NA:
                    row_max(n + 1)
                k = keys_of(ATT[n][1])
                st = SML[:, 4 * (n % 2):4 * (n % 2) + 4]
                dve.wait_ge(S("att_exp"), n + 1)
                step(V.reciprocal(st[:, 3:4], st[:, 2:3]))
                V.tensor_scalar(PR[:, n % 2, 0:k], PR[:, n % 2, 0:k], st[:, 3:4], None, ALU.mult).then_inc(S("att_probs"), 1)
                dve.wait_ge(S("att_turned"), n + 1)
                if n >= 2:
                    dve.wait_ge(S("att_values"), n - 1)
                V.tensor_copy(PT[:, n % 2, 0:k], pair(4, k)).then_inc(S("att_pt"), 1)

        def attn_act(act):
            def head_out(n):
                h, t = ATT[n]
                r = slice(64 * (h % 2), 64 * (h % 2) + 64)
                act.wait_ge(S("att_values"), n + 1)
                A.activation(unit(U_MIX + h // 2)[r, 128 * t:128 * t + 128], PS[r, 6 + n % 2, 0:128],
                             ACT.Copy).then_inc(S("att_out"), 1)

            for n in range(NA):
                k = keys_of(ATT[n][1])
                st = SML[:, 4 * (n % 2):4 * (n % 2) + 4]
                act.wait_ge(S("att_max"), n + 1)
                if n >= 2:
                    act.wait_ge(S("att_turned"), n - 1)
                A.activation(PR[:, n % 2, 0:k], pair(2 * (n % 2), k), ACT.Exp, scale=ATTN_SCALE, bias=st[:, 1:2],
                             accum_out=st[:, 2:3]).then_inc(S("att_exp"), 1)
                if n >= 1:
                    head_out(n - 1)
            head_out(NA - 1)

        VB = unit(U_VB, 4).rearrange("p u t -> p (u t)").rearrange("p (t c) -> p t c", t=TT_)
        EB, QD, KI, OD = unit(U_S, 2), unit(U_S + 2, 2), unit(U_S + 4, 2), unit(U_S + 6, 2)
        HT = unit(U_S + 8, 2)
        HGM = flat((U_S + 10) * T, 512).rearrange("p (s h c) -> p s h c", s=2, h=2)
        HKT = flat((U_S + 10) * T + 512, 256).rearrange("p (s c) -> p s c", s=2)
        HS = flat((U_S + 12) * T, 512).rearrange("p (d s v) -> p d s v", d=2, s=4)
        HS2 = flat((U_S + 12) * T + 512, 64)
        HU = [(p, i, d) for p in range(4) for i in range(5) for d in range(2)]

        def tile_of(i, d):
            return 4 if i == 4 else (i if d == 0 else 3 - i)

        def hgrn_pe(pe):
            n = 0
            for p in range(4):
                pe.wait_ge(S("hgrn_staged"), p + 1)
                for i in range(5):
                    for d in range(2):
                        t = tile_of(i, d)
                        tk = slice(128 * t, 128 * t + 128)
                        if n:
                            pe.wait_ge(S("hgrn_masked"), n)
                        for h in range(2):
                            r = slice(64 * h, 64 * h + 64)
                            ins = mm(PS[:, h, 0:128], KI[r, d, tk], QD[r, d, tk])
                        ins.then_inc(S("hgrn_scores"), 1)
                        if n:
                            pe.wait_ge(S("hgrn_key_rows"), n)
                        nc.tensor.transpose(PS[:, 2, 0:128], KI[:, d, tk], ident).then_inc(S("hgrn_turned"), 1)
                        pe.wait_ge(S("hgrn_masked"), n + 1)
                        if n:
                            pe.wait_ge(S("hgrn_out_a"), n)
                            pe.wait_ge(S("hgrn_out_b"), n)
                        for h in range(2):
                            r = slice(64 * h, 64 * h + 64)
                            mm(PS[r, 3 + h, 0:128], VB[:, t, 128 * p + 64 * h:128 * p + 64 * h + 64], HGM[:, n % 2, h, :],
                               start=True, stop=False)
                        pe.wait_ge(S("hgrn_key_rows"), n + 1)
                        for s in range(2):
                            c = s if d == 0 else 1 - s
                            k = 2 * n + s
                            pe.wait_ge(S("hgrn_state_init"), 4 * (p + 1))
                            pe.wait_ge(S("hgrn_state_load"), 32 * (p + 1))
                            if k:
                                pe.wait_ge(S("hgrn_state"), k - 1 if (s == 0 and d == 1) else k - 1)
                                pe.wait_ge(S("hgrn_state"), k)
                            st = HS[:, d, (2 if i == 4 else 0) + s, :]
                            for h in range(2):
                                r = slice(64 * h, 64 * h + 64)
                                ins = mm(PS[r, 3 + h, 64 * c:64 * c + 64], st[r, :], QD[r, d, 128 * t + 64 * c:128 * t + 64 * c + 64],
                                         start=False, stop=s == 1)
                            if s == 1:
                                ins.then_inc(S("hgrn_out_psum"), 1)
                            cr = slice(64 * c, 64 * c + 64)
                            for h in range(2):
                                r = slice(64 * h, 64 * h + 64)
                                ins = mm(PS[r, 5, 0:64], HKT[cr, n % 2, 64 * h:64 * h + 64],
                                         VB[cr, t, 128 * p + 64 * h:128 * p + 64 * h + 64])
                            ins.then_inc(S("hgrn_ds"), 1)
                        n += 1
                pe.wait_ge(S("hgrn_o_square"), p + 1)
                mm(PS[:, 6, 0:NS], bd64, HT[:, 0, 0:NS])
                mm(PS[:, 7, 0:NP_], bd64, HT[:, 0, NS:T]).then_inc(S("hgrn_o_sum"), 1)

        def hgrn_dve(dve, step):
            n = 0
            lb, oml = LB[:, 4, :], LB[:, 5, :]
            for p in range(4):
                q, g = unit(U_QB + p), unit(U_GB + p)
                dve.wait_ge(S("hgrn_sig"), 2 * p + 2)
                V.tensor_tensor(q, q, HT[:, 0, :], ALU.mult)
                step(V.tensor_tensor(g, g, HT[:, 1, :], ALU.mult))
                for d in range(2):
                    f = unit(U_F + 4 * d + p)
                    V.tensor_scalar(f, f, oml[:, p:p + 1], lb[:, p:p + 1], ALU.mult, ALU.add).then_inc(S("hgrn_f"), 1)
                for d in range(2):
                    f = unit(U_F + 4 * d + p)
                    dve.wait_ge(S("hgrn_log"), 2 * p + d + 1)
                    m = CON[:, C_SCAN:C_SCAN + T] if d == 0 else CON[:, C_SCAN + T:C_SCAN:-1]
                    x = HT[:, d, :] if d == 0 else HT[:, d, ::-1]
                    V.tensor_tensor_scan(EB[:, d, :] if d == 0 else EB[:, d, ::-1], m, x, 0.0,
                                         ALU.mult, ALU.add).then_inc(S("hgrn_cum"), 1)
                    step(V.tensor_scalar(f, f, -1.0, 1.0, ALU.mult, ALU.add))
                for d in range(2):
                    f = unit(U_F + 4 * d + p)
                    dve.wait_ge(S("hgrn_decay"), 2 * p + d + 1)
                    V.tensor_tensor(QD[:, d, :], q, EB[:, d, :], ALU.mult)
                    ins = V.tensor_tensor(KI[:, d, :], f, HT[:, d, :], ALU.mult)
                ins.then_inc(S("hgrn_staged"), 1)
                for i in range(5):
                    for d in range(2):
                        t = tile_of(i, d)
                        dve.wait_ge(S("hgrn_scores"), n + 1)
                        mask = con(C_HGRN + 128 * d).unsqueeze(1).broadcast_to([P, 2, 128])
                        V.tensor_tensor(HGM[:, n % 2, :, :], PS[:, 0:2, 0:128], mask, ALU.mult).then_inc(S("hgrn_masked"), 1)
                        for s in range(2):
                            k = 2 * n + s
                            c = s if d == 0 else 1 - s
                            s0 = (2 if i == 4 else 0) + s
                            s1 = (2 if i == 4 else 0) + 1 - s
                            e = 128 * t + 64 * c + (63 if d == 0 else 0)
                            dec = EB[:, d, e:e + 1]
                            dve.wait_ge(S("hgrn_state_load"), 32 * (p + 1))
                            dve.wait_ge(S("hgrn_state_init"), 4 * (p + 1))
                            if k:
                                dve.wait_ge(S("hgrn_state"), k)
                            step(V.tensor_scalar(HS2, HS[:, d, s0, :], dec, None, ALU.mult))
                            dve.wait_ge(S("hgrn_ds"), k + 1)
                            V.scalar_tensor_tensor(HS[:, d, s1, :], PS[:, 5, 0:64], dec, HS2, ALU.mult, ALU.add)\
                                .then_inc(S("hgrn_state"), 1)
                        dve.wait_ge(S("hgrn_out_psum"), n + 1)
                        V.tensor_copy(OD[64:128, d, 128 * t:128 * t + 128], PS[64:128, 4, 0:128]).then_inc(S("hgrn_out_b"), 1)
                        n += 1
                dve.wait_ge(S("hgrn_out_a"), n)
                dve.wait_ge(S("hgrn_out_b"), n)
                V.tensor_tensor(OD[:, 0, :], OD[:, 0, :], OD[:, 1, :], ALU.add).then_inc(S("hgrn_o"), 1)
                dve.wait_ge(S("hgrn_o_rms"), p + 1)
                step(V.scalar_tensor_tensor(OD[:, 0, :], OD[:, 0, :], PC[:, 2, R_GN:R_GN + 1], HT[:, 1, :], ALU.mult, ALU.mult))
                V.tensor_tensor(unit(U_MIX + 4 + p), OD[:, 0, :], g, ALU.mult).then_inc(S("hgrn_pair_done"), 1)

        def hgrn_act(act, step):
            act.wait_ge(S("kv_stored"), 32)
            n = 0
            for p in range(4):
                if p:
                    act.wait_ge(S("hgrn_pair_done"), p)
                A.activation(HT[:, 0, :], unit(U_QB + p), ACT.Sigmoid).then_inc(S("hgrn_sig"), 1)
                A.activation(HT[:, 1, :], unit(U_GB + p), ACT.Sigmoid).then_inc(S("hgrn_sig"), 1)
                for d in range(2):
                    act.wait_ge(S("hgrn_f"), 2 * p + d + 1)
                    A.activation(HT[:, d, :], unit(U_F + 4 * d + p), ACT.Ln).then_inc(S("hgrn_log"), 1)
                for d in range(2):
                    act.wait_ge(S("hgrn_cum"), 2 * p + d + 1)
                    A.activation(HT[:, d, :], EB[:, d, :], ACT.Exp, scale=-1.0)
                    A.activation(EB[:, d, :], EB[:, d, :], ACT.Exp).then_inc(S("hgrn_decay"), 1)
                for i in range(5):
                    for d in range(2):
                        t = tile_of(i, d)
                        act.wait_ge(S("hgrn_turned"), n + 1)
                        if n >= 2:
                            act.wait_ge(S("hgrn_ds"), 2 * (n - 1))
                        A.activation(HKT[:, n % 2, :], PS[:, 2, 0:128], ACT.Copy).then_inc(S("hgrn_key_rows"), 1)
                        act.wait_ge(S("hgrn_out_psum"), n + 1)
                        A.activation(OD[0:64, d, 128 * t:128 * t + 128], PS[0:64, 3, 0:128], ACT.Copy).then_inc(S("hgrn_out_a"), 1)
                        n += 1
                act.wait_ge(S("hgrn_o"), p + 1)
                A.activation(HT[:, 0, :], OD[:, 0, :], ACT.Square).then_inc(S("hgrn_o_square"), 1)
                act.wait_ge(S("hgrn_o_sum"), p + 1)
                step(A.activation(HT[:, 1, :], pair(6), ACT.Ln, bias=EPSC[:, 0:1]))
                A.activation(HT[:, 1, :], HT[:, 1, :], ACT.Exp, scale=-0.5).then_inc(S("hgrn_o_rms"), 1)

        def hgrn_pool(pool):
            for p in range(4):
                if p:
                    pool.wait_ge(S("hgrn_pair_done"), p)
                    pool.wait_ge(S("hgrn_final_out"), 32 * p)
                for d in range(2):
                    G.memset(HS[:, d, 2, :], 0.0).then_inc(S("hgrn_state_init"), 1)
                    G.memset(HS[:, d, 3, :], 0.0).then_inc(S("hgrn_state_init"), 1)

        def hgrn_sp(sp):
            for p in range(4):
                if p:
                    sp.wait_ge(S("hgrn_pair_done"), p)
                for d, n in enumerate(("state_hgrn_fwd", "state_hgrn_bwd")):
                    sp.dma_start(HS[:, d, 0, :], a[n][0, 0, 2 * p:2 * p + 2].rearrange("h k v -> (h k) v"))\
                        .then_inc(S("hgrn_state_load"), 16)
                sp.wait_ge(S("hgrn_pair_done"), p + 1)
                for d in range(2):
                    sp.dma_start(o["hgrn"][d][0, 0, 2 * p:2 * p + 2].rearrange("h k v -> (h k) v"), HS[:, d, 2, :])\
                        .then_inc(S("hgrn_final_out"), 16)

        off = [(U_MID + 3) * T]

        def take(n):
            off[0] += n
            assert off[0] <= ARENA
            return flat(off[0] - n, n)

        XI = [unit(U_XI, 8), unit(U_XI + 8, 8)]
        ARD = [take(NCH * 128).rearrange("p (c x) -> p c x", c=NCH) for _ in range(2)]
        BKD = [take(NCH * 128).rearrange("p (c x) -> p c x", c=NCH) for _ in range(2)]
        SV = [take(2 * 11 * 64).rearrange("p (h c v) -> p h c v", h=2, c=11) for _ in range(2)]
        UV = [take(2 * 10 * 64).rearrange("p (h c v) -> p h c v", h=2, c=10) for _ in range(2)]
        YD = [take(T) for _ in range(2)]
        ED = [take(T) for _ in range(2)]
        BN = take(T)
        STL = take(128).rearrange("p (d k) -> p d k", d=2)
        STO = take(128).rearrange("p (d k) -> p d k", d=2)
        LW = take(384).rearrange("p (w c) -> p w c", w=3)
        XS = take(128).rearrange("p (d v) -> p d v", d=2)
        S2 = take(128).rearrange("p (d v) -> p d v", d=2)
        RT = take(T)
        q0 = off[0]
        SW = [take(T) for _ in range(2)]
        AD = [take(T) for _ in range(2)]
        BC = [take(T) for _ in range(2)]
        KKN, SQ = take(T), take(T)
        end1 = off[0]
        off[0] = q0
        def sq4():
            return take(512).rearrange("p (u x) -> p u x", u=4)
        Qm, Qd, Qo, QdT, Q2, QT2, P1, P2, TTm, BT = (sq4() for _ in range(10))
        Lm = take(512).rearrange("p (h u x) -> p h u x", h=2, u=4)
        Rm = take(512).rearrange("p (h u x) -> p h u x", h=2, u=4)
        off[0] = max(end1, off[0])

        R, K = unit(U_R, 8), unit(U_RK, 8)
        RV = unit(U_RV, 8).rearrange("p u t -> p (u t)").rearrange("p (t c) -> p t c", t=TT_)
        MID = unit(U_MID, 3)

        MIXES = [(0, 0, 2), (2, 2, 4), (3, 4, 6), (1, 6, 7), (4, 7, 8), (5, 8, 9)]

        def stage_of_block(i):
            return next(s for s, (_, b0, b1) in enumerate(MIXES) if b0 <= i < b1)

        def proj_tiles_upto(s):
            return first_tile["proj"] + sum(len(b[3]) for b in stages["proj"][:MIXES[s][2]])

        def proj_dve(dve, step):
            H = unit(U_H, 8)
            for s, (mrow, _, _) in enumerate(MIXES):
                xi = XI[s % 2]
                if s >= 2:
                    dve.wait_ge(S("tile_product"), proj_tiles_upto(s - 2))
                mix = PC[:, 1, R_MIX + 8 * mrow:R_MIX + 8 * mrow + 8]
                omm = SML[:, 8:16]
                step(V.tensor_scalar(omm, mix, -1.0, 1.0, ALU.mult, ALU.add))
                for k in range(KT):
                    step(V.tensor_scalar(xi[:, k, :], H[:, k, :], omm[:, k:k + 1], None, ALU.mult))
                    for t0, n in GROUPS:
                        dst, src = (t0 + 1, t0) if k < 4 else (t0, t0 + 1)
                        ins = V.scalar_tensor_tensor(xi[:, k, dst:dst + n - 1], H[:, k, src:src + n - 1], mix[:, k:k + 1],
                                                     xi[:, k, dst:dst + n - 1], ALU.mult, ALU.add)
                        step(ins) if (k, t0) != (KT - 1, NS) else ins.then_inc(S("mixed_input"), 1)
                dve.wait_ge(S("mixed_input"), s + 1)

        UNITS = [(d, h) for d in range(2) for h in range(2)]
        PR_ = {k: i + 1 for i, k in enumerate(("QT", "Q2", "QT2", "Q4", "QT4", "P2", "QT8", "P3", "D", "DT", "NT", "H1", "H2", "H3"))}
        VE_ = {k: i + 1 for i, k in enumerate(("QA", "QB", "Qd", "Qo", "QdT", "QT2", "QT4", "P2", "P3", "D", "H1", "H2", "H3"))}
        SC_ = {k: i + 1 for i, k in enumerate(("Q2", "Q4", "QT8", "DT", "NT"))}
        PO_ = {k: i + 1 for i, k in enumerate(("P1", "IQ"))}
        B0 = [p * 5 for p in range(8)]

        def chunk(i, d, h):
            return 2 * tile_of(i, d) + h

        def rwkv_pe(pe):
            for p in range(8):
                if p:
                    pe.wait_ge(S("rwkv_pair_done"), p)
                pe.wait_ge(S("rwkv_weights"), 80 * (p + 1))
                for w in range(2):
                    for d in range(2):
                        r = slice(64 * d, 64 * d + 64)
                        b = 4 * w + 2 * d
                        mm(PS[:, b, 0:NS], LW[r, w, :], MID[r, w, 0:NS])
                        mm(PS[:, b + 1, 0:NP_], LW[r, w, :], MID[r, w, NS:T]).then_inc(S("rwkv_lora"), 1)
                pe.wait_ge(S("rwkv_k_square"), p + 1)
                pe.wait_ge(S("rwkv_sig"), 4 * p + 1)
                mm(PS[:, 0, 0:NS], bd64, SQ[:, 0:NS])
                mm(PS[:, 1, 0:NP_], bd64, SQ[:, NS:T]).then_inc(S("rwkv_k_sum"), 1)
                pe.wait_ge(S("rwkv_sig"), 4 * p + 4)
                for d in range(2):
                    for h in range(2):
                        r = slice(64 * h, 64 * h + 64)
                        ins = mm(PS[r, 6 + h, 64 * d:64 * d + 64], STL[r, d, :], CON[r, 64 * h:64 * h + 64])
                ins.then_inc(S("rwkv_state_psum"), 1)
                pe.wait_ge(S("rwkv_staged"), p + 1)
                pe.wait_ge(S("rwkv_state_in"), 4 * (p + 1))
                pe.wait_ge(S("rwkv_values_staged"), 2 * p + 2)
                for i in range(5):
                    n = 5 * p + i
                    if n:
                        pe.wait_ge(S("rwkv_y"), 4 * n)
                    if i == 0:
                        pe.wait_ge(S("rwkv_k_max"), p + 1)
                    for h in range(2):
                        r = slice(64 * h, 64 * h + 64)
                        for u, (d, hh) in enumerate(UNITS):
                            c = chunk(i, d, hh)
                            ins = mm(PS[:, h, 128 * u:128 * u + 128], BKD[d][r, c, :], ARD[d][r, c, :])
                    ins.then_inc(S("rwkv_gram"), 1)
                    if n:
                        pe.wait_ge(S("rwkv_bt"), n)
                    for u, (d, hh) in enumerate(UNITS):
                        ins = nc.tensor.transpose(PS[:, 2, 128 * u:128 * u + 128], BKD[d][:, chunk(i, d, hh), :], ident)
                    ins.then_inc(S("rwkv_bk_turned"), 1)

                    def prod(name, bank, lhsT, rhs):
                        for u in range(4):
                            ins = mm(PS[:, bank, 128 * u:128 * u + 128], lhsT[:, u, :], rhs[:, u, :])
                        ins.then_inc(S("inverse_products"), 1)

                    def need(ve=None, sc=None, po=None):
                        if ve:
                            pe.wait_ge(S("inverse_vector"), 13 * n + VE_[ve])
                        if sc:
                            pe.wait_ge(S("inverse_scalar"), 5 * n + SC_[sc])
                        if po:
                            pe.wait_ge(S("inverse_pool"), 2 * n + PO_[po])

                    need(ve="QB")
                    for u in range(4):
                        ins = nc.tensor.transpose(PS[:, 3, 128 * u:128 * u + 128], Qm[:, u, :], ident)
                    ins.then_inc(S("inverse_products"), 1)
                    need(ve="QdT")
                    prod("Q2", 4, QdT, Qd)
                    prod("QT2", 5, Qd, QdT)
                    need(ve="QT2", sc="Q2")
                    prod("Q4", 3, QT2, Q2)
                    prod("QT4", 4, Q2, QT2)
                    need(po="P1")
                    prod("P2", 5, QT2, P1)
                    need(ve="QT4", sc="Q4")
                    prod("QT8", 3, Qd, QdT)
                    need(ve="P2")
                    prod("P3", 4, QdT, P2)
                    need(ve="P3", sc="QT8")
                    prod("D", 5, Q2, QT2)
                    need(po="IQ")
                    prod("DT", 3, QT2, P1)
                    need(sc="DT")
                    prod("NT", 4, Qo, QdT)
                    need(sc="NT", ve="D")
                    prod("H1", 5, Q2, Qd)
                    need(ve="H1")
                    prod("H2", 3, Q2, QT2)
                    need(ve="H2")
                    prod("H3", 4, Q2, P2)
                    need(ve="H3")
                    pe.wait_ge(S("rwkv_masked"), 4 * (n + 1))
                    pe.wait_ge(S("rwkv_alpha"), 4 * (n + 1))
                    pe.wait_ge(S("rwkv_bt"), n + 1)
                    for s in range(2):
                        k = 2 * n + s
                        cs = [chunk(i, 0, s), chunk(i, 1, 1 - s)]
                        us = [s, 3 - s]
                        pe.wait_ge(S("rwkv_state"), k)
                        for d in range(2):
                            for h in range(2):
                                ins = mm(PS[64 * h:64 * h + 64, 6, 64 * d:64 * d + 64], Lm[:, h, us[d], :], SV[d][:, h, cs[d], :])
                        ins.then_inc(S("rwkv_x_psum"), 1)
                        pe.wait_ge(S("rwkv_x"), k + 1)
                        for d in range(2):
                            ins = mm(PS[:, 7, 64 * d:64 * d + 64], TTm[:, us[d], :], XS[:, d, :])
                        ins.then_inc(S("rwkv_u_psum"), 1)
                        pe.wait_ge(S("rwkv_u_a"), 2 * (k + 1))
                        pe.wait_ge(S("rwkv_u_b"), 2 * (k + 1))
                        for d in range(2):
                            for h in range(2):
                                ins = mm(PS[64 * h:64 * h + 64, 6, 128 + 64 * d:192 + 64 * d], BT[:, us[d], 64 * h:64 * h + 64],
                                         UV[d][:, h, cs[d], :])
                        ins.then_inc(S("rwkv_s_psum"), 1)
                        for d in range(2):
                            for h in range(2):
                                r = slice(64 * h, 64 * h + 64)
                                mm(PS[r, h, 64 * us[d]:64 * us[d] + 64], UV[d][:, h, cs[d], :], Rm[:, h, us[d], :],
                                   start=True, stop=False)
                                ins = mm(PS[r, h, 64 * us[d]:64 * us[d] + 64], SV[d][r, h, cs[d], :], ARD[d][r, cs[d], 64:128],
                                         start=False, stop=True)
                    ins.then_inc(S("rwkv_y_psum"), 1)
                pe.wait_ge(S("rwkv_state"), 2 * (5 * p + 5))
                for d in range(2):
                    for h in range(2):
                        r = slice(64 * h, 64 * h + 64)
                        ins = mm(PS[r, 2 + h, 64 * d:64 * d + 64], SV[d][r, h, 10, :], CON[r, 64 * h:64 * h + 64])
                ins.then_inc(S("rwkv_final_psum"), 1)
                pe.wait_ge(S("rwkv_ysum"), p + 1)
                mm(PS[:, 0, 0:NS], bd64, YD[0][:, 0:NS])
                mm(PS[:, 1, 0:NP_], bd64, YD[0][:, NS:T]).then_inc(S("rwkv_mean"), 1)
                mm(PS[:, 4, 0:NS], bd64, BN[:, 0:NS])
                mm(PS[:, 5, 0:NP_], bd64, BN[:, NS:T])
                for t in range(TT_):
                    ins = nc.tensor.transpose(pair(6)[:, 128 * t:128 * t + 128], RV[:, t, 128 * p:128 * p + 128], ident)
                ins.then_inc(S("rwkv_bonus_psum"), 1)
                pe.wait_ge(S("rwkv_yc_square"), p + 1)
                pe.wait_ge(S("rwkv_final"), 2 * (p + 1))
                mm(PS[:, 2, 0:NS], bd64, SQ[:, 0:NS])
                mm(PS[:, 3, 0:NP_], bd64, SQ[:, NS:T]).then_inc(S("rwkv_var"), 1)
                mm(PS[:, 0, 0:NS], LW[:, 2, :], MID[:, 2, 0:NS])
                mm(PS[:, 1, 0:NP_], LW[:, 2, :], MID[:, 2, NS:T]).then_inc(S("rwkv_gate"), 1)

        def rwkv_act(act, step):
            for p in range(8):
                if p:
                    act.wait_ge(S("rwkv_pair_done"), p)
                for w in range(2):
                    for d in range(2):
                        act.wait_ge(S("rwkv_lora"), 4 * p + 2 * w + d + 1)
                        dst = (SW, AD)[w][d]
                        col = (R_W0, R_A0)[w] + 8 * d + p
                        A.activation(dst, pair(4 * w + 2 * d), ACT.Sigmoid, bias=PC[:, 1, col:col + 1]).then_inc(S("rwkv_sig"), 1)
                act.wait_ge(S("rwkv_k_raw"), p + 1)
                A.activation(SQ, KKN, ACT.Square).then_inc(S("rwkv_k_square"), 1)
                act.wait_ge(S("rwkv_state_psum"), p + 1)
                for d in range(2):
                    c0 = 0 if d == 0 else 7
                    for h in range(2):
                        r = slice(64 * h, 64 * h + 64)
                        A.activation(SV[d][r, h, c0, :], PS[r, 6 + h, 64 * d:64 * d + 64], ACT.Copy).then_inc(S("rwkv_state_in"), 1)
                act.wait_ge(S("rwkv_k_max"), p + 1)
                step(A.activation(RT, RT, ACT.Sqrt, scale=64.0))
                step(A.activation(RT, RT, ACT.Ln))
                A.activation(RT, RT, ACT.Exp, scale=-1.0).then_inc(S("rwkv_k_rs"), 1)
                for d in range(2):
                    act.wait_ge(S("rwkv_cum"), 2 * p + d + 1)
                    step(A.activation(ED[d], BC[d], ACT.Exp, scale=-DECAY))
                    step(A.activation(BC[d], BC[d], ACT.Exp, scale=DECAY))
                    A.activation(SW[d], SW[d], ACT.Exp, scale=-DECAY).then_inc(S("rwkv_decays"), 1)
                for i in range(5):
                    n = 5 * p + i
                    act.wait_ge(S("rwkv_bk_turned"), n + 1)
                    A.activation(BT.rearrange("p u x -> p (u x)"), PS[:, 2, :], ACT.Copy).then_inc(S("rwkv_bt"), 1)

                    def ev(name, bank, dst):
                        act.wait_ge(S("inverse_products"), 14 * n + PR_[name])
                        A.activation(dst.rearrange("p u x -> p (u x)"), PS[:, bank, :], ACT.Copy).then_inc(S("inverse_scalar"), 1)

                    ev("Q2", 4, Q2)
                    act.wait_ge(S("inverse_pool"), 2 * n + PO_["P1"])
                    ev("Q4", 3, Qd)
                    act.wait_ge(S("inverse_products"), 14 * n + PR_["P2"])
                    ev("QT8", 3, Q2)
                    ev("DT", 3, QdT)
                    ev("NT", 4, Q2)
                    for s in range(2):
                        k = 2 * n + s
                        act.wait_ge(S("rwkv_x_psum"), k + 1)
                        A.activation(XS.rearrange("p d v -> p (d v)"), PS[:, 6, 0:128], ACT.Copy).then_inc(S("rwkv_x"), 1)
                        act.wait_ge(S("rwkv_u_psum"), k + 1)
                        cs = [chunk(i, 0, s), chunk(i, 1, 1 - s)]
                        for d in range(2):
                            A.activation(UV[d][0:64, 0, cs[d], :], PS[0:64, 7, 64 * d:64 * d + 64], ACT.Copy)\
                                .then_inc(S("rwkv_u_a"), 1)
                    act.wait_ge(S("rwkv_y_psum"), n + 1)
                    for d in range(2):
                        t = tile_of(i, d)
                        for h in range(2):
                            r = slice(64 * h, 64 * h + 64)
                            A.activation(YD[d][r, 128 * t:128 * t + 128], PS[r, h, 128 * d:128 * d + 128], ACT.Copy)\
                                .then_inc(S("rwkv_y"), 1)
                act.wait_ge(S("rwkv_final_psum"), p + 1)
                if p:
                    act.wait_ge(S("rwkv_final_out"), 64 * p)
                for h in range(2):
                    r = slice(64 * h, 64 * h + 64)
                    A.activation(STO[r, :, :].rearrange("p d k -> p (d k)"), PS[r, 2 + h, 0:128], ACT.Copy)\
                        .then_inc(S("rwkv_final"), 1)
                act.wait_ge(S("rwkv_centred"), p + 1)
                A.activation(SQ, YD[1], ACT.Square).then_inc(S("rwkv_yc_square"), 1)
                act.wait_ge(S("rwkv_var"), p + 1)
                step(A.activation(RT, pair(2), ACT.Ln, bias=EPSC[:, 1:2]))
                A.activation(RT, RT, ACT.Exp, scale=-0.5).then_inc(S("rwkv_y_rs"), 1)

        def rwkv_dve(dve, step):
            q64 = bass
            for p in range(8):
                if p:
                    dve.wait_ge(S("rwkv_pair_done"), p)
                r_, k_ = R[:, p, :], K[:, p, :]

                def pcol(row):
                    return PC[:, 1, row + p:row + p + 1]

                V.tensor_scalar(KKN, k_, pcol(R_KK), None, ALU.mult).then_inc(S("rwkv_k_raw"), 1)
                for d in range(2):
                    dve.wait_ge(S("rwkv_sig"), 4 * p + d + 1)
                    m = CON[:, C_SCAN:C_SCAN + T] if d == 0 else CON[:, C_SCAN + T:C_SCAN:-1]
                    x, y = (SW[d], BC[d]) if d == 0 else (SW[d][:, ::-1], BC[d][:, ::-1])
                    step(V.tensor_tensor_scan(y, m, x, 0.0, ALU.mult, ALU.add))
                    V.tensor_tensor(SW[d], BC[d], SW[d], ALU.subtract).then_inc(S("rwkv_cum"), 1)
                dve.wait_ge(S("rwkv_k_sum"), p + 1)
                V.tensor_scalar(RT, pair(0), 1e-24 / 64, None, ALU.max).then_inc(S("rwkv_k_max"), 1)
                oka = SML[:, 16:17]
                step(V.tensor_scalar(oka, pcol(R_KA), -1.0, 1.0, ALU.mult, ALU.add))
                dve.wait_ge(S("rwkv_k_rs"), p + 1)
                step(V.tensor_tensor(KKN, KKN, RT, ALU.mult))

                def v3(x):
                    return x.rearrange("p (c x) -> p c x", c=NCH)

                for d in range(2):
                    dve.wait_ge(S("rwkv_decays"), 2 * p + d + 1)
                    dve.wait_ge(S("rwkv_sig"), 4 * p + 4)
                    V.tensor_tensor(ARD[d][:, :, 64:128], v3(r_), v3(ED[d]), ALU.mult)
                    V.scalar_tensor_tensor(ARD[d][:, :, 0:64], v3(KKN), -1.0, v3(SW[d]), ALU.mult, ALU.mult)
                    step(V.tensor_tensor(RT, KKN, AD[d], ALU.mult))
                    V.tensor_tensor(BKD[d][:, :, 0:64], v3(RT), v3(BC[d]), ALU.mult)
                    step(V.tensor_scalar(AD[d], AD[d], pcol(R_KA), oka, ALU.mult, ALU.add))
                    step(V.tensor_tensor(AD[d], AD[d], k_, ALU.mult))
                    step(V.tensor_tensor(BKD[d][:, :, 64:128], v3(AD[d]), v3(BC[d]), ALU.mult))
                step(V.tensor_tensor(BN, AD[0], AD[1], ALU.add))
                step(V.scalar_tensor_tensor(BN, BN, pcol(R_RK), r_, ALU.mult, ALU.mult))
                V.memset(Qm, 0.0).then_inc(S("rwkv_staged"), 1)
                dve.wait_ge(S("rwkv_staged"), p + 1)
                for i in range(5):
                    n = 5 * p + i
                    dve.wait_ge(S("rwkv_gram"), n + 1)

                    def g4(bank, rows, c0):
                        x = PS[rows, bank, :].rearrange("p (d h x) -> p d h x", d=2, h=2)
                        return x[:, :, :, c0:c0 + 64]

                    def m4(rows, c0):
                        x = CON[rows, C_RWKV:C_RWKV + 256].rearrange("p (d x) -> p d x", d=2)[:, :, c0:c0 + 64]
                        return x.unsqueeze(2).broadcast_to([rows.stop - rows.start, 2, 2, 64])

                    def o4(x):
                        return x.rearrange("p (d h) x -> p d h x", d=2)

                    lo, hi, al = slice(0, 64), slice(64, 128), slice(0, 128)
                    inv = S("inverse_vector")
                    if n:
                        dve.wait_ge(S("inverse_products"), 14 * n)
                    V.tensor_tensor(o4(Qm[lo, :, 0:64]), g4(0, lo, 0), m4(lo, 0), ALU.mult).then_inc(inv, 1)
                    V.tensor_tensor(o4(Qm[hi, :, 64:128]), g4(1, lo, 0), m4(lo, 0), ALU.mult).then_inc(inv, 1)
                    dve.wait_ge(inv, 13 * n + VE_["QB"])
                    f = lambda x: x.rearrange("p u x -> p (u x)")
                    bd = con(C_BD16).unsqueeze(1).broadcast_to([P, 4, 128])
                    V.tensor_tensor(Qd, Qm, bd, ALU.mult).then_inc(inv, 1)
                    dve.wait_ge(inv, 13 * n + VE_["Qd"])
                    V.tensor_tensor(Qo, Qm, Qd, ALU.subtract).then_inc(inv, 1)
                    dve.wait_ge(S("inverse_products"), 14 * n + PR_["QT"])
                    V.tensor_tensor(QdT, PS[:, 3, :].rearrange("p (u x) -> p u x", u=4), bd, ALU.mult).then_inc(inv, 1)
                    msk = S("rwkv_masked")
                    V.tensor_tensor(o4(Lm[hi, 0, :, :]), g4(0, hi, 0), m4(hi, 0), ALU.mult).then_inc(msk, 1)
                    V.tensor_tensor(o4(Lm[lo, 1, :, :]), g4(1, hi, 0), m4(hi, 0), ALU.mult).then_inc(msk, 1)
                    V.tensor_tensor(o4(Rm[:, 0, :, :]), g4(0, al, 64), m4(al, 64), ALU.mult).then_inc(msk, 1)
                    V.tensor_tensor(o4(Rm[:, 1, :, :]), g4(1, al, 64), m4(al, 64), ALU.mult).then_inc(msk, 1)

                    def ev(name, bank, dst, plus=None, mine=None):
                        dve.wait_ge(S("inverse_products"), 14 * n + PR_[name])
                        if mine:
                            dve.wait_ge(inv, 13 * n + VE_[mine])
                        if plus is None:
                            ins = V.tensor_copy(f(dst), PS[:, bank, :])
                        else:
                            ins = V.tensor_tensor(f(dst), PS[:, bank, :], f(plus), ALU.add)
                        ins.then_inc(inv, 1)

                    ev("QT2", 5, QT2)
                    ev("QT4", 4, QdT)
                    dve.wait_ge(S("inverse_pool"), 2 * n + PO_["P1"])
                    ev("P2", 5, P2, P1)
                    ev("P3", 4, QT2, P2, "P2")
                    ev("D", 5, Qd, QT2, "P3")
                    dve.wait_ge(S("inverse_products"), 14 * n + PR_["DT"])
                    ev("H1", 5, QT2, Qd, "D")
                    ev("H2", 3, P2, Qd)
                    ev("H3", 4, TTm, Qd)
                    for s in range(2):
                        k = 2 * n + s
                        cs = [chunk(i, 0, s), chunk(i, 1, 1 - s)]
                        dve.wait_ge(S("rwkv_u_psum"), k + 1)
                        for d in range(2):
                            V.tensor_copy(UV[d][0:64, 1, cs[d], :], PS[64:128, 7, 64 * d:64 * d + 64]).then_inc(S("rwkv_u_b"), 1)
                        dve.wait_ge(S("rwkv_s_psum"), k + 1)
                        dve.wait_ge(S("rwkv_s2"), 4 * (k + 1))
                        for d in range(2):
                            nxt = {7: None, 9: 10}.get(cs[d], cs[d] + 1) if d == 0 else {0: None, 8: 10}.get(cs[d], cs[d] - 1)
                            e = 64 * cs[d] + (63 if d == 0 else 0)
                            for h in range(2):
                                r = slice(64 * h, 64 * h + 64)
                                dst = SV[d][r, h, nxt, :] if nxt is not None else RT[r, 64 * d:64 * d + 64]
                                ins = V.scalar_tensor_tensor(dst, PS[r, 6, 128 + 64 * d:192 + 64 * d], ED[d][r, e:e + 1],
                                                             S2[r, d, :], ALU.mult, ALU.add)
                        ins.then_inc(S("rwkv_state"), 1)
                dve.wait_ge(S("rwkv_y"), 4 * (5 * p + 5))
                V.tensor_tensor(YD[0], YD[0], YD[1], ALU.add).then_inc(S("rwkv_ysum"), 1)
                dve.wait_ge(S("rwkv_ysum"), p + 1)
                dve.wait_ge(S("rwkv_mean"), p + 1)
                V.tensor_tensor(YD[1], YD[0], pair(0), ALU.subtract).then_inc(S("rwkv_centred"), 1)
                dve.wait_ge(S("rwkv_centred"), p + 1)
                dve.wait_ge(S("rwkv_bonus_psum"), p + 1)
                step(V.tensor_scalar(BN, pair(4), 64.0, None, ALU.mult))
                step(V.tensor_tensor(BN, BN, pair(6), ALU.mult))
                dve.wait_ge(S("rwkv_y_rs"), p + 1)
                step(V.tensor_tensor(YD[1], YD[1], RT, ALU.mult))
                step(V.tensor_scalar(YD[1], YD[1], pcol(R_LNW), pcol(R_LNB), ALU.mult, ALU.add))
                step(V.tensor_tensor(YD[1], YD[1], BN, ALU.add))
                dve.wait_ge(S("rwkv_gate"), p + 1)
                V.tensor_tensor(unit(U_H + p), YD[1], pair(0), ALU.mult).then_inc(S("rwkv_pair_done"), 1)

        def rwkv_pool(pool, step):
            for p in range(8):
                if p:
                    pool.wait_ge(S("rwkv_pair_done"), p)
                for d in range(2):
                    for h in range(2):
                        for par in range(2):
                            src = RV[64 * par:64 * par + 64, :, 128 * p + 64 * h:128 * p + 64 * h + 64]
                            row = slice(64, 128) if h == 0 else slice(0, 64)
                            step(G.tensor_copy(SV[d][row, h, par:10:2, :], src))
                            step(G.tensor_copy(UV[d][64:128, h, par:10:2, :], src))
                    step(G.memset(SV[d][0:64, 0, 8 + d, :], 0.0))
                    ins = G.memset(SV[d][64:128, 1, 8 + d, :], 0.0)
                    ins.then_inc(S("rwkv_values_staged"), 1)
                    pool.wait_ge(S("rwkv_values_staged"), 2 * p + d + 1)
                pool.wait_ge(S("rwkv_staged"), p + 1)
                for i in range(5):
                    n = 5 * p + i
                    pool.wait_ge(S("inverse_vector"), 13 * n + VE_["Qd"])
                    idb = ident.unsqueeze(1).broadcast_to([P, 4, 128])
                    if n:
                        pool.wait_ge(S("inverse_products"), 14 * n)
                    G.tensor_tensor(P1, Qd, idb, ALU.add).then_inc(S("inverse_pool"), 1)
                    pool.wait_ge(S("inverse_pool"), 2 * n + 1)
                    for d in range(2):
                        t = tile_of(i, d)
                        for h in range(2):
                            r = slice(64 * h, 64 * h + 64)
                            G.tensor_copy(Lm[r, h, 2 * d:2 * d + 2, :], ARD[d][r, 2 * t:2 * t + 2, 0:64]).then_inc(S("rwkv_alpha"), 1)
                            pool.wait_ge(S("rwkv_alpha"), 4 * n + 2 * d + h + 1)
                    pool.wait_ge(S("inverse_scalar"), 5 * n + SC_["QT8"])
                    pool.wait_ge(S("inverse_vector"), 13 * n + VE_["P2"])
                    G.tensor_tensor(P1, Q2, idb, ALU.add).then_inc(S("inverse_pool"), 1)
                    pool.wait_ge(S("inverse_pool"), 2 * n + 2)
                    for s in range(2):
                        k = 2 * n + s
                        cs = [chunk(i, 0, s), chunk(i, 1, 1 - s)]
                        pool.wait_ge(S("rwkv_state"), k)
                        pool.wait_ge(S("rwkv_state_in"), 4 * (p + 1))
                        pool.wait_ge(S("rwkv_values_staged"), 2 * p + 2)
                        for d in range(2):
                            e = 64 * cs[d] + (63 if d == 0 else 0)
                            for h in range(2):
                                r = slice(64 * h, 64 * h + 64)
                                G.tensor_scalar(S2[r, d, :], SV[d][r, h, cs[d], :], ED[d][r, e:e + 1], None, ALU.mult)\
                                    .then_inc(S("rwkv_s2"), 1)
                                pool.wait_ge(S("rwkv_s2"), 4 * k + 2 * d + h + 1)

        def rwkv_sp(sp):
            for p in range(8):
                if p:
                    sp.wait_ge(S("rwkv_pair_done"), p)
                c = slice(128 * p, 128 * p + 128)
                sp.dma_start(LW[:, 0, :], a["rwkv_w2"][0, :, :, c].rearrange("d k n -> (d k) n")).then_inc(S("rwkv_weights"), 16)
                sp.dma_start(LW[:, 1, :], a["rwkv_a2"][0, :, :, c].rearrange("d k n -> (d k) n")).then_inc(S("rwkv_weights"), 16)
                sp.dma_start(LW[:, 2, :], a["rwkv_g2"][0, :, c]).then_inc(S("rwkv_weights"), 16)
                for d, n in enumerate(("state_rwkv_fwd", "state_rwkv_bwd")):
                    sp.dma_start(STL[:, d, :], a[n][0, 0, 2 * p:2 * p + 2].rearrange("h v k -> (h v) k"))\
                        .then_inc(S("rwkv_weights"), 16)
                sp.wait_ge(S("rwkv_final"), 2 * (p + 1))
                for d in range(2):
                    for h in range(2):
                        r = slice(64 * h, 64 * h + 64)
                        sp.dma_start(o["rwkv"][d][0, 0, 2 * p + h], STO[r, d, :]).then_inc(S("rwkv_final_out"), 16)

        XROWS = flat(U_H1 * T, TT_ * D).rearrange("p (t d) -> p t d", t=TT_)
        PROWS = flat(U_S * T, 3 * 128).rearrange("p (w c) -> p w c", w=3)

        def load_all(sp):
            sp.dma_start(con(0, C_END), a["constants"]).then_inc(S("const_loaded"), 16)
            rows = [(0, R_ADAB, a["ada_b"].rearrange("l (r p) -> (l r) p", p=P), 96),
                    (0, R_N1, a["norm1_w"].rearrange("l (r p) -> (l r) p", p=P), 16),
                    (0, R_N2, a["norm2_w"].rearrange("l (r p) -> (l r) p", p=P), 16),
                    (1, R_MIX, a["rwkv_mix"].rearrange("o i (r p) -> (o i r) p", p=P), 48),
                    (1, R_W0, a["rwkv_w0"].rearrange("o i (r p) -> (o i r) p", p=P), 16),
                    (1, R_A0, a["rwkv_a0"].rearrange("o i (r p) -> (o i r) p", p=P), 16),
                    (1, R_KK, a["rwkv_k_k"].rearrange("o (r p) -> (o r) p", p=P), 8),
                    (1, R_KA, a["rwkv_k_a"].rearrange("o (r p) -> (o r) p", p=P), 8),
                    (1, R_RK, a["rwkv_r_k"].rearrange("o (r h) n -> (o r) (h n)", h=2), 8),
                    (1, R_LNW, a["rwkv_ln_w"].rearrange("o (r p) -> (o r) p", p=P), 8),
                    (1, R_LNB, a["rwkv_ln_b"].rearrange("o (r p) -> (o r) p", p=P), 8),
                    (2, R_C, a["c"].rearrange("o (r p) -> (o r) p", p=P), 8),
                    (2, R_C + 8, a["c_ctx"].rearrange("(r p) -> r p", p=P), 8),
                    (2, R_LB, a["hgrn_lb"].rearrange("o (r p) -> (o r) p", p=P), 8)]
            for w, r, src, n in rows:
                sp.dma_start(PROWS[r:r + n, w, :], src).then_inc(S("rows_loaded"), 16)
            for r, name in ((R_QN, "attn_q_norm"), (R_KN, "attn_k_norm"), (R_GN, "hgrn_g_norm")):
                for h in range(2):
                    sp.dma_start(PROWS[r:r + 1, 2, 64 * h:64 * h + 64], a[name]).then_inc(S("rows_loaded"), 16)
            sp.dma_start(XROWS[:, 0:4, :], a["x_sample"][0].rearrange("(t p) d -> p t d", p=P)).then_inc(S("x_loaded"), 16)
            sp.dma_start(XROWS[:, 4, :], a["x_prompt"][0]).then_inc(S("x_loaded"), 16)
        ROWS = 16 * 20

        def setup_pe(pe):
            pe.wait_ge(S("const_loaded"), 16)
            pe.wait_ge(S("rows_loaded"), ROWS)
            for w, n in enumerate((P, R1, R2)):
                ins = nc.tensor.transpose(PS[:, 7, 128 * w:128 * w + n], PROWS[0:n, w, :], ident[0:n, 0:n])
            ins.then_inc(S("params_psum"), 1)
            pe.wait_ge(S("x_loaded"), 32)
            for k in range(KT):
                b = 2 * (k % 2)
                if k >= 2:
                    pe.wait_ge(S("x_in"), k - 1)
                for t in range(TT_):
                    ins = nc.tensor.transpose(pair(b)[:, 128 * t:128 * t + 128], XROWS[:, t, 128 * k:128 * k + 128], ident)
                ins.then_inc(S("x_turned"), 1)

        def setup_act(act, step):
            act.wait_ge(S("params"), 3)
            c = PC[:, 2, R_C:R_C + 16].rearrange("p (g k) -> p g k", g=2)
            A.activation(SC, c, ACT.Sigmoid).then_inc(S("sig_c"), 1)
            act.wait_ge(S("lb_max"), 1)
            step(A.activation(LB[:, 0, :], LB[:, 2, :], ACT.Exp))
            A.activation(LB[:, 1, :], LB[:, 3, :], ACT.Exp).then_inc(S("lb_exp"), 1)
            for k in range(KT):
                act.wait_ge(S("x_turned"), k + 1)
                A.activation(unit(U_X + k), pair(2 * (k % 2)), ACT.Copy).then_inc(S("x_in"), 1)

        def setup_dve(dve, step):
            step(V.memset(EPSC[:, 0:1], EPS))
            step(V.memset(EPSC[:, 1:2], LN_X_EPS))
            dve.wait_ge(S("params_psum"), 1)
            for w, n in enumerate((P, R1, R2)):
                V.tensor_copy(PC[:, w, 0:n], PS[:, 7, 128 * w:128 * w + n]).then_inc(S("params"), 1)
            dve.wait_ge(S("params"), 3)
            l0, l1 = PC[:, 2, R_LB:R_LB + 4], PC[:, 2, R_LB + 4:R_LB + 8]
            step(V.tensor_tensor(LB[:, 4, :], l0, l1, ALU.max))
            V.tensor_tensor(LB[:, 2, :], l0, LB[:, 4, :], ALU.subtract)
            V.tensor_tensor(LB[:, 3, :], l1, LB[:, 4, :], ALU.subtract).then_inc(S("lb_max"), 1)
            dve.wait_ge(S("sig_c"), 1)
            c = PC[:, 2, R_C:R_C + 16].rearrange("p (g k) -> p g k", g=2)
            step(V.tensor_tensor(SC, SC, c, ALU.mult))
            dve.wait_ge(S("lb_exp"), 1)
            step(V.tensor_tensor(LB[:, 1, :], LB[:, 0, :], LB[:, 1, :], ALU.add))
            step(V.reciprocal(LB[:, 1, :], LB[:, 1, :]))
            step(V.tensor_tensor(LB[:, 4, :], LB[:, 0, :], LB[:, 1, :], ALU.mult))
            step(V.tensor_scalar(LB[:, 5, :], LB[:, 4, :], -1.0, 1.0, ALU.mult, ALU.add))

        def out_pe(pe):
            for t in range(TT_):
                for b in range(2):
                    i = 2 * t + b
                    if i >= 2:
                        pe.wait_ge(S("rows_out"), i - 1)
                    for k in range(4):
                        ins = nc.tensor.transpose(PS[:, b, 128 * k:128 * k + 128],
                                                  unit(U_X + 4 * b + k)[:, 128 * t:128 * t + 128], ident)
                    ins.then_inc(S("rows_turned"), 1)

        def out_act(act):
            for i in range(2 * TT_):
                act.wait_ge(S("rows_turned"), i + 1)
                A.activation(XROWS[:, i // 2, 512 * (i % 2):512 * (i % 2) + 512], PS[:, i % 2, :], ACT.Copy)\
                    .then_inc(S("rows_out"), 1)

        def out_sp(sp):
            for t in range(TT_):
                sp.wait_ge(S("rows_out"), 2 * t + 2)
                dst = o["y_sample"][0, 128 * t:128 * t + 128] if t < 4 else o["y_prompt"][0]
                sp.dma_start(dst, XROWS[:, t, :]).then_inc(S("y_stored"), 16)
            sp.wait_ge(S("y_stored"), 16 * TT_)
            sp.wait_ge(S("hgrn_final_out"), 4 * 32)
            sp.wait_ge(S("rwkv_final_out"), 8 * 64)
            sp.wait_ge(S("kv_stored"), 32)

        block = ctx.enter_context(nc.Block())

        @block.sync
        def _(sp):
            load_all(sp)
            load_blocks(sp, "ada0")
            load_blocks(sp, "in")
            sp.wait_ge(S("stage_done"), 4 * 4)
            sp.dma_start(flat((U_S + 4) * T, 2 * NS), a["rope"]).then_inc(S("rope_loaded"), 16)
            sp.dma_start(CK[:, 0, :], a["cache_attn_k"][0, 0].rearrange("t h c -> t (h c)")).then_inc(S("cache_loaded"), 16)
            sp.dma_start(CK[:, 1, :], a["cache_attn_v"][0, 0].rearrange("t h c -> t (h c)")).then_inc(S("cache_loaded"), 16)
            sp.wait_ge(S("key_out"), 1)
            sp.dma_start(o["k"][0, 0].rearrange("t h c -> t (h c)"), KOUT).then_inc(S("kv_stored"), 16)
            sp.dma_start(o["v"][0, 0].rearrange("t h c -> t (h c)"), VA[:, 4, :]).then_inc(S("kv_stored"), 16)
            sp.wait_ge(S("kv_stored"), 32)
            sp.wait_ge(S("stage_done"), 4 * 6)
            hgrn_sp(sp)
            for name in ("out0", "up0", "down0", "ada1", "proj"):
                load_blocks(sp, name)
            sp.wait_ge(S("stage_done"), 4 * 14)
            rwkv_sp(sp)
            sp.wait_ge(S("stage_done"), 4 * 15)
            for name in ("out1", "up1", "down1"):
                load_blocks(sp, name)
            out_sp(sp)

        def act_h(i, k):
            return unit(U_H + k)

        @block.tensor
        def _(pe):
            setup_pe(pe)
            stage_end(pe, "pe")
            ada_pe(pe, 0)
            stage_end(pe, "pe")
            norm_pe(pe, 0)
            stage_end(pe, "pe")
            products(pe, "in", act_h)
            stage_end(pe, "pe")
            attn_prep_pe(pe)
            stage_end(pe, "pe")
            attn_pe(pe)
            stage_end(pe, "pe")
            hgrn_pe(pe)
            stage_end(pe, "pe")
            products(pe, "out0", lambda i, k: unit(U_MIX + k))
            stage_end(pe, "pe")
            norm_pe(pe, 1)
            stage_end(pe, "pe")
            products(pe, "up0", act_h)
            stage_end(pe, "pe")
            products(pe, "down0", lambda i, k: unit(U_H1 + k))
            stage_end(pe, "pe")
            ada_pe(pe, 1)
            stage_end(pe, "pe")
            norm_pe(pe, 2)
            stage_end(pe, "pe")
            products(pe, "proj", lambda i, k: XI[stage_of_block(i) % 2][:, k, :],
                     before=lambda i: pe.wait_ge(S("mixed_input"), stage_of_block(i) + 1))
            stage_end(pe, "pe")
            rwkv_pe(pe)
            stage_end(pe, "pe")
            products(pe, "out1", act_h)
            stage_end(pe, "pe")
            norm_pe(pe, 3)
            stage_end(pe, "pe")
            products(pe, "up1", act_h)
            stage_end(pe, "pe")
            products(pe, "down1", lambda i, k: unit(U_H1 + k))
            stage_end(pe, "pe")
            out_pe(pe)

        @block.vector
        def _(dve):
            step = Steps(dve, "vector_step")
            setup_dve(dve, step)
            stage_end(dve, "dve")
            ada_dve(dve, step, 0)
            V.memset(SML[:, 20:21], 0.0).then_inc(S("tile_evacuated"), 48)
            stage_end(dve, "dve")
            norm_dve(dve, 0)
            stage_end(dve, "dve")
            stage_end(dve, "dve")
            attn_prep_dve(dve, step)
            stage_end(dve, "dve")
            attn_dve(dve, step)
            stage_end(dve, "dve")
            hgrn_dve(dve, step)
            stage_end(dve, "dve")
            residual_dve(dve, "out0", 16)
            stage_end(dve, "dve")
            norm_dve(dve, 1)
            stage_end(dve, "dve")
            up_dve(dve, 0)
            stage_end(dve, "dve")
            residual_dve(dve, "down0", 40)
            stage_end(dve, "dve")
            ada_dve(dve, step, 1)
            V.memset(SML[:, 20:21], 0.0).then_inc(S("tile_evacuated"), 48)
            stage_end(dve, "dve")
            norm_dve(dve, 2)
            stage_end(dve, "dve")
            proj_dve(dve, step)
            stage_end(dve, "dve")
            rwkv_dve(dve, step)
            stage_end(dve, "dve")
            residual_dve(dve, "out1", 16)
            stage_end(dve, "dve")
            norm_dve(dve, 3)
            stage_end(dve, "dve")
            up_dve(dve, 1)
            stage_end(dve, "dve")
            residual_dve(dve, "down1", 40)
            stage_end(dve, "dve")

        @block.scalar
        def _(act):
            step = Steps(act, "scalar_step")
            setup_act(act, step)
            stage_end(act, "act")
            stage_end(act, "act")
            norm_act(act, step, 0, 0)
            stage_end(act, "act")
            evac_act(act, "in", lambda u: ACT.Sigmoid if U_F <= u < U_F + 8 else ACT.Copy,
                     lambda kind, j, t: (VB[:, t, :], 512) if kind == "tm" else (VA[:, t, :], 128))
            stage_end(act, "act")
            attn_prep_act(act, step)
            stage_end(act, "act")
            attn_act(act)
            stage_end(act, "act")
            hgrn_act(act, step)
            stage_end(act, "act")
            stage_end(act, "act")
            norm_act(act, step, 1, 1)
            stage_end(act, "act")
            up_act(act, 0)
            stage_end(act, "act")
            stage_end(act, "act")
            stage_end(act, "act")
            norm_act(act, step, 2, 0)
            stage_end(act, "act")
            evac_act(act, "proj", lambda u: {U_MID: ACT.Tanh, U_MID + 2: ACT.Sigmoid}.get(u, ACT.Copy),
                     lambda kind, j, t: (RV[:, t, 512 * j:512 * j + 512], 512))
            stage_end(act, "act")
            rwkv_act(act, step)
            stage_end(act, "act")
            stage_end(act, "act")
            norm_act(act, step, 3, 1)
            stage_end(act, "act")
            up_act(act, 1)
            stage_end(act, "act")
            stage_end(act, "act")
            out_act(act)

        @block.gpsimd
        def _(pool):
            step = Steps(pool, "pool_step")
            for i in range(6):
                stage_end(pool, "pool")
            hgrn_pool(pool)
            for i in range(8):
                stage_end(pool, "pool")
            rwkv_pool(pool, step)
            for i in range(5):
                stage_end(pool, "pool")


_IN = ["x_prompt", "x_sample", "cache_attn_k", "cache_attn_v", "state_hgrn_fwd", "state_hgrn_bwd", "state_rwkv_fwd",
       "state_rwkv_bwd", "c", "c_ctx", "ada_w", "ada_b", "norm1_w", "norm2_w", "ab_w_in", "ab_w_out", "attn_q_norm",
       "attn_k_norm", "hgrn_lb", "hgrn_g_norm", "rwkv_mix", "rwkv_wr", "rwkv_wk", "rwkv_wv", "rwkv_wo", "rwkv_w0",
       "rwkv_w1", "rwkv_w2", "rwkv_a0", "rwkv_a1", "rwkv_a2", "rwkv_g1", "rwkv_g2", "rwkv_k_k", "rwkv_k_a", "rwkv_r_k",
       "rwkv_ln_w", "rwkv_ln_b", "mlp_w1", "mlp_w2"]
_OUT = [("y_prompt", (1, 128, 1024)), ("y_sample", (1, 512, 1024)), ("new_attn_k", (1, 1, 128, 2, 64)),
        ("new_attn_v", (1, 1, 128, 2, 64)), ("new_hgrn_fwd", (1, 1, 8, 64, 64)), ("new_hgrn_bwd", (1, 1, 8, 64, 64)),
        ("new_rwkv_fwd", (1, 1, 16, 64, 64)), ("new_rwkv_bwd", (1, 1, 16, 64, 64))]


def kernel(**inputs):
    import concourse.bacc as bacc
    from concourse.bass_utils import run_bass_kernel_spmd as run

    nc = bacc.Bacc("TRN2", target_bir_lowering=False, num_devices=1)
    arrays = {n: np.ascontiguousarray(inputs[n]) for n in _IN}
    arrays["constants"] = constants()
    arrays["rope"] = rope_tables()
    arrays = {"in_" + n: v for n, v in arrays.items()}
    a = {n[3:]: nc.dram_tensor(n, v.shape, F32, kind="ExternalInput").ap() for n, v in arrays.items()}
    outs = {n: nc.dram_tensor("out_" + n, s, F32, kind="ExternalOutput").ap() for n, s in _OUT}
    o = {"y_prompt": outs["y_prompt"], "y_sample": outs["y_sample"], "k": outs["new_attn_k"], "v": outs["new_attn_v"],
         "hgrn": (outs["new_hgrn_fwd"], outs["new_hgrn_bwd"]), "rwkv": (outs["new_rwkv_fwd"], outs["new_rwkv_bwd"])}
    program(nc, a, o)
    r = run(nc, [arrays], core_ids=[0])
    return tuple(r.results[0]["out_" + n] for n, _ in _OUT)
```

```python
from contextlib import ExitStack

import numpy as np

import concourse.bass as bass
from concourse import mybir

F32 = mybir.dt.float32
ALU = mybir.AluOpType
ACT = mybir.ActivationFunctionType
AXX = mybir.AxisListType.X

P = 128
D = 1024
KT = D // P
NS, NP_ = 512, 128
T = NS + NP_
TT_ = T // P
DFF = 4096
HD = 64
CH = 64
NCH = T // CH
EPS = 1e-6
LN_X_EPS = 64e-5
DECAY = float(np.exp(-0.5))
ATTN_SCALE = HD ** -0.5
LAYERS = 2

C_ID, C_MEAN, C_BD64, C_BD16, C_ROPE, C_RWKV, C_HGRN, C_SEL, C_SCAN, C_END = (
    0, 128, 256, 384, 512, 640, 896, 1152, 1154, 1154 + T + 1)


def constants():
    c = np.zeros((P, C_END), np.float32)
    i, j = np.arange(P)[:, None], np.arange(P)[None, :]
    c[:, C_ID:C_ID + P] = i == j
    c[:, C_MEAN:C_MEAN + P] = 1.0 / D
    c[:, C_BD64:C_BD64 + P] = (i // 64 == j // 64) / 64.0
    c[:, C_BD16:C_BD16 + P] = i // 16 == j // 16
    c[:, C_ROPE:C_ROPE + P] = (i == j - 1) * (j % 2 == 1) - 1.0 * (i == j + 1) * (j % 2 == 0)
    s, t = i % 64, j % 64
    c[:, C_RWKV:C_RWKV + P] = np.where(j < 64, s < t, s <= t)
    c[:, C_RWKV + P:C_RWKV + 2 * P] = np.where(j < 64, s > t, s >= t)
    same = i // 64 == j // 64
    c[:, C_HGRN:C_HGRN + P] = same & (i <= j)
    c[:, C_HGRN + P:C_HGRN + 2 * P] = same & (i >= j)
    c[:, C_SEL:C_SEL + 2] = i % 32 == np.arange(2)[None, :]
    c[:, C_SCAN:] = np.arange(T + 1)[None, :] % CH != 0
    return c


def rope_tables():
    tok = np.arange(NS)
    inv = (np.float32(10000.0) ** (-np.arange(0, 32, 2, dtype=np.float32) / np.float32(32))).astype(np.float32)
    ang = np.concatenate([(tok // 64).astype(np.float32)[:, None] * inv,
                          (tok % 64).astype(np.float32)[:, None] * inv], axis=-1)
    both = np.stack([np.cos(ang), np.sin(ang)]).astype(np.float32)
    both = np.repeat(both, 2, axis=2)
    both = np.concatenate([both, both], axis=2)
    return np.ascontiguousarray(both.transpose(2, 0, 1)).reshape(P, 2 * NS)


R_ADAB, R_N1, R_N2 = 0, 96, 112
R_MIX, R_W0, R_A0, R_KK, R_KA, R_RK, R_LNW, R_LNB, R1 = 0, 48, 64, 80, 88, 96, 104, 112, 120
R_C, R_LB, R_QN, R_KN, R_GN, R2 = 0, 16, 24, 25, 26, 27

U_X, U_H = 0, 8
U_Q, U_K, U_VA, U_QB, U_F, U_VB, U_GB = 16, 20, 21, 22, 26, 34, 38
U_MIX = 42
U_S = 50
U_H1 = 16
U_R, U_RK, U_RV, U_MID, U_XI = 16, 24, 32, 40, 43
RING = 66 * T
SLOT = 4096
ARENA = RING + 2 * SLOT


def program(nc, a, o):
    with ExitStack() as ctx:
        def sb(name, shape):
            return ctx.enter_context(nc.sbuf_tensor(name, shape, F32))

        AR = sb("arena", [P, ARENA])[:, :]
        CON = sb("constants", [P, C_END + 1])[:, :]
        PC = sb("param_cols", [P, 3, P])
        ADAS = sb("ada", [P, LAYERS, 48, 2])
        SC = sb("silu_c", [P, 2, KT])[:, :, :]
        SCW = sb("silu_c_rows", [P, KT, 32])[:, :, :]
        GAIN = sb("gain", [P, 2 * LAYERS, KT, 2])
        LB = sb("lower_bound", [P, 6, 4])
        SML = sb("small", [P, 32])
        EPSC = sb("eps_cols", [P, 4])
        PS = ctx.enter_context(nc.psum_tensor("psum", [P, 8, 512], F32))

        sems = {}

        def S(name):
            if name not in sems:
                sems[name] = ctx.enter_context(nc.semaphore(name))
            return sems[name]

        def unit(u, n=1):
            return AR[:, u * T:(u + n) * T] if n == 1 else AR[:, u * T:(u + n) * T].rearrange("p (u t) -> p u t", u=n)

        def flat(off, n):
            return AR[:, off:off + n]

        def pair(b, n=T):
            return PS[:, b:b + 2, :].rearrange("p b n -> p (b n)")[:, 0:n]

        def con(c, n=P):
            return CON[:, c:c + n]

        ident = con(C_ID)
        bd64 = con(C_BD64)
        GROUPS = ((0, NS), (NS, NP_))

        stage = {}

        def stage_end(eng, key):
            eng.drain().then_inc(S("stage_done"), 1)
            stage[key] = stage.get(key, 0) + 1
            eng.wait_ge(S("stage_done"), 4 * stage[key])

        def mm(out, lhsT, rhs, start=True, stop=True):
            return nc.tensor.matmul(out, lhsT, rhs, start=start, stop=stop)

        class Steps:

            def __init__(self, eng, name):
                self.eng, self.sem, self.n = eng, S(name), 0

            def __call__(self, ins):
                self.n += 1
                ins.then_inc(self.sem, 1)
                self.eng.wait_ge(self.sem, self.n)

        V, A, G = nc.vector, nc.scalar, nc.gpsimd

        def cols(w, c0, n):
            return w[:, c0:c0 + n].rearrange("(k p) n -> p k n", p=P)

        def cm_tiles(m0, n):
            return [("cm", j, m0 + j) for j in range(n)]

        stages = {}
        order = []

        def add_stage(name, blocks):
            stages[name] = blocks
            order.append(name)

        def ada_stage(l):
            add_stage(f"ada{l}", [(cols(a["ada_w"][l], 512 * b, 512), 8, 512, [("ada", 0, b)]) for b in range(12)])

        for l in range(LAYERS):
            if l == 0:
                ada_stage(0)
                w = a["ab_w_in"][0]
                tm = [("tm", 0, t) for t in range(TT_)]
                add_stage("in", [(cols(w, 0, 512), 8, 512, cm_tiles(U_Q, 4)),
                                 (cols(w, 512, 256), 8, 256, [("cm", 0, U_K)] + [("tmk", 1, t) for t in range(TT_)]),
                                 (cols(w, 768, 512), 8, 512, cm_tiles(U_QB, 4)),
                                 (cols(w, 1280, 512), 8, 512, cm_tiles(U_F, 4)),
                                 (cols(w, 1792, 512), 8, 512, cm_tiles(U_F + 4, 4)),
                                 (cols(w, 2304, 512), 8, 512, tm),
                                 (cols(w, 2816, 512), 8, 512, cm_tiles(U_GB, 4))])
                ada_stage(1)
                add_stage("out0", [(cols(a["ab_w_out"][0], 512 * b, 512), 8, 512, cm_tiles(4 * b, 4)) for b in range(2)])
            else:
                bl = []
                for u, n in ((U_R, "rwkv_wr"), (U_RK, "rwkv_wk")):
                    bl += [(cols(a[n][0], 512 * b, 512), 8, 512, cm_tiles(u + 4 * b, 4)) for b in range(2)]
                bl += [(cols(a["rwkv_wv"][0], 512 * b, 512), 8, 512, [("tm", b, t) for t in range(TT_)]) for b in range(2)]
                bl += [("lora_w1", 8, 128, cm_tiles(U_MID, 1)), ("lora_a1", 8, 128, cm_tiles(U_MID + 1, 1)),
                       (cols(a["rwkv_g1"][0], 0, 128), 8, 128, cm_tiles(U_MID + 2, 1))]
                add_stage("proj", bl)
                add_stage("out1", [(cols(a["rwkv_wo"][0], 512 * b, 512), 8, 512, cm_tiles(4 * b, 4)) for b in range(2)])
            add_stage(f"up{l}", [(cols(a["mlp_w1"][l], 512 * b, 512), 8, 512, cm_tiles(U_H1 + 4 * b, 4)) for b in range(8)])
            add_stage(f"down{l}", [(a["mlp_w2"][l][:, 128 * m:128 * m + 128].rearrange("(k p) n -> p k n", p=P),
                                    32, 128, cm_tiles(m, 1)) for m in range(8)])

        first_block, first_tile, tiles_upto, nb, nt = {}, {}, [0], 0, 0
        for name in order:
            first_block[name], first_tile[name] = nb, nt
            for b in stages[name]:
                nb, nt = nb + 1, nt + len(b[3])
                tiles_upto.append(nt)

        def slot(b, kt, n):
            s = RING + (b % 2) * SLOT
            return flat(s, kt * n).rearrange("p (k n) -> p k n", k=kt)

        loads = [0, 0]
        loaded_at = {}

        def load_blocks(sp, name):
            for i, (w, kt, n, _) in enumerate(stages[name]):
                b = first_block[name] + i
                if b >= 2:
                    sp.wait_ge(S("tile_product"), tiles_upto[b - 1])
                dst = slot(b, kt, n)
                if w in ("lora_w1", "lora_a1"):
                    src = a["rwkv_w1" if w == "lora_w1" else "rwkv_a1"][0]
                    parts = [(dst[:, :, 64 * d:64 * d + 64], src[d].rearrange("(k p) n -> p k n", p=P)) for d in range(2)]
                else:
                    parts = [(dst, w)]
                for x, y in parts:
                    sp.dma_start(x, y).then_inc(S(f"ring_loaded{b % 2}"), 16)

        per = [0, 0]
        b = 0
        for name in order:
            for blk in stages[name]:
                per[b % 2] += 2 if isinstance(blk[0], str) else 1
                loaded_at[b] = 16 * per[b % 2]
                b += 1

        def products(pe, name, act, before=None):
            n = first_tile[name]
            for i, (_, kt, cn, tiles) in enumerate(stages[name]):
                b = first_block[name] + i
                pe.wait_ge(S(f"ring_loaded{b % 2}"), loaded_at[b])
                w = slot(b, kt, cn)
                if before:
                    before(i)
                for kind, j, _x in tiles:
                    pb = 2 * (n % 2)
                    if n - first_tile[name] >= 2:
                        pe.wait_ge(S("tile_evacuated"), n - 1)
                    for k in range(kt):
                        se = dict(start=k == 0, stop=k == kt - 1)
                        if kind == "cm":
                            lw = w[:, k, 128 * j:128 * j + 128]
                            mm(PS[:, pb, 0:NS], lw, act(i, k)[:, 0:NS], **se)
                            last = mm(PS[:, pb + 1, 0:NP_], lw, act(i, k)[:, NS:T], **se)
                        elif kind == "tm":
                            last = mm(PS[:, pb, 0:cn], act(i, k)[:, 128 * _x:128 * _x + 128], w[:, k, :], **se)
                        else:
                            last = mm(PS[:, pb, 0:128], act(i, k)[:, 128 * _x:128 * _x + 128], w[:, k, 128:256], **se)
                    last.then_inc(S("tile_product"), 1)
                    n += 1

        def tile_list(name):
            n = first_tile[name]
            for i, (_, kt, cn, tiles) in enumerate(stages[name]):
                for t in tiles:
                    yield n, i, t
                    n += 1

        AROW = flat(U_S * T, 1024).rearrange("p (s n) -> p s n", s=2)
        def ada_bank(l, b):
            return 7 if l else 6 + b % 2

        def ada_rows_pe(pe, l, b):
            i = first_block[f"ada{l}"] + b
            pe.wait_ge(S(f"ring_loaded{i % 2}"), loaded_at[i])
            if b >= 2 - l:
                pe.wait_ge(S("ada_cols"), 12 * l + b - 1 + l)
            w = slot(i, 8, 512)
            for k in range(KT):
                st = 32 * (k % 4)
                last = mm(PS[st:st + 32, ada_bank(l, b), :], SCW[:, k, :], w[:, k, :], start=k < 4, stop=k >= 4)
            last.then_inc(S("tile_product"), 1)

        def ada_turn_pe(pe, l, b):
            pe.wait_ge(S("ada_rows"), 12 * l + b + 1)
            for j in range(4):
                ins = mm(PS[:, ada_bank(l, b), 2 * j:2 * j + 2], AROW[:, b % 2, 128 * j:128 * j + 128], con(C_SEL, 2))
            ins.then_inc(S("ada_turned"), 1)

        def ada_act(act, l, b):
            act.wait_ge(S("tile_product"), first_tile[f"ada{l}"] + b + 1)
            if b >= 2:
                act.wait_ge(S("ada_turned"), 12 * l + b - 1)
            A.activation(AROW[:, b % 2, :], PS[:, ada_bank(l, b), :], ACT.Copy).then_inc(S("ada_rows"), 1)

        def ada_cols_act(act, l, b):
            act.wait_ge(S("ada_turned"), 12 * l + b + 1)
            A.activation(ADAS[:, l, 4 * b:4 * b + 4, :].rearrange("p m g -> p (m g)"), PS[:, ada_bank(l, b), 0:8],
                         ACT.Copy).then_inc(S("ada_cols"), 1)

        def ada_pe(pe, l):
            for b in range(12):
                ada_rows_pe(pe, l, b)
                if b:
                    ada_turn_pe(pe, l, b - 1)
            ada_turn_pe(pe, l, 11)

        def ada_dve(dve, step, l):
            ADA = ADAS[:, l, :, :]
            dve.wait_ge(S("ada_cols"), 12 * l + 12)
            bias = PC[:, 0, R_ADAB + 48 * l:R_ADAB + 48 * l + 48]
            for g in range(2):
                step(V.tensor_tensor(ADA[:, :, g], ADA[:, :, g], bias, ALU.add))
            for w, (row, q) in enumerate(((R_N1, 8), (R_N2, 32))):
                for g in range(2):
                    step(V.scalar_tensor_tensor(GAIN[:, 2 * l + w, :, g], ADA[:, q:q + 8, g], 1.0,
                                                PC[:, 0, row + 8 * l:row + 8 * l + 8], ALU.add, ALU.mult))
            V.memset(SML[:, 20:21], 0.0).then_inc(S("tile_evacuated"), 12)

        norms = [0]

        def norm_act(act, step, i, w):
            X = unit(U_X, 8)
            for k in range(KT):
                if k >= 2:
                    act.wait_ge(S("norm_sum"), 8 * i + k - 1)
                A.activation(unit(U_S + k % 2), X[:, k, :], ACT.Square).then_inc(S("norm_square"), 1)
            act.wait_ge(S("norm_sum"), 8 * i + 8)
            r = unit(U_S + 2)
            step(A.activation(r, pair(0), ACT.Ln, bias=EPSC[:, 0:1]))
            A.activation(r, r, ACT.Exp, scale=-0.5).then_inc(S("norm_rms"), 1)
            H = unit(U_H, 8)
            sh = 0 if w == 0 else 24
            for k in range(KT):
                act.wait_ge(S("norm_scaled"), 8 * i + k + 1)
                for g, (t0, n) in enumerate(GROUPS):
                    ins = A.activation(H[:, k, t0:t0 + n], unit(U_S + 3 + k % 2)[:, t0:t0 + n], ACT.Identity,
                                       scale=GAIN[:, i, k, g:g + 1], bias=ADAS[:, i // 2, sh + k, g:g + 1])
                ins.then_inc(S("norm_out"), 1)

        def norm_pe(pe, i):
            for k in range(KT):
                pe.wait_ge(S("norm_square"), 8 * i + k + 1)
                sq = unit(U_S + k % 2)
                mm(PS[:, 0, 0:NS], con(C_MEAN), sq[:, 0:NS], start=k == 0, stop=k == 7)
                mm(PS[:, 1, 0:NP_], con(C_MEAN), sq[:, NS:T], start=k == 0, stop=k == 7).then_inc(S("norm_sum"), 1)

        def norm_dve(dve, i):
            X = unit(U_X, 8)
            dve.wait_ge(S("norm_rms"), i + 1)
            for k in range(KT):
                if k >= 2:
                    dve.wait_ge(S("norm_out"), 8 * i + k - 1)
                V.tensor_tensor(unit(U_S + 3 + k % 2), X[:, k, :], unit(U_S + 2), ALU.mult).then_inc(S("norm_scaled"), 1)

        def residual_dve(dve, name, gate):
            ADA = ADAS[:, int(name[-1]), :, :]
            X = unit(U_X, 8)
            for n, _, (_, j, m) in tile_list(name):
                dve.wait_ge(S("tile_product"), n + 1)
                pb = 2 * (n % 2)
                for g, (t0, c) in enumerate(GROUPS):
                    x = X[:, m, t0:t0 + c]
                    ins = V.scalar_tensor_tensor(x, PS[:, pb + g, 0:c], ADA[:, gate + m, g:g + 1], x, ALU.mult, ALU.add)
                ins.then_inc(S("tile_evacuated"), 1)

        def up_act(act, l):
            for n, _, (_, j, u) in tile_list(f"up{l}"):
                act.wait_ge(S("tile_product"), n + 1)
                A.activation(unit(u), pair(2 * (n % 2)), ACT.Relu).then_inc(S("tile_evacuated"), 1)

        def up_dve(dve, l):
            for n, _, (_, j, u) in tile_list(f"up{l}"):
                dve.wait_ge(S("tile_evacuated"), n + 1)
                V.tensor_tensor(unit(u), unit(u), unit(u), ALU.mult)

        def evac_act(act, name, func, tm_dst):
            for n, i, (kind, j, x) in tile_list(name):
                act.wait_ge(S("tile_product"), n + 1)
                pb = 2 * (n % 2)
                if kind == "cm":
                    ins = A.activation(unit(x), pair(pb), func(x))
                else:
                    dst, c = tm_dst(kind, j, x)
                    ins = A.activation(dst, PS[:, pb, 0:c], ACT.Copy)
                ins.then_inc(S("tile_evacuated"), 1)

        VA = unit(U_VA).rearrange("p (t c) -> p t c", t=TT_)
        COS = flat((U_S + 4) * T, NS)
        SIN = flat((U_S + 4) * T + NS, NS)
        KD = flat((U_S + 6) * T, 2 * 768).rearrange("p (k t) -> p k t", k=2)
        CK = flat((U_S + 9) * T, 256).rearrange("p (a c) -> p a c", a=2)
        KOUT = flat((U_S + 9) * T + 256, 128)
        PR = unit(U_S + 10, 2)
        PT = unit(U_S + 12, 2)

        def attn_prep_act(act, step):
            for t in range(5):
                u = unit(U_Q + t)
                if t >= 2:
                    act.wait_ge(S("qk_sum"), t - 1)
                A.activation(unit(U_S + t % 2), u, ACT.Square).then_inc(S("qk_square"), 1)
                act.wait_ge(S("qk_sum"), t + 1)
                r = unit(U_S + 2 + t % 2)
                if t >= 2:
                    act.wait_ge(S("qk_normed"), t - 1)
                step(A.activation(r, pair(2 * (t % 2)), ACT.Ln, bias=EPSC[:, 0:1]))
                A.activation(r, r, ACT.Exp, scale=-0.5).then_inc(S("qk_rms"), 1)
            act.wait_ge(S("key_out_psum"), 1)
            A.activation(KOUT, PS[:, 6, 0:128], ACT.Copy).then_inc(S("key_out"), 1)
            act.wait_ge(S("qk_roped"), 5)
            act.wait_ge(S("cache_key"), 1)
            K = unit(U_K)
            for kv in range(2):
                r0 = 64 * kv
                for half in range(2):
                    h = slice(64 * half, 64 * half + 64)
                    A.activation(KD[h, kv, 0:NS], K[r0:r0 + 64, 0:NS], ACT.Copy)
                    A.activation(KD[h, kv, NS:T], PS[r0:r0 + 64, 7, 0:128], ACT.Copy)
                    A.activation(KD[h, kv, T:768], K[r0:r0 + 64, NS:T], ACT.Copy)

        def attn_prep_pe(pe):
            for t in range(5):
                pe.wait_ge(S("qk_square"), t + 1)
                if t >= 2:
                    pe.wait_ge(S("qk_rms"), t - 1)
                sq, b = unit(U_S + t % 2), 2 * (t % 2)
                mm(PS[:, b, 0:NS], bd64, sq[:, 0:NS])
                mm(PS[:, b + 1, 0:NP_], bd64, sq[:, NS:T]).then_inc(S("qk_sum"), 1)
                if t >= 1:
                    rope_pe(pe, t - 1)
            rope_pe(pe, 4)
            nc.tensor.transpose(PS[:, 6, 0:128], unit(U_K)[:, NS:T], ident).then_inc(S("key_out_psum"), 1)
            pe.wait_ge(S("cache_loaded"), 32)
            nc.tensor.transpose(PS[:, 7, 0:128], CK[:, 0, :], ident).then_inc(S("cache_key"), 1)

        def rope_pe(pe, t):
            pe.wait_ge(S("qk_normed"), t + 1)
            if t >= 2:
                pe.wait_ge(S("qk_roped"), t - 1)
            mm(PS[:, 4 + t % 2, 0:NS], con(C_ROPE), unit(U_Q + t)[:, 0:NS]).then_inc(S("qk_swapped"), 1)

        def attn_prep_dve(dve, step):
            dve.wait_ge(S("rope_loaded"), 16)
            for t in range(5):
                u = unit(U_Q + t)
                col = PC[:, 2, R_QN:R_QN + 1] if t < 4 else PC[:, 2, R_KN:R_KN + 1]
                dve.wait_ge(S("qk_rms"), t + 1)
                V.scalar_tensor_tensor(u, u, col, unit(U_S + 2 + t % 2), ALU.mult, ALU.mult).then_inc(S("qk_normed"), 1)
                dve.wait_ge(S("qk_swapped"), t + 1)
                tmp = unit(U_S + 14)[:, 0:NS]
                step(V.tensor_tensor(tmp, PS[:, 4 + t % 2, 0:NS], SIN, ALU.mult))
                step(V.tensor_tensor(u[:, 0:NS], u[:, 0:NS], COS, ALU.mult))
                V.tensor_tensor(u[:, 0:NS], u[:, 0:NS], tmp, ALU.add).then_inc(S("qk_roped"), 1)
                dve.wait_ge(S("qk_roped"), t + 1)

        ATT = [(h, t) for h in range(8) for t in range(TT_)]
        NA = len(ATT)

        def keys_of(t):
            return T if t < 4 else 128

        def att_scores(n):
            h, t = ATT[n]
            r = slice(64 * (h % 2), 64 * (h % 2) + 64)
            q = unit(U_Q + h // 2)[r, 128 * t:128 * t + 128]
            kd = KD[r, h // 4, :]
            b = 2 * (n % 2)
            if t < 4:
                mm(PS[:, b, 0:NS], q, kd[:, 0:NS])
                return mm(PS[:, b + 1, 0:128], q, kd[:, NS:T])
            return mm(PS[:, b, 0:128], q, kd[:, T:768])

        def attn_pe(pe):
            def scores(n):
                if n >= 2:
                    pe.wait_ge(S("att_exp"), n - 1)
                att_scores(n).then_inc(S("att_scores"), 1)

            def turn(n):
                pe.wait_ge(S("att_probs"), n + 1)
                if n >= 1:
                    pe.wait_ge(S("att_pt"), n)
                for j in range(keys_of(ATT[n][1]) // 128):
                    ins = nc.tensor.transpose(pair(4)[:, 128 * j:128 * j + 128], PR[:, n % 2, 128 * j:128 * j + 128], ident)
                ins.then_inc(S("att_turned"), 1)

            def values(n):
                h, t = ATT[n]
                kt = keys_of(t) // 128
                pe.wait_ge(S("att_pt"), n + 1)
                if n:
                    pe.wait_ge(S("att_out"), n)
                r = slice(64 * (h % 2), 64 * (h % 2) + 64)
                vc = slice(64 * (h // 4), 64 * (h // 4) + 64)
                for j in range(kt):
                    v = VA[:, 4, vc] if t == 4 else (VA[:, j, vc] if j < 4 else CK[:, 1, vc])
                    ins = mm(att_out(n)[r, :], v, PT[:, n % 2, 128 * j:128 * j + 128], start=j == 0, stop=j == kt - 1)
                ins.then_inc(S("att_values"), 1)

            scores(0)
            for n in range(NA):
                if n + 1 < NA:
                    scores(n + 1)
                if n % 3 == 1 and n // 3 < 12:
                    ada_rows_pe(pe, 1, n // 3)
                turn(n)
                if n % 3 == 2 and n // 3 < 12:
                    ada_turn_pe(pe, 1, n // 3)
                if n:
                    values(n - 1)
            values(NA - 1)

        def att_out(n):
            return PS[:, 6, 0:128]

        def attn_dve(dve, step):
            def row_max(n):
                k = keys_of(ATT[n][1])
                dve.wait_ge(S("att_scores"), n + 1)
                if n >= 2:
                    dve.wait_ge(S("att_exp"), n - 1)
                st = SML[:, 4 * (n % 2):4 * (n % 2) + 4]
                step(V.tensor_reduce(st[:, 0:1], pair(2 * (n % 2), k), AXX, ALU.max))
                V.tensor_scalar(st[:, 1:2], st[:, 0:1], -ATTN_SCALE, None, ALU.mult).then_inc(S("att_max"), 1)

            row_max(0)
            for n in range(NA):
                k = keys_of(ATT[n][1])
                st = SML[:, 4 * (n % 2):4 * (n % 2) + 4]
                dve.wait_ge(S("att_exp"), n + 1)
                step(V.reciprocal(st[:, 3:4], st[:, 2:3]))
                V.tensor_scalar(PR[:, n % 2, 0:k], PR[:, n % 2, 0:k], st[:, 3:4], None, ALU.mult).then_inc(S("att_probs"), 1)
                if n + 1 < NA:
                    row_max(n + 1)
                dve.wait_ge(S("att_turned"), n + 1)
                if n >= 2:
                    dve.wait_ge(S("att_values"), n - 1)
                V.tensor_copy(PT[:, n % 2, 0:k], pair(4, k)).then_inc(S("att_pt"), 1)
            ada_dve(dve, step, 1)

        def attn_act(act):
            def head_out(n):
                h, t = ATT[n]
                r = slice(64 * (h % 2), 64 * (h % 2) + 64)
                act.wait_ge(S("att_values"), n + 1)
                A.activation(unit(U_MIX + h // 2)[r, 128 * t:128 * t + 128], att_out(n)[r, :],
                             ACT.Copy).then_inc(S("att_out"), 1)

            def exps(n):
                k = keys_of(ATT[n][1])
                st = SML[:, 4 * (n % 2):4 * (n % 2) + 4]
                act.wait_ge(S("att_max"), n + 1)
                if n >= 2:
                    act.wait_ge(S("att_turned"), n - 1)
                A.activation(PR[:, n % 2, 0:k], pair(2 * (n % 2), k), ACT.Exp, scale=ATTN_SCALE, bias=st[:, 1:2],
                             accum_out=st[:, 2:3]).then_inc(S("att_exp"), 1)

            exps(0)
            for n in range(NA):
                if n + 1 < NA:
                    exps(n + 1)
                if n % 3 == 1 and n // 3 < 12:
                    ada_act(act, 1, n // 3)
                if n % 3 == 2 and n // 3 < 12:
                    ada_cols_act(act, 1, n // 3)
                if n:
                    head_out(n - 1)
            head_out(NA - 1)

        VB = unit(U_VB, 4).rearrange("p u t -> p (u t)").rearrange("p (t c) -> p t c", t=TT_)
        EB, QD, KI, OD = unit(U_S, 2), unit(U_S + 2, 2), unit(U_S + 4, 2), unit(U_S + 6, 2)
        HT = unit(U_S + 8, 2)
        HGM = flat((U_S + 10) * T, 512).rearrange("p (s h c) -> p s h c", s=2, h=2)
        HKT = flat((U_S + 10) * T + 512, 256).rearrange("p (s c) -> p s c", s=2)
        HS = flat((U_S + 12) * T, 512).rearrange("p (d s v) -> p d s v", d=2, s=4)
        HS2 = flat((U_S + 12) * T + 512, 64)
        HU = [(p, i, d) for p in range(4) for i in range(5) for d in range(2)]

        def tile_of(i, d):
            return 4 if i == 4 else (i if d == 0 else 3 - i)

        def hgrn_pe(pe):
            n = 0
            for p in range(4):
                pe.wait_ge(S("hgrn_staged"), p + 1)
                for i in range(5):
                    for d in range(2):
                        t = tile_of(i, d)
                        tk = slice(128 * t, 128 * t + 128)
                        if n:
                            pe.wait_ge(S("hgrn_masked"), n)
                        for h in range(2):
                            r = slice(64 * h, 64 * h + 64)
                            ins = mm(PS[:, h, 0:128], KI[r, d, tk], QD[r, d, tk])
                        ins.then_inc(S("hgrn_scores"), 1)
                        if n:
                            pe.wait_ge(S("hgrn_key_rows"), n)
                        nc.tensor.transpose(PS[:, 2, 0:128], KI[:, d, tk], ident).then_inc(S("hgrn_turned"), 1)
                        pe.wait_ge(S("hgrn_masked"), n + 1)
                        if n:
                            pe.wait_ge(S("hgrn_out_a"), n)
                            pe.wait_ge(S("hgrn_out_b"), n)
                        for h in range(2):
                            r = slice(64 * h, 64 * h + 64)
                            mm(PS[r, 3 + h, 0:128], VB[:, t, 128 * p + 64 * h:128 * p + 64 * h + 64], HGM[:, n % 2, h, :],
                               start=True, stop=False)
                        pe.wait_ge(S("hgrn_key_rows"), n + 1)
                        for s in range(2):
                            c = s if d == 0 else 1 - s
                            k = 2 * n + s
                            pe.wait_ge(S("hgrn_state_init"), 4 * (p + 1))
                            pe.wait_ge(S("hgrn_state_load"), 32 * (p + 1))
                            if k:
                                pe.wait_ge(S("hgrn_state"), k - 1 if (s == 0 and d == 1) else k - 1)
                                pe.wait_ge(S("hgrn_state"), k)
                            st = HS[:, d, (2 if i == 4 else 0) + s, :]
                            for h in range(2):
                                r = slice(64 * h, 64 * h + 64)
                                ins = mm(PS[r, 3 + h, 64 * c:64 * c + 64], st[r, :], QD[r, d, 128 * t + 64 * c:128 * t + 64 * c + 64],
                                         start=False, stop=s == 1)
                            if s == 1:
                                ins.then_inc(S("hgrn_out_psum"), 1)
                            cr = slice(64 * c, 64 * c + 64)
                            for h in range(2):
                                r = slice(64 * h, 64 * h + 64)
                                ins = mm(PS[r, 5, 0:64], HKT[cr, n % 2, 64 * h:64 * h + 64],
                                         VB[cr, t, 128 * p + 64 * h:128 * p + 64 * h + 64])
                            ins.then_inc(S("hgrn_ds"), 1)
                        n += 1
                pe.wait_ge(S("hgrn_o_square"), p + 1)
                mm(PS[:, 6, 0:NS], bd64, HT[:, 0, 0:NS])
                mm(PS[:, 7, 0:NP_], bd64, HT[:, 0, NS:T]).then_inc(S("hgrn_o_sum"), 1)

        def hgrn_dve(dve, step):
            n = 0
            lb, oml = LB[:, 4, :], LB[:, 5, :]
            for p in range(4):
                q, g = unit(U_QB + p), unit(U_GB + p)
                dve.wait_ge(S("hgrn_sig"), 2 * p + 2)
                V.tensor_tensor(q, q, HT[:, 0, :], ALU.mult)
                step(V.tensor_tensor(g, g, HT[:, 1, :], ALU.mult))
                for d in range(2):
                    f = unit(U_F + 4 * d + p)
                    V.tensor_scalar(f, f, oml[:, p:p + 1], lb[:, p:p + 1], ALU.mult, ALU.add).then_inc(S("hgrn_f"), 1)
                for d in range(2):
                    f = unit(U_F + 4 * d + p)
                    dve.wait_ge(S("hgrn_log"), 2 * p + d + 1)
                    m = CON[:, C_SCAN:C_SCAN + T] if d == 0 else CON[:, C_SCAN + T:C_SCAN:-1]
                    x = HT[:, d, :] if d == 0 else HT[:, d, ::-1]
                    V.tensor_tensor_scan(EB[:, d, :] if d == 0 else EB[:, d, ::-1], m, x, 0.0,
                                         ALU.mult, ALU.add).then_inc(S("hgrn_cum"), 1)
                    step(V.tensor_scalar(f, f, -1.0, 1.0, ALU.mult, ALU.add))
                for d in range(2):
                    f = unit(U_F + 4 * d + p)
                    dve.wait_ge(S("hgrn_decay"), 2 * p + d + 1)
                    V.tensor_tensor(QD[:, d, :], q, EB[:, d, :], ALU.mult)
                    ins = V.tensor_tensor(KI[:, d, :], f, HT[:, d, :], ALU.mult)
                ins.then_inc(S("hgrn_staged"), 1)
                for i in range(5):
                    for d in range(2):
                        t = tile_of(i, d)
                        dve.wait_ge(S("hgrn_scores"), n + 1)
                        mask = con(C_HGRN + 128 * d).unsqueeze(1).broadcast_to([P, 2, 128])
                        V.tensor_tensor(HGM[:, n % 2, :, :], PS[:, 0:2, 0:128], mask, ALU.mult).then_inc(S("hgrn_masked"), 1)
                        for s in range(2):
                            k = 2 * n + s
                            c = s if d == 0 else 1 - s
                            s0 = (2 if i == 4 else 0) + s
                            s1 = (2 if i == 4 else 0) + 1 - s
                            e = 128 * t + 64 * c + (63 if d == 0 else 0)
                            dec = EB[:, d, e:e + 1]
                            dve.wait_ge(S("hgrn_state_load"), 32 * (p + 1))
                            dve.wait_ge(S("hgrn_state_init"), 4 * (p + 1))
                            if k:
                                dve.wait_ge(S("hgrn_state"), k)
                            step(V.tensor_scalar(HS2, HS[:, d, s0, :], dec, None, ALU.mult))
                            dve.wait_ge(S("hgrn_ds"), k + 1)
                            V.scalar_tensor_tensor(HS[:, d, s1, :], PS[:, 5, 0:64], dec, HS2, ALU.mult, ALU.add)\
                                .then_inc(S("hgrn_state"), 1)
                        dve.wait_ge(S("hgrn_out_psum"), n + 1)
                        V.tensor_copy(OD[64:128, d, 128 * t:128 * t + 128], PS[64:128, 4, 0:128]).then_inc(S("hgrn_out_b"), 1)
                        n += 1
                dve.wait_ge(S("hgrn_out_a"), n)
                dve.wait_ge(S("hgrn_out_b"), n)
                V.tensor_tensor(OD[:, 0, :], OD[:, 0, :], OD[:, 1, :], ALU.add).then_inc(S("hgrn_o"), 1)
                dve.wait_ge(S("hgrn_o_rms"), p + 1)
                step(V.scalar_tensor_tensor(OD[:, 0, :], OD[:, 0, :], PC[:, 2, R_GN:R_GN + 1], HT[:, 1, :], ALU.mult, ALU.mult))
                V.tensor_tensor(unit(U_MIX + 4 + p), OD[:, 0, :], g, ALU.mult).then_inc(S("hgrn_pair_done"), 1)

        def hgrn_act(act, step):
            act.wait_ge(S("kv_stored"), 32)
            n = 0
            for p in range(4):
                if p:
                    act.wait_ge(S("hgrn_pair_done"), p)
                A.activation(HT[:, 0, :], unit(U_QB + p), ACT.Sigmoid).then_inc(S("hgrn_sig"), 1)
                A.activation(HT[:, 1, :], unit(U_GB + p), ACT.Sigmoid).then_inc(S("hgrn_sig"), 1)
                for d in range(2):
                    act.wait_ge(S("hgrn_f"), 2 * p + d + 1)
                    A.activation(HT[:, d, :], unit(U_F + 4 * d + p), ACT.Ln).then_inc(S("hgrn_log"), 1)
                for d in range(2):
                    act.wait_ge(S("hgrn_cum"), 2 * p + d + 1)
                    A.activation(HT[:, d, :], EB[:, d, :], ACT.Exp, scale=-1.0)
                    A.activation(EB[:, d, :], EB[:, d, :], ACT.Exp).then_inc(S("hgrn_decay"), 1)
                for i in range(5):
                    for d in range(2):
                        t = tile_of(i, d)
                        act.wait_ge(S("hgrn_turned"), n + 1)
                        if n >= 2:
                            act.wait_ge(S("hgrn_ds"), 2 * (n - 1))
                        A.activation(HKT[:, n % 2, :], PS[:, 2, 0:128], ACT.Copy).then_inc(S("hgrn_key_rows"), 1)
                        act.wait_ge(S("hgrn_out_psum"), n + 1)
                        A.activation(OD[0:64, d, 128 * t:128 * t + 128], PS[0:64, 3, 0:128], ACT.Copy).then_inc(S("hgrn_out_a"), 1)
                        n += 1
                act.wait_ge(S("hgrn_o"), p + 1)
                A.activation(HT[:, 0, :], OD[:, 0, :], ACT.Square).then_inc(S("hgrn_o_square"), 1)
                act.wait_ge(S("hgrn_o_sum"), p + 1)
                step(A.activation(HT[:, 1, :], pair(6), ACT.Ln, bias=EPSC[:, 0:1]))
                A.activation(HT[:, 1, :], HT[:, 1, :], ACT.Exp, scale=-0.5).then_inc(S("hgrn_o_rms"), 1)

        def hgrn_pool(pool):
            for p in range(4):
                if p:
                    pool.wait_ge(S("hgrn_pair_done"), p)
                    pool.wait_ge(S("hgrn_final_out"), 32 * p)
                for d in range(2):
                    G.memset(HS[:, d, 2, :], 0.0).then_inc(S("hgrn_state_init"), 1)
                    G.memset(HS[:, d, 3, :], 0.0).then_inc(S("hgrn_state_init"), 1)

        def hgrn_sp(sp):
            for p in range(4):
                if p:
                    sp.wait_ge(S("hgrn_pair_done"), p)
                for d, n in enumerate(("state_hgrn_fwd", "state_hgrn_bwd")):
                    sp.dma_start(HS[:, d, 0, :], a[n][0, 0, 2 * p:2 * p + 2].rearrange("h k v -> (h k) v"))\
                        .then_inc(S("hgrn_state_load"), 16)
                sp.wait_ge(S("hgrn_pair_done"), p + 1)
                for d in range(2):
                    sp.dma_start(o["hgrn"][d][0, 0, 2 * p:2 * p + 2].rearrange("h k v -> (h k) v"), HS[:, d, 2, :])\
                        .then_inc(S("hgrn_final_out"), 16)

        spans = [[U_H * T, (U_H + 8) * T], [(U_MID + 3) * T, ARENA]]

        def take(n):
            for span in spans:
                if span[1] - span[0] >= n:
                    span[0] += n
                    return flat(span[0] - n, n)
            raise AssertionError("the arena is full")

        def sq4():
            return take(512).rearrange("p (u x) -> p u x", u=4)

        XI = [unit(U_XI, 8), unit(U_XI + 8, 8)]
        NSLOT = 12
        ARD = [take(NSLOT * 128).rearrange("p (c x) -> p c x", c=NSLOT) for _ in range(2)]
        BKD = [take(NSLOT * 128).rearrange("p (c x) -> p c x", c=NSLOT) for _ in range(2)]
        SV = [take(2 * 11 * 64).rearrange("p (h c v) -> p h c v", h=2, c=11) for _ in range(2)]
        UV = [take(2 * 10 * 64).rearrange("p (h c v) -> p h c v", h=2, c=10) for _ in range(2)]
        YD = [take(T) for _ in range(2)]
        BN = take(T)
        SW = [take(T) for _ in range(2)]
        BC = [take(T) for _ in range(2)]
        AD = [take(T) for _ in range(2)]
        KKN, SQ, RT = take(T), take(T), take(T)
        YS, YC = BC
        STL = take(128).rearrange("p (d k) -> p d k", d=2)
        STO = take(128).rearrange("p (d k) -> p d k", d=2)
        LW = take(256).rearrange("p (w c) -> p w c", w=2)
        G2 = take(256).rearrange("p (s c) -> p s c", s=2)
        XS = take(128).rearrange("p (d v) -> p d v", d=2)
        S2 = take(128).rearrange("p (d v) -> p d v", d=2)
        PE_ = take(40).rearrange("p (s d c) -> p s d c", s=2, d=2)
        Qm, Qd, QdT, Q2, QT2, P1, P2 = (sq4() for _ in range(7))
        TTs, BTs = [sq4(), sq4()], [sq4(), sq4()]
        Ls = [take(512).rearrange("p (h u x) -> p h u x", h=2, u=4) for _ in range(2)]
        Rs = [take(512).rearrange("p (h u x) -> p h u x", h=2, u=4) for _ in range(2)]

        R, K = unit(U_R, 8), unit(U_RK, 8)
        RV = unit(U_RV, 8).rearrange("p u t -> p (u t)").rearrange("p (t c) -> p t c", t=TT_)
        MID = unit(U_MID, 3)

        MIXES = [(0, 0, 2), (2, 2, 4), (3, 4, 6), (1, 6, 7), (4, 7, 8), (5, 8, 9)]

        def stage_of_block(i):
            return next(s for s, (_, b0, b1) in enumerate(MIXES) if b0 <= i < b1)

        def proj_tiles_upto(s):
            return first_tile["proj"] + sum(len(b[3]) for b in stages["proj"][:MIXES[s][2]])

        def proj_dve(dve, step):
            H = unit(U_H, 8)
            for s, (mrow, _, _) in enumerate(MIXES):
                xi = XI[s % 2]
                if s >= 2:
                    dve.wait_ge(S("tile_product"), proj_tiles_upto(s - 2))
                mix = PC[:, 1, R_MIX + 8 * mrow:R_MIX + 8 * mrow + 8]
                omm = SML[:, 8:16]
                step(V.tensor_scalar(omm, mix, -1.0, 1.0, ALU.mult, ALU.add))
                for k in range(KT):
                    step(V.tensor_scalar(xi[:, k, :], H[:, k, :], omm[:, k:k + 1], None, ALU.mult))
                    for t0, n in GROUPS:
                        dst, src = (t0 + 1, t0) if k < 4 else (t0, t0 + 1)
                        ins = V.scalar_tensor_tensor(xi[:, k, dst:dst + n - 1], H[:, k, src:src + n - 1], mix[:, k:k + 1],
                                                     xi[:, k, dst:dst + n - 1], ALU.mult, ALU.add)
                        step(ins) if (k, t0) != (KT - 1, NS) else ins.then_inc(S("mixed_input"), 1)
                dve.wait_ge(S("mixed_input"), s + 1)

        NB = 40
        UNITS = [(d, h) for d in range(2) for h in range(2)]
        PR_ = {k: i + 1 for i, k in enumerate(("QT", "Q2", "QT2", "Q4", "QT4", "P2", "QT8", "P3", "D", "DT", "NT", "H1", "H2", "H3"))}
        VE_ = {k: i + 1 for i, k in enumerate(("QA", "QB", "Qd", "Qo", "QT2", "QT4", "P2", "P3", "D", "H1", "H2", "H3"))}
        SC_ = {k: i + 1 for i, k in enumerate(("QT", "Q2", "Q4", "QT8", "DT", "NT"))}
        PO_ = {k: i + 1 for i, k in enumerate(("P1", "IQ"))}

        def chunk(i, d, h):
            return 2 * tile_of(i, d) + h

        def cslot(p, c):
            return c if c < 8 else c + 2 * (p % 2)

        def steps_of(n, s):
            return [chunk(n % 5, 0, s), chunk(n % 5, 1, 1 - s)], [s, 3 - s]

        def aside(n):
            p, i = n // 5, n % 5
            last, this, nxt = p - 1, p, p + 1
            r = [[("final", last), ("mean", last), ("var", last)],
                 [("gate", last), ("w0", nxt), ("w1", nxt)],
                 [("bonus", this), ("values", this), ("a0", nxt)],
                 [("a1", nxt), ("k_sum", nxt), ("state", nxt)],
                 []][i]
            return [x for x in r if 0 <= x[1] < 8]

        FIRST_ASIDE = [(x, 0) for x in ("w0", "w1", "a0", "a1", "k_sum", "state")]
        LAST_ASIDE = [(x, 7) for x in ("final", "mean", "var", "gate")]

        def evacuated(eng, item):
            kind, q = item
            sem, val = {"y": ("rwkv_y", 4 * q + 4), "final": ("rwkv_final", 2 * q + 2), "mean": ("rwkv_centred", q + 1),
                        "var": ("rwkv_y_rs", q + 1), "gate": ("rwkv_pair_done", q + 1), "w0": ("rwkv_sig", 4 * q + 1),
                        "w1": ("rwkv_sig", 4 * q + 2), "a0": ("rwkv_sig", 4 * q + 3), "a1": ("rwkv_sig", 4 * q + 4),
                        "bonus": ("rwkv_bonus", q + 1), "values": ("rwkv_bonus_v", q + 1),
                        "k_sum": ("rwkv_k_max", q + 1), "state": ("rwkv_state_in", 4 * q + 4)}[kind]
            eng.wait_ge(S(sem), val)

        def rwkv_pe(pe):
            before = [None]

            def wide(lhsT, rhs):
                mm(PS[:, 6, 0:NS], lhsT, rhs[:, 0:NS])
                return mm(PS[:, 7, 0:NP_], lhsT, rhs[:, NS:T])

            def side(item):
                kind, q = item
                if before[0]:
                    evacuated(pe, before[0])
                before[0] = item
                if kind in ("w0", "w1", "a0", "a1"):
                    w, d = "wa".index(kind[0]), int(kind[1])
                    pe.wait_ge(S("rwkv_weights"), 64 * (q + 1))
                    r = slice(64 * d, 64 * d + 64)
                    wide(LW[r, w, :], MID[r, w, :]).then_inc(S("rwkv_lora"), 1)
                elif kind == "k_sum":
                    pe.wait_ge(S("rwkv_k_square"), q + 1)
                    wide(bd64, SQ).then_inc(S("rwkv_k_sum"), 1)
                elif kind == "state":
                    for d in range(2):
                        for h in range(2):
                            r = slice(64 * h, 64 * h + 64)
                            ins = mm(PS[r, 6 + h, 64 * d:64 * d + 64], STL[r, d, :], CON[r, 64 * h:64 * h + 64])
                    ins.then_inc(S("rwkv_state_psum"), 1)
                elif kind == "final":
                    pe.wait_ge(S("rwkv_state"), 2 * (5 * q + 5))
                    for d in range(2):
                        for h in range(2):
                            r = slice(64 * h, 64 * h + 64)
                            ins = mm(PS[r, 6 + h, 64 * d:64 * d + 64], SV[d][r, h, 10, :], CON[r, 64 * h:64 * h + 64])
                    ins.then_inc(S("rwkv_final_psum"), 1)
                elif kind == "mean":
                    pe.wait_ge(S("rwkv_ysum"), q + 1)
                    wide(bd64, YS).then_inc(S("rwkv_mean"), 1)
                elif kind == "var":
                    pe.wait_ge(S("rwkv_yc_square"), q + 1)
                    wide(bd64, SQ).then_inc(S("rwkv_var"), 1)
                elif kind == "gate":
                    pe.wait_ge(S("rwkv_gate_weights"), 16 * (q + 1))
                    wide(G2[:, q % 2, :], MID[:, 2, :]).then_inc(S("rwkv_gate"), 1)
                elif kind == "bonus":
                    pe.wait_ge(S("rwkv_bonus_raw"), q + 1)
                    wide(bd64, BN).then_inc(S("rwkv_bonus_psum"), 1)
                elif kind == "values":
                    for t in range(TT_):
                        ins = nc.tensor.transpose(pair(6)[:, 128 * t:128 * t + 128], RV[:, t, 128 * q:128 * q + 128], ident)
                    ins.then_inc(S("rwkv_values_psum"), 1)

            def gram(n):
                q = n // 5
                pe.wait_ge(S("rwkv_staged"), q + 1)
                if n:
                    pe.wait_ge(S("inverse_vector"), 12 * n)
                for h in range(2):
                    r = slice(64 * h, 64 * h + 64)
                    for u, (d, hh) in enumerate(UNITS):
                        c = cslot(q, chunk(n % 5, d, hh))
                        ins = mm(PS[:, h, 128 * u:128 * u + 128], BKD[d][r, c, :], ARD[d][r, c, :])
                ins.then_inc(S("rwkv_gram"), 1)
                for u, (d, hh) in enumerate(UNITS):
                    ins = nc.tensor.transpose(PS[:, 2, 128 * u:128 * u + 128], BKD[d][:, cslot(q, chunk(n % 5, d, hh)), :], ident)
                ins.then_inc(S("rwkv_bk_turned"), 1)

            def prod(name, bank, lhsT, rhs):
                for u in range(4):
                    ins = mm(PS[:, bank, 128 * u:128 * u + 128], lhsT[:, u, :], rhs[:, u, :])
                ins.then_inc(S("inverse_products"), 1)

            def need(n, ve=None, sc=None, po=None):
                if ve:
                    pe.wait_ge(S("inverse_vector"), 12 * n + VE_[ve])
                if sc:
                    pe.wait_ge(S("inverse_scalar"), 6 * n + SC_[sc])
                if po:
                    pe.wait_ge(S("inverse_pool"), 2 * n + PO_[po])

            def inv_a(n):
                need(n, ve="Qd")
                for u in range(4):
                    ins = nc.tensor.transpose(PS[:, 3, 128 * u:128 * u + 128], Qd[:, u, :], ident)
                ins.then_inc(S("inverse_products"), 1)

            def inv_b(n):
                need(n, sc="QT")
                pe.wait_ge(S("rwkv_bt"), n + 1)
                prod("Q2", 2, QdT, Qd)
                prod("QT2", 3, Qd, QdT)

            def inv_c(n):
                need(n, ve="QT2", sc="Q2")
                pe.wait_ge(S("rwkv_masked"), 4 * (n + 1))
                prod("Q4", 0, QT2, Q2)
                prod("QT4", 1, Q2, QT2)
                need(n, po="P1")
                prod("P2", 2, QT2, P1)

            def inv_d(n):
                need(n, ve="QT4", sc="Q4")
                prod("QT8", 3, Qd, QdT)
                need(n, ve="P2")
                prod("P3", 0, QdT, P2)

            def inv_e(n):
                need(n, ve="P3", sc="QT8")
                prod("D", 1, Q2, QT2)
                need(n, po="IQ")
                prod("DT", 2, QT2, P1)

            def inv_f(n):
                need(n, sc="DT")
                prod("NT", 3, Qm, QdT)

            def inv_g(n):
                need(n, sc="NT", ve="D")
                prod("H1", 0, Q2, Qd)

            def inv_h(n):
                need(n, ve="H1")
                prod("H2", 1, Q2, QT2)

            def inv_i(n):
                need(n, ve="H2")
                prod("H3", 2, Q2, P2)

            def walk_x(n, s):
                (cs, us), k = steps_of(n, s), 2 * n + s
                pe.wait_ge(S("rwkv_state"), k)
                if s == 0:
                    pe.wait_ge(S("rwkv_masked"), 4 * (n + 1))
                    pe.wait_ge(S("rwkv_alpha"), 4 * (n + 1))
                    pe.wait_ge(S("inverse_vector"), 12 * (n + 1))
                    pe.wait_ge(S("rwkv_state_in"), 4 * (n // 5 + 1))
                    pe.wait_ge(S("rwkv_values_staged"), n // 5 + 1)
                    if n >= 0 and n % 5 == 4:
                        pe.wait_ge(S("rwkv_prompt_staged"), n // 5 + 1)
                for d in range(2):
                    for h in range(2):
                        ins = mm(PS[64 * h:64 * h + 64, 4, 64 * d:64 * d + 64], Ls[n % 2][:, h, us[d], :], SV[d][:, h, cs[d], :])
                ins.then_inc(S("rwkv_x_psum"), 1)

            def walk_u(n, s):
                (cs, us), k = steps_of(n, s), 2 * n + s
                pe.wait_ge(S("rwkv_x"), k + 1)
                for d in range(2):
                    ins = mm(PS[:, 5, 64 * d:64 * d + 64], TTs[n % 2][:, us[d], :], XS[:, d, :])
                ins.then_inc(S("rwkv_u_psum"), 1)

            def walk_s(n, s):
                (cs, us), k = steps_of(n, s), 2 * n + s
                pe.wait_ge(S("rwkv_u_a"), 2 * (k + 1))
                pe.wait_ge(S("rwkv_u_b"), 2 * (k + 1))
                for d in range(2):
                    for h in range(2):
                        ins = mm(PS[64 * h:64 * h + 64, 5, 128 + 64 * d:192 + 64 * d], BTs[n % 2][:, us[d], 64 * h:64 * h + 64],
                                 UV[d][:, h, cs[d], :])
                ins.then_inc(S("rwkv_s_psum"), 1)
                if s == 0 and before[0]:
                    evacuated(pe, before[0])
                for d in range(2):
                    for h in range(2):
                        r = slice(64 * h, 64 * h + 64)
                        out = PS[r, 6 + h, 64 * us[d]:64 * us[d] + 64]
                        mm(out, UV[d][:, h, cs[d], :], Rs[n % 2][:, h, us[d], :], start=True, stop=False)
                        ins = mm(out, SV[d][r, h, cs[d], :], ARD[d][r, cslot(n // 5, cs[d]), 64:128], start=False, stop=True)
                if s == 1:
                    ins.then_inc(S("rwkv_y_psum"), 1)
                    before[0] = ("y", n)

            for item in FIRST_ASIDE:
                side(item)
            for n in range(-1, NB):
                m = n + 1
                walk = [(f, s) for s in range(2) for f in (walk_x, walk_u, walk_s)] if n >= 0 else []
                inv = [gram, inv_a, inv_b, inv_c, inv_d, inv_e] if m < NB else []
                if n >= 0 and n % 5 == 4:
                    for f, s in walk:
                        f(n, s)
                    walk = []
                for x in range(6):
                    if inv:
                        inv[x](m)
                    if walk:
                        walk[x][0](n, walk[x][1])
                items = aside(n) if n >= 0 else []
                for x, f in enumerate((inv_f, inv_g, inv_h, inv_i)):
                    if m < NB:
                        f(m)
                    if x < len(items):
                        side(items[x])
            for item in LAST_ASIDE:
                side(item)

        def rwkv_act(act, step):
            def side(item):
                kind, q = item
                if kind in ("w0", "w1", "a0", "a1"):
                    w, d = "wa".index(kind[0]), int(kind[1])
                    if w == 1 and q:
                        act.wait_ge(S("rwkv_bonus_raw"), q)
                    if w == 0 and q:
                        act.wait_ge(S("rwkv_staged"), q)
                    act.wait_ge(S("rwkv_lora"), 4 * q + 2 * w + d + 1)
                    col = (R_W0, R_A0)[w] + 8 * d + q
                    A.activation((SW, AD)[w][d], pair(6), ACT.Sigmoid, bias=PC[:, 1, col:col + 1]).then_inc(S("rwkv_sig"), 1)
                elif kind == "k_sum":
                    act.wait_ge(S("rwkv_k_max"), q + 1)
                    step(A.activation(RT, RT, ACT.Sqrt, scale=64.0))
                    step(A.activation(RT, RT, ACT.Ln))
                    A.activation(RT, RT, ACT.Exp, scale=-1.0).then_inc(S("rwkv_k_rs"), 1)
                elif kind == "state":
                    act.wait_ge(S("rwkv_state_psum"), q + 1)
                    for d in range(2):
                        for h in range(2):
                            r = slice(64 * h, 64 * h + 64)
                            A.activation(SV[d][r, h, 7 * d, :], PS[r, 6 + h, 64 * d:64 * d + 64], ACT.Copy)\
                                .then_inc(S("rwkv_state_in"), 1)
                elif kind == "final":
                    act.wait_ge(S("rwkv_final_psum"), q + 1)
                    if q:
                        act.wait_ge(S("rwkv_final_out"), 64 * q)
                    for h in range(2):
                        r = slice(64 * h, 64 * h + 64)
                        A.activation(STO[r, :, :].rearrange("p d k -> p (d k)"), PS[r, 6 + h, 0:128], ACT.Copy)\
                            .then_inc(S("rwkv_final"), 1)
                elif kind == "mean":
                    act.wait_ge(S("rwkv_centred"), q + 1)
                    A.activation(SQ, YC, ACT.Square).then_inc(S("rwkv_yc_square"), 1)
                elif kind == "var":
                    act.wait_ge(S("rwkv_var"), q + 1)
                    step(A.activation(RT, pair(6), ACT.Ln, bias=EPSC[:, 1:2]))
                    A.activation(RT, RT, ACT.Exp, scale=-0.5).then_inc(S("rwkv_y_rs"), 1)

            def k_square(q):
                act.wait_ge(S("rwkv_k_raw"), q + 1)
                A.activation(SQ, KKN, ACT.Square).then_inc(S("rwkv_k_square"), 1)

            def decays(q):
                pr = 8 + 2 * (q % 2)
                if q:
                    act.wait_ge(S("rwkv_y_psum"), 5 * q - 1)
                for d in range(2):
                    act.wait_ge(S("rwkv_cum"), 2 * q + d + 1)
                    e = 63 if d == 0 else 0
                    for x0, src in ((64, BC[d]), (0, SW[d])):
                        sv = src.rearrange("p (c x) -> p c x", c=NCH)
                        for dst, c in ((ARD[d][:, 0:8, x0:x0 + 64], sv[:, 0:8, :]), (ARD[d][:, pr:pr + 2, x0:x0 + 64], sv[:, 8:10, :])):
                            step(A.activation(dst, c, ACT.Exp, scale=-DECAY))
                    step(A.activation(PE_[:, q % 2, d, 0:8], ARD[d][:, 0:8, 64 + e], ACT.Copy))
                    step(A.activation(PE_[:, q % 2, d, 8:10], ARD[d][:, pr:pr + 2, 64 + e], ACT.Copy))
                    A.activation(BC[d], BC[d], ACT.Exp, scale=DECAY).then_inc(S("rwkv_decays"), 1)

            def ev(n, name, bank, dst):
                act.wait_ge(S("inverse_products"), 14 * n + PR_[name])
                A.activation(dst.rearrange("p u x -> p (u x)"), PS[:, bank, :], ACT.Copy).then_inc(S("inverse_scalar"), 1)

            def bt(n):
                act.wait_ge(S("rwkv_bk_turned"), n + 1)
                if n >= 2:
                    act.wait_ge(S("rwkv_s_psum"), 2 * (n - 1))
                A.activation(BTs[n % 2].rearrange("p u x -> p (u x)"), PS[:, 2, :], ACT.Copy).then_inc(S("rwkv_bt"), 1)

            def inv_c(n):
                act.wait_ge(S("inverse_pool"), 2 * n + PO_["P1"])
                ev(n, "Q4", 0, Qd)

            def inv_d(n):
                act.wait_ge(S("inverse_products"), 14 * n + PR_["P2"])
                ev(n, "QT8", 3, Q2)

            def walk_x(n, s):
                k = 2 * n + s
                act.wait_ge(S("rwkv_x_psum"), k + 1)
                A.activation(XS.rearrange("p d v -> p (d v)"), PS[:, 4, 0:128], ACT.Copy).then_inc(S("rwkv_x"), 1)

            def walk_u(n, s):
                (cs, us), k = steps_of(n, s), 2 * n + s
                act.wait_ge(S("rwkv_u_psum"), k + 1)
                for d in range(2):
                    A.activation(UV[d][0:64, 0, cs[d], :], PS[0:64, 5, 64 * d:64 * d + 64], ACT.Copy).then_inc(S("rwkv_u_a"), 1)

            def walk_y(n, s):
                if s == 0:
                    return
                act.wait_ge(S("rwkv_y_psum"), n + 1)
                if n >= 5:
                    act.wait_ge(S("rwkv_ysum"), n // 5)
                for d in range(2):
                    t = tile_of(n % 5, d)
                    for h in range(2):
                        r = slice(64 * h, 64 * h + 64)
                        A.activation(YD[d][r, 128 * t:128 * t + 128], PS[r, 6 + h, 128 * d:128 * d + 128], ACT.Copy)\
                            .then_inc(S("rwkv_y"), 1)

            for item in FIRST_ASIDE:
                if item[0] == "k_sum":
                    k_square(0)
                side(item)
            decays(0)
            for n in range(-1, NB):
                m = n + 1
                walk = [(f, s) for s in range(2) for f in (walk_x, walk_u, walk_y)] if n >= 0 else []
                inv = [bt, lambda n: ev(n, "QT", 3, QdT), lambda n: ev(n, "Q2", 2, Q2), inv_c, inv_d,
                       lambda n: ev(n, "DT", 2, QdT)] if m < NB else []
                if n >= 0 and n % 5 == 4:
                    if m < NB:
                        decays(m // 5)
                    for f, s in walk:
                        f(n, s)
                    walk = []
                for x in range(6):
                    if inv:
                        inv[x](m)
                    if walk:
                        walk[x][0](n, walk[x][1])
                items = aside(n) if n >= 0 else []
                if m < NB:
                    ev(m, "NT", 3, Q2)
                for item in items:
                    if item[0] == "k_sum":
                        k_square(item[1])
                    side(item)
            for item in LAST_ASIDE:
                side(item)

        def rwkv_dve(dve, step):
            inv = S("inverse_vector")
            lo, hi, al = slice(0, 64), slice(64, 128), slice(0, 128)
            f = lambda x: x.rearrange("p u x -> p (u x)")
            bd = con(C_BD16).unsqueeze(1).broadcast_to([P, 4, 128])
            oka = SML[:, 16:17]

            def pcol(row, q):
                return PC[:, 1, row + q:row + q + 1]

            def cum(q, d):
                dve.wait_ge(S("rwkv_sig"), 4 * q + d + 1)
                m = CON[:, C_SCAN:C_SCAN + T] if d == 0 else CON[:, C_SCAN + T:C_SCAN:-1]
                x, y = (SW[d], BC[d]) if d == 0 else (SW[d][:, ::-1], BC[d][:, ::-1])
                step(V.tensor_tensor_scan(y, m, x, 0.0, ALU.mult, ALU.add))
                V.tensor_tensor(SW[d], BC[d], SW[d], ALU.subtract).then_inc(S("rwkv_cum"), 1)

            def k_raw(q):
                if q:
                    dve.wait_ge(S("rwkv_staged"), q)
                V.tensor_scalar(KKN, K[:, q, :], pcol(R_KK, q), None, ALU.mult).then_inc(S("rwkv_k_raw"), 1)

            def k_max(q):
                dve.wait_ge(S("rwkv_k_sum"), q + 1)
                V.tensor_scalar(RT, pair(6), 1e-24 / 64, None, ALU.max).then_inc(S("rwkv_k_max"), 1)

            def keys(q):
                step(V.tensor_scalar(oka, pcol(R_KA, q), -1.0, 1.0, ALU.mult, ALU.add))
                dve.wait_ge(S("rwkv_k_rs"), q + 1)
                step(V.tensor_tensor(KKN, KKN, RT, ALU.mult))
                dve.wait_ge(S("rwkv_sig"), 4 * q + 4)
                for d in range(2):
                    V.tensor_tensor((SQ, RT)[d], KKN, AD[d], ALU.mult)
                for d in range(2):
                    step(V.tensor_scalar(AD[d], AD[d], pcol(R_KA, q), oka, ALU.mult, ALU.add))
                for d in range(2):
                    step(V.tensor_tensor(AD[d], AD[d], K[:, q, :], ALU.mult))

            def staging(q, d):
                pr = 8 + 2 * (q % 2)
                dve.wait_ge(S("rwkv_decays"), 2 * q + d + 1)
                if q:
                    dve.wait_ge(S("rwkv_y_psum"), 5 * q - 1)
                v3 = lambda x: x.rearrange("p (c x) -> p c x", c=NCH)
                for sl, cc in ((slice(0, 8), slice(0, 8)), (slice(pr, pr + 2), slice(8, 10))):
                    rr, aa = ARD[d][:, sl, 64:128], ARD[d][:, sl, 0:64]
                    V.tensor_tensor(rr, rr, v3(R[:, q, :])[:, cc, :], ALU.mult)
                    V.scalar_tensor_tensor(aa, aa, -1.0, v3(KKN)[:, cc, :], ALU.mult, ALU.mult)
                    V.tensor_tensor(BKD[d][:, sl, 0:64], v3((SQ, RT)[d])[:, cc, :], v3(BC[d])[:, cc, :], ALU.mult)
                    ins = V.tensor_tensor(BKD[d][:, sl, 64:128], v3(AD[d])[:, cc, :], v3(BC[d])[:, cc, :], ALU.mult)
                ins.then_inc(S("rwkv_staged_half"), 1)
                if d == 1:
                    dve.wait_ge(S("rwkv_staged_half"), 2 * q + 2)
                    V.memset(SML[:, 17:18], 0.0).then_inc(S("rwkv_staged"), 1)

            def gram(n):
                dve.wait_ge(S("rwkv_gram"), n + 1)
                if n:
                    dve.wait_ge(S("inverse_products"), 14 * n)
                V.tensor_tensor(o4(Qm[lo, :, 0:64]), g4(0, lo, 0), m4(lo, 0), ALU.mult).then_inc(inv, 1)
                V.tensor_tensor(o4(Qm[hi, :, 64:128]), g4(1, lo, 0), m4(lo, 0), ALU.mult).then_inc(inv, 1)
                dve.wait_ge(inv, 12 * n + VE_["QB"])
                V.tensor_tensor(Qd, Qm, bd, ALU.mult).then_inc(inv, 1)
                dve.wait_ge(inv, 12 * n + VE_["Qd"])
                V.tensor_tensor(Qm, Qm, Qd, ALU.subtract).then_inc(inv, 1)

            def g4(bank, rows, c0):
                x = PS[rows, bank, :].rearrange("p (d h x) -> p d h x", d=2, h=2)
                return x[:, :, :, c0:c0 + 64]

            def m4(rows, c0):
                x = CON[rows, C_RWKV:C_RWKV + 256].rearrange("p (d x) -> p d x", d=2)[:, :, c0:c0 + 64]
                return x.unsqueeze(2).broadcast_to([rows.stop - rows.start, 2, 2, 64])

            def o4(x):
                return x.rearrange("p (d h) x -> p d h x", d=2)

            def masks(n):
                Lm, Rm, msk = Ls[n % 2], Rs[n % 2], S("rwkv_masked")
                if n >= 2:
                    dve.wait_ge(S("rwkv_y_psum"), n - 1)
                V.tensor_tensor(o4(Lm[hi, 0, :, :]), g4(0, hi, 0), m4(hi, 0), ALU.mult).then_inc(msk, 1)
                V.tensor_tensor(o4(Lm[lo, 1, :, :]), g4(1, hi, 0), m4(hi, 0), ALU.mult).then_inc(msk, 1)
                V.tensor_tensor(o4(Rm[:, 0, :, :]), g4(0, al, 64), m4(al, 64), ALU.mult).then_inc(msk, 1)
                V.tensor_tensor(o4(Rm[:, 1, :, :]), g4(1, al, 64), m4(al, 64), ALU.mult).then_inc(msk, 1)

            def ev(n, name, bank, dst, plus=None, mine=None):
                dve.wait_ge(S("inverse_products"), 14 * n + PR_[name])
                if mine:
                    dve.wait_ge(inv, 12 * n + VE_[mine])
                if plus is None:
                    ins = V.tensor_copy(f(dst), PS[:, bank, :])
                else:
                    ins = V.tensor_tensor(f(dst), PS[:, bank, :], f(plus), ALU.add)
                ins.then_inc(inv, 1)

            def inv_b(n):
                ev(n, "QT2", 3, QT2)

            def inv_c(n):
                ev(n, "QT4", 1, QdT)
                dve.wait_ge(S("inverse_pool"), 2 * n + PO_["P1"])
                ev(n, "P2", 2, P2, P1)

            def inv_d(n):
                ev(n, "P3", 0, QT2, P2, "P2")

            def inv_e(n):
                ev(n, "D", 1, Qd, QT2, "P3")

            def inv_g(n):
                dve.wait_ge(S("inverse_products"), 14 * n + PR_["DT"])
                ev(n, "H1", 0, QT2, Qd, "D")

            def inv_h(n):
                ev(n, "H2", 1, P2, Qd)

            def inv_i(n):
                ev(n, "H3", 2, TTs[n % 2], Qd)

            def walk_u(n, s):
                (cs, us), k = steps_of(n, s), 2 * n + s
                dve.wait_ge(S("rwkv_u_psum"), k + 1)
                for d in range(2):
                    V.tensor_copy(UV[d][0:64, 1, cs[d], :], PS[64:128, 5, 64 * d:64 * d + 64]).then_inc(S("rwkv_u_b"), 1)

            def walk_s(n, s):
                (cs, us), k = steps_of(n, s), 2 * n + s
                dve.wait_ge(S("rwkv_s_psum"), k + 1)
                dve.wait_ge(S("rwkv_s2"), 4 * (k + 1))
                for d in range(2):
                    nxt = {7: None, 9: 10}.get(cs[d], cs[d] + 1) if d == 0 else {0: None, 8: 10}.get(cs[d], cs[d] - 1)
                    for h in range(2):
                        r = slice(64 * h, 64 * h + 64)
                        if nxt is None:
                            continue
                        V.scalar_tensor_tensor(SV[d][r, h, nxt, :], PS[r, 5, 128 + 64 * d:192 + 64 * d],
                                               PE_[r, (n // 5) % 2, d, cs[d]:cs[d] + 1], S2[r, d, :], ALU.mult, ALU.add)
                V.memset(SML[:, 18:19], 0.0).then_inc(S("rwkv_state"), 1)

            def side(item):
                kind, q = item
                if kind == "k_sum":
                    k_max(q)
                elif kind == "mean":
                    dve.wait_ge(S("rwkv_mean"), q + 1)
                    V.tensor_tensor(YC, YS, pair(6), ALU.subtract).then_inc(S("rwkv_centred"), 1)
                elif kind == "gate":
                    dve.wait_ge(S("rwkv_gate"), q + 1)
                    V.tensor_tensor(R[:, q, :], YC, pair(6), ALU.mult).then_inc(S("rwkv_pair_done"), 1)
                elif kind == "bonus":
                    dve.wait_ge(S("rwkv_bonus_psum"), q + 1)
                    V.tensor_scalar(BN, pair(6), 64.0, None, ALU.mult).then_inc(S("rwkv_bonus"), 1)
                elif kind == "values":
                    dve.wait_ge(S("rwkv_bonus"), q + 1)
                    dve.wait_ge(S("rwkv_values_psum"), q + 1)
                    V.tensor_tensor(BN, BN, pair(6), ALU.mult).then_inc(S("rwkv_bonus_v"), 1)

            def y_sum(q):
                dve.wait_ge(S("rwkv_y"), 4 * (5 * q + 5))
                V.tensor_tensor(YS, YD[0], YD[1], ALU.add).then_inc(S("rwkv_ysum"), 1)
                dve.wait_ge(S("rwkv_ysum"), q + 1)

            def y_norm(q):
                dve.wait_ge(S("rwkv_y_rs"), q + 1)
                dve.wait_ge(S("rwkv_centred"), q + 1)
                step(V.tensor_tensor(YC, YC, RT, ALU.mult))
                step(V.tensor_scalar(YC, YC, pcol(R_LNW, q), pcol(R_LNB, q), ALU.mult, ALU.add))
                dve.wait_ge(S("rwkv_bonus_v"), q + 1)
                step(V.tensor_tensor(YC, YC, BN, ALU.add))

            def bonus_raw(q):
                step(V.tensor_tensor(BN, AD[0], AD[1], ALU.add))
                V.scalar_tensor_tensor(BN, BN, pcol(R_RK, q), R[:, q, :], ALU.mult, ALU.mult).then_inc(S("rwkv_bonus_raw"), 1)

            step(V.memset(Qm, 0.0))
            k_raw(0)
            cum(0, 0)
            cum(0, 1)
            k_max(0)
            keys(0)
            staging(0, 0)
            staging(0, 1)
            for n in range(-1, NB):
                m = n + 1
                p, i = n // 5, n % 5
                walk = [(w, s) for s in range(2) for w in (None, walk_u, walk_s)] if n >= 0 else []
                inv_ = [gram, masks, inv_b, inv_c, inv_d, inv_e] if m < NB else []
                if i == 0 and p > 0:
                    y_sum(p - 1)
                if i == 2 and p < 7:
                    cum(p + 1, 0)
                    cum(p + 1, 1)
                    k_raw(p + 1)
                if i == 4 and n >= 0:
                    if m < NB:
                        staging(p + 1, 0)
                    for w, s in walk:
                        if w:
                            w(n, s)
                        if s == 0 and w is walk_s and m < NB:
                            staging(p + 1, 1)
                    walk = []
                for x in range(6):
                    if inv_:
                        inv_[x](m)
                    if walk and walk[x][0]:
                        walk[x][0](n, walk[x][1])
                items = aside(n) if n >= 0 else []
                for x, g in enumerate((None, inv_g, inv_h, inv_i)):
                    if m < NB and g:
                        g(m)
                    if x < len(items):
                        side(items[x])
                if i == 0 and p > 0:
                    y_norm(p - 1)
                if i == 1:
                    bonus_raw(p)
                if i == 3 and p < 7:
                    keys(p + 1)
            y_sum(7)
            side(("mean", 7))
            y_norm(7)
            side(("gate", 7))

        def rwkv_pool(pool, step):
            idb = ident.unsqueeze(1).broadcast_to([P, 4, 128])

            def values(q, part):
                for d, h, par in [(d, h, par) for d in range(2) for h in range(2) for par in range(2)][4 * part:4 * part + 4]:
                    src = RV[64 * par:64 * par + 64, 0:4, 128 * q + 64 * h:128 * q + 64 * h + 64]
                    row = slice(64, 128) if h == 0 else slice(0, 64)
                    step(G.tensor_copy(SV[d][row, h, par:8:2, :], src))
                    ins = G.tensor_copy(UV[d][64:128, h, par:8:2, :], src)
                    if (d, h, par) == (1, 1, 1):
                        ins.then_inc(S("rwkv_values_staged"), 1)
                        pool.wait_ge(S("rwkv_values_staged"), q + 1)
                    else:
                        step(ins)

            def prompt_values(q):
                for d in range(2):
                    for h in range(2):
                        row = slice(64, 128) if h == 0 else slice(0, 64)
                        for par in range(2):
                            src = RV[64 * par:64 * par + 64, 4, 128 * q + 64 * h:128 * q + 64 * h + 64]
                            step(G.tensor_copy(SV[d][row, h, 8 + par, :], src))
                            step(G.tensor_copy(UV[d][64:128, h, 8 + par, :], src))
                        step(G.memset(SV[d][64 * h:64 * h + 64, h, 8 + d, :], 0.0))
                G.memset(SML[:, 19:20], 0.0).then_inc(S("rwkv_prompt_staged"), 1)
                pool.wait_ge(S("rwkv_prompt_staged"), q + 1)

            def s2(n, s):
                (cs, us), k = steps_of(n, s), 2 * n + s
                pool.wait_ge(S("rwkv_state"), k)
                pool.wait_ge(S("rwkv_state_in"), 4 * (n // 5 + 1))
                for d in range(2):
                    for h in range(2):
                        r = slice(64 * h, 64 * h + 64)
                        G.tensor_scalar(S2[r, d, :], SV[d][r, h, cs[d], :], PE_[r, (n // 5) % 2, d, cs[d]:cs[d] + 1], None, ALU.mult)\
                            .then_inc(S("rwkv_s2"), 1)
                        pool.wait_ge(S("rwkv_s2"), 4 * k + 2 * d + h + 1)

            def start(n):
                pool.wait_ge(S("inverse_vector"), 12 * n + VE_["Qd"])
                if n:
                    pool.wait_ge(S("inverse_products"), 14 * n)
                G.tensor_tensor(P1, Qd, idb, ALU.add).then_inc(S("inverse_pool"), 1)
                pool.wait_ge(S("inverse_pool"), 2 * n + 1)
                for d in range(2):
                    c = cslot(n // 5, 2 * tile_of(n % 5, d))
                    for h in range(2):
                        r = slice(64 * h, 64 * h + 64)
                        G.tensor_copy(Ls[n % 2][r, h, 2 * d:2 * d + 2, :], ARD[d][r, c:c + 2, 0:64]).then_inc(S("rwkv_alpha"), 1)
                        pool.wait_ge(S("rwkv_alpha"), 4 * n + 2 * d + h + 1)

            def iq(n):
                pool.wait_ge(S("inverse_scalar"), 6 * n + SC_["QT8"])
                pool.wait_ge(S("inverse_vector"), 12 * n + VE_["P2"])
                G.tensor_tensor(P1, Q2, idb, ALU.add).then_inc(S("inverse_pool"), 1)
                pool.wait_ge(S("inverse_pool"), 2 * n + 2)

            values(0, 0)
            values(0, 1)
            prompt_values(0)
            for n in range(-1, NB):
                m = n + 1
                p, i = n // 5, n % 5
                if n >= 0:
                    s2(n, 0)
                if i == 4 and n >= 0:
                    if m < NB:
                        pool.wait_ge(S("rwkv_y_psum"), n)
                        values(p + 1, 0)
                    s2(n, 1)
                    if m < NB:
                        values(p + 1, 1)
                        start(m)
                else:
                    if m < NB:
                        start(m)
                    if n >= 0:
                        s2(n, 1)
                if m < NB:
                    iq(m)
                if i == 1 and p > 0:
                    prompt_values(p)

        def rwkv_sp(sp):
            for q in range(10):
                c = slice(128 * q, 128 * q + 128)
                if q < 8:
                    if q:
                        sp.wait_ge(S("rwkv_sig"), 4 * q)
                        sp.wait_ge(S("rwkv_state_psum"), q)
                    for w, n in enumerate(("rwkv_w2", "rwkv_a2")):
                        sp.dma_start(LW[:, w, :], a[n][0, :, :, c].rearrange("d k n -> (d k) n")).then_inc(S("rwkv_weights"), 16)
                    for d, n in enumerate(("state_rwkv_fwd", "state_rwkv_bwd")):
                        sp.dma_start(STL[:, d, :], a[n][0, 0, 2 * q:2 * q + 2].rearrange("h v k -> (h v) k"))\
                            .then_inc(S("rwkv_weights"), 16)
                if q >= 2:
                    p = q - 2
                    sp.wait_ge(S("rwkv_final"), 2 * (p + 1))
                    for d in range(2):
                        for h in range(2):
                            r = slice(64 * h, 64 * h + 64)
                            sp.dma_start(o["rwkv"][d][0, 0, 2 * p + h], STO[r, d, :]).then_inc(S("rwkv_final_out"), 16)
                if q < 8:
                    if q >= 2:
                        sp.wait_ge(S("rwkv_pair_done"), q - 1)
                    sp.dma_start(G2[:, q % 2, :], a["rwkv_g2"][0, :, c]).then_inc(S("rwkv_gate_weights"), 16)

        XROWS = flat(U_H1 * T, TT_ * D).rearrange("p (t d) -> p t d", t=TT_)
        PROWS = flat(U_S * T, 3 * 128).rearrange("p (w c) -> p w c", w=3)

        def load_all(sp):
            sp.dma_start(con(0, C_END), a["constants"]).then_inc(S("const_loaded"), 16)
            rows = [(0, R_ADAB, a["ada_b"].rearrange("l (r p) -> (l r) p", p=P), 96),
                    (0, R_N1, a["norm1_w"].rearrange("l (r p) -> (l r) p", p=P), 16),
                    (0, R_N2, a["norm2_w"].rearrange("l (r p) -> (l r) p", p=P), 16),
                    (1, R_MIX, a["rwkv_mix"].rearrange("o i (r p) -> (o i r) p", p=P), 48),
                    (1, R_W0, a["rwkv_w0"].rearrange("o i (r p) -> (o i r) p", p=P), 16),
                    (1, R_A0, a["rwkv_a0"].rearrange("o i (r p) -> (o i r) p", p=P), 16),
                    (1, R_KK, a["rwkv_k_k"].rearrange("o (r p) -> (o r) p", p=P), 8),
                    (1, R_KA, a["rwkv_k_a"].rearrange("o (r p) -> (o r) p", p=P), 8),
                    (1, R_RK, a["rwkv_r_k"].rearrange("o (r h) n -> (o r) (h n)", h=2), 8),
                    (1, R_LNW, a["rwkv_ln_w"].rearrange("o (r p) -> (o r) p", p=P), 8),
                    (1, R_LNB, a["rwkv_ln_b"].rearrange("o (r p) -> (o r) p", p=P), 8),
                    (2, R_C, a["c"].rearrange("o (r p) -> (o r) p", p=P), 8),
                    (2, R_C + 8, a["c_ctx"].rearrange("(r p) -> r p", p=P), 8),
                    (2, R_LB, a["hgrn_lb"].rearrange("o (r p) -> (o r) p", p=P), 8)]
            for w, r, src, n in rows:
                sp.dma_start(PROWS[r:r + n, w, :], src).then_inc(S("rows_loaded"), 16)
            for r, name in ((R_QN, "attn_q_norm"), (R_KN, "attn_k_norm"), (R_GN, "hgrn_g_norm")):
                for h in range(2):
                    sp.dma_start(PROWS[r:r + 1, 2, 64 * h:64 * h + 64], a[name]).then_inc(S("rows_loaded"), 16)
            sp.dma_start(XROWS[:, 0:4, :], a["x_sample"][0].rearrange("(t p) d -> p t d", p=P)).then_inc(S("x_loaded"), 16)
            sp.dma_start(XROWS[:, 4, :], a["x_prompt"][0]).then_inc(S("x_loaded"), 16)
        ROWS = 16 * 20

        def setup_pe(pe):
            pe.wait_ge(S("const_loaded"), 16)
            pe.wait_ge(S("rows_loaded"), ROWS)
            for w, n in enumerate((P, R1, R2)):
                ins = nc.tensor.transpose(PS[:, 7, 128 * w:128 * w + n], PROWS[0:n, w, :], ident[0:n, 0:n])
            ins.then_inc(S("params_psum"), 1)
            pe.wait_ge(S("x_loaded"), 32)
            for k in range(KT):
                b = 2 * (k % 2)
                if k >= 2:
                    pe.wait_ge(S("x_in"), k - 1)
                for t in range(TT_):
                    ins = nc.tensor.transpose(pair(b)[:, 128 * t:128 * t + 128], XROWS[:, t, 128 * k:128 * k + 128], ident)
                ins.then_inc(S("x_turned"), 1)

        def setup_act(act, step):
            act.wait_ge(S("params"), 3)
            c = PC[:, 2, R_C:R_C + 16].rearrange("p (g k) -> p g k", g=2)
            A.activation(SC, c, ACT.Sigmoid).then_inc(S("sig_c"), 1)
            act.wait_ge(S("lb_max"), 1)
            step(A.activation(LB[:, 0, :], LB[:, 2, :], ACT.Exp))
            A.activation(LB[:, 1, :], LB[:, 3, :], ACT.Exp).then_inc(S("lb_exp"), 1)
            for k in range(KT):
                act.wait_ge(S("x_turned"), k + 1)
                A.activation(unit(U_X + k), pair(2 * (k % 2)), ACT.Copy).then_inc(S("x_in"), 1)

        def setup_dve(dve, step):
            step(V.memset(EPSC[:, 0:1], EPS))
            step(V.memset(EPSC[:, 1:2], LN_X_EPS))
            dve.wait_ge(S("params_psum"), 1)
            for w, n in enumerate((P, R1, R2)):
                V.tensor_copy(PC[:, w, 0:n], PS[:, 7, 128 * w:128 * w + n]).then_inc(S("params"), 1)
            dve.wait_ge(S("params"), 3)
            l0, l1 = PC[:, 2, R_LB:R_LB + 4], PC[:, 2, R_LB + 4:R_LB + 8]
            step(V.tensor_tensor(LB[:, 4, :], l0, l1, ALU.max))
            V.tensor_tensor(LB[:, 2, :], l0, LB[:, 4, :], ALU.subtract)
            V.tensor_tensor(LB[:, 3, :], l1, LB[:, 4, :], ALU.subtract).then_inc(S("lb_max"), 1)
            dve.wait_ge(S("sig_c"), 1)
            c = PC[:, 2, R_C:R_C + 16].rearrange("p (g k) -> p g k", g=2)
            step(V.memset(SCW, 0.0))
            step(V.tensor_tensor(SCW[:, :, 0:2].rearrange("p k g -> p g k"), SC, c, ALU.mult))
            dve.wait_ge(S("lb_exp"), 1)
            step(V.tensor_tensor(LB[:, 1, :], LB[:, 0, :], LB[:, 1, :], ALU.add))
            step(V.reciprocal(LB[:, 1, :], LB[:, 1, :]))
            step(V.tensor_tensor(LB[:, 4, :], LB[:, 0, :], LB[:, 1, :], ALU.mult))
            step(V.tensor_scalar(LB[:, 5, :], LB[:, 4, :], -1.0, 1.0, ALU.mult, ALU.add))

        def out_pe(pe):
            for t in range(TT_):
                for b in range(2):
                    i = 2 * t + b
                    if i >= 2:
                        pe.wait_ge(S("rows_out"), i - 1)
                    for k in range(4):
                        ins = nc.tensor.transpose(PS[:, b, 128 * k:128 * k + 128],
                                                  unit(U_X + 4 * b + k)[:, 128 * t:128 * t + 128], ident)
                    ins.then_inc(S("rows_turned"), 1)

        def out_act(act):
            for i in range(2 * TT_):
                act.wait_ge(S("rows_turned"), i + 1)
                A.activation(XROWS[:, i // 2, 512 * (i % 2):512 * (i % 2) + 512], PS[:, i % 2, :], ACT.Copy)\
                    .then_inc(S("rows_out"), 1)

        def out_sp(sp):
            for t in range(TT_):
                sp.wait_ge(S("rows_out"), 2 * t + 2)
                dst = o["y_sample"][0, 128 * t:128 * t + 128] if t < 4 else o["y_prompt"][0]
                sp.dma_start(dst, XROWS[:, t, :]).then_inc(S("y_stored"), 16)
            sp.wait_ge(S("y_stored"), 16 * TT_)
            sp.wait_ge(S("hgrn_final_out"), 4 * 32)
            sp.wait_ge(S("rwkv_final_out"), 8 * 64)
            sp.wait_ge(S("kv_stored"), 32)

        block = ctx.enter_context(nc.Block())

        @block.sync
        def _(sp):
            load_all(sp)
            load_blocks(sp, "ada0")
            load_blocks(sp, "in")
            sp.wait_ge(S("stage_done"), 4 * 4)
            sp.dma_start(flat((U_S + 4) * T, 2 * NS), a["rope"]).then_inc(S("rope_loaded"), 16)
            sp.dma_start(CK[:, 0, :], a["cache_attn_k"][0, 0].rearrange("t h c -> t (h c)")).then_inc(S("cache_loaded"), 16)
            sp.dma_start(CK[:, 1, :], a["cache_attn_v"][0, 0].rearrange("t h c -> t (h c)")).then_inc(S("cache_loaded"), 16)
            sp.wait_ge(S("key_out"), 1)
            sp.dma_start(o["k"][0, 0].rearrange("t h c -> t (h c)"), KOUT).then_inc(S("kv_stored"), 16)
            sp.dma_start(o["v"][0, 0].rearrange("t h c -> t (h c)"), VA[:, 4, :]).then_inc(S("kv_stored"), 16)
            load_blocks(sp, "ada1")
            sp.wait_ge(S("kv_stored"), 32)
            sp.wait_ge(S("stage_done"), 4 * 6)
            hgrn_sp(sp)
            for name in ("out0", "up0", "down0", "proj"):
                load_blocks(sp, name)
            sp.wait_ge(S("stage_done"), 4 * 13)
            rwkv_sp(sp)
            sp.wait_ge(S("stage_done"), 4 * 14)
            for name in ("out1", "up1", "down1"):
                load_blocks(sp, name)
            out_sp(sp)

        def act_h(i, k):
            return unit(U_H + k)

        @block.tensor
        def _(pe):
            setup_pe(pe)
            stage_end(pe, "pe")
            ada_pe(pe, 0)
            stage_end(pe, "pe")
            norm_pe(pe, 0)
            stage_end(pe, "pe")
            products(pe, "in", act_h)
            stage_end(pe, "pe")
            attn_prep_pe(pe)
            stage_end(pe, "pe")
            attn_pe(pe)
            stage_end(pe, "pe")
            hgrn_pe(pe)
            stage_end(pe, "pe")
            products(pe, "out0", lambda i, k: unit(U_MIX + k))
            stage_end(pe, "pe")
            norm_pe(pe, 1)
            stage_end(pe, "pe")
            products(pe, "up0", act_h)
            stage_end(pe, "pe")
            products(pe, "down0", lambda i, k: unit(U_H1 + k))
            stage_end(pe, "pe")
            norm_pe(pe, 2)
            stage_end(pe, "pe")
            products(pe, "proj", lambda i, k: XI[stage_of_block(i) % 2][:, k, :],
                     before=lambda i: pe.wait_ge(S("mixed_input"), stage_of_block(i) + 1))
            stage_end(pe, "pe")
            rwkv_pe(pe)
            stage_end(pe, "pe")
            products(pe, "out1", lambda i, k: unit(U_R + k))
            stage_end(pe, "pe")
            norm_pe(pe, 3)
            stage_end(pe, "pe")
            products(pe, "up1", act_h)
            stage_end(pe, "pe")
            products(pe, "down1", lambda i, k: unit(U_H1 + k))
            stage_end(pe, "pe")
            out_pe(pe)

        @block.vector
        def _(dve):
            step = Steps(dve, "vector_step")
            setup_dve(dve, step)
            stage_end(dve, "dve")
            ada_dve(dve, step, 0)
            stage_end(dve, "dve")
            norm_dve(dve, 0)
            stage_end(dve, "dve")
            stage_end(dve, "dve")
            attn_prep_dve(dve, step)
            stage_end(dve, "dve")
            attn_dve(dve, step)
            stage_end(dve, "dve")
            hgrn_dve(dve, step)
            stage_end(dve, "dve")
            residual_dve(dve, "out0", 16)
            stage_end(dve, "dve")
            norm_dve(dve, 1)
            stage_end(dve, "dve")
            up_dve(dve, 0)
            stage_end(dve, "dve")
            residual_dve(dve, "down0", 40)
            stage_end(dve, "dve")
            norm_dve(dve, 2)
            stage_end(dve, "dve")
            proj_dve(dve, step)
            stage_end(dve, "dve")
            rwkv_dve(dve, step)
            stage_end(dve, "dve")
            residual_dve(dve, "out1", 16)
            stage_end(dve, "dve")
            norm_dve(dve, 3)
            stage_end(dve, "dve")
            up_dve(dve, 1)
            stage_end(dve, "dve")
            residual_dve(dve, "down1", 40)
            stage_end(dve, "dve")

        @block.scalar
        def _(act):
            step = Steps(act, "scalar_step")
            setup_act(act, step)
            stage_end(act, "act")
            for b in range(12):
                ada_act(act, 0, b)
                if b:
                    ada_cols_act(act, 0, b - 1)
            ada_cols_act(act, 0, 11)
            stage_end(act, "act")
            norm_act(act, step, 0, 0)
            stage_end(act, "act")
            evac_act(act, "in", lambda u: ACT.Sigmoid if U_F <= u < U_F + 8 else ACT.Copy,
                     lambda kind, j, t: (VB[:, t, :], 512) if kind == "tm" else (VA[:, t, :], 128))
            stage_end(act, "act")
            attn_prep_act(act, step)
            stage_end(act, "act")
            attn_act(act)
            stage_end(act, "act")
            hgrn_act(act, step)
            stage_end(act, "act")
            stage_end(act, "act")
            norm_act(act, step, 1, 1)
            stage_end(act, "act")
            up_act(act, 0)
            stage_end(act, "act")
            stage_end(act, "act")
            norm_act(act, step, 2, 0)
            stage_end(act, "act")
            evac_act(act, "proj", lambda u: {U_MID: ACT.Tanh, U_MID + 2: ACT.Sigmoid}.get(u, ACT.Copy),
                     lambda kind, j, t: (RV[:, t, 512 * j:512 * j + 512], 512))
            stage_end(act, "act")
            rwkv_act(act, step)
            stage_end(act, "act")
            stage_end(act, "act")
            norm_act(act, step, 3, 1)
            stage_end(act, "act")
            up_act(act, 1)
            stage_end(act, "act")
            stage_end(act, "act")
            out_act(act)

        @block.gpsimd
        def _(pool):
            step = Steps(pool, "pool_step")
            for i in range(6):
                stage_end(pool, "pool")
            hgrn_pool(pool)
            for i in range(7):
                stage_end(pool, "pool")
            rwkv_pool(pool, step)
            for i in range(5):
                stage_end(pool, "pool")


_IN = ["x_prompt", "x_sample", "cache_attn_k", "cache_attn_v", "state_hgrn_fwd", "state_hgrn_bwd", "state_rwkv_fwd",
       "state_rwkv_bwd", "c", "c_ctx", "ada_w", "ada_b", "norm1_w", "norm2_w", "ab_w_in", "ab_w_out", "attn_q_norm",
       "attn_k_norm", "hgrn_lb", "hgrn_g_norm", "rwkv_mix", "rwkv_wr", "rwkv_wk", "rwkv_wv", "rwkv_wo", "rwkv_w0",
       "rwkv_w1", "rwkv_w2", "rwkv_a0", "rwkv_a1", "rwkv_a2", "rwkv_g1", "rwkv_g2", "rwkv_k_k", "rwkv_k_a", "rwkv_r_k",
       "rwkv_ln_w", "rwkv_ln_b", "mlp_w1", "mlp_w2"]
_OUT = [("y_prompt", (1, 128, 1024)), ("y_sample", (1, 512, 1024)), ("new_attn_k", (1, 1, 128, 2, 64)),
        ("new_attn_v", (1, 1, 128, 2, 64)), ("new_hgrn_fwd", (1, 1, 8, 64, 64)), ("new_hgrn_bwd", (1, 1, 8, 64, 64)),
        ("new_rwkv_fwd", (1, 1, 16, 64, 64)), ("new_rwkv_bwd", (1, 1, 16, 64, 64))]


def kernel(**inputs):
    import concourse.bacc as bacc
    from concourse.bass_utils import run_bass_kernel_spmd as run

    nc = bacc.Bacc("TRN2", target_bir_lowering=False, num_devices=1)
    arrays = {n: np.ascontiguousarray(inputs[n]) for n in _IN}
    arrays["constants"] = constants()
    arrays["rope"] = rope_tables()
    arrays = {"in_" + n: v for n, v in arrays.items()}
    a = {n[3:]: nc.dram_tensor(n, v.shape, F32, kind="ExternalInput").ap() for n, v in arrays.items()}
    outs = {n: nc.dram_tensor("out_" + n, s, F32, kind="ExternalOutput").ap() for n, s in _OUT}
    o = {"y_prompt": outs["y_prompt"], "y_sample": outs["y_sample"], "k": outs["new_attn_k"], "v": outs["new_attn_v"],
         "hgrn": (outs["new_hgrn_fwd"], outs["new_hgrn_bwd"]), "rwkv": (outs["new_rwkv_fwd"], outs["new_rwkv_bwd"])}
    program(nc, a, o)
    r = run(nc, [arrays], core_ids=[0])
    return tuple(r.results[0]["out_" + n] for n, _ in _OUT)
```

```python
from contextlib import ExitStack

import numpy as np

import concourse.bass as bass
from concourse import mybir

F32 = mybir.dt.float32
F32R = mybir.dt.float32r
ALU = mybir.AluOpType
ACT = mybir.ActivationFunctionType
AXX = mybir.AxisListType.X

P = 128
D = 1024
KT = D // P
NS, NP_ = 512, 128
T = NS + NP_
TT_ = T // P
DFF = 4096
HD = 64
CH = 64
NCH = T // CH
EPS = 1e-6
LN_X_EPS = 64e-5
DECAY = float(np.exp(-0.5))
ATTN_SCALE = HD ** -0.5
LAYERS = 2

C_ID, C_MEAN, C_BD64, C_BD16, C_ROPE, C_RWKV, C_HGRN, C_SEL, C_SCAN, C_END = (
    0, 128, 256, 384, 512, 640, 896, 1152, 1154, 1154 + T + 1)


def constants():
    c = np.zeros((P, C_END), np.float32)
    i, j = np.arange(P)[:, None], np.arange(P)[None, :]
    c[:, C_ID:C_ID + P] = i == j
    c[:, C_MEAN:C_MEAN + P] = 1.0 / D
    c[:, C_BD64:C_BD64 + P] = (i // 64 == j // 64) / 64.0
    c[:, C_BD16:C_BD16 + P] = i // 16 == j // 16
    c[:, C_ROPE:C_ROPE + P] = (i == j - 1) * (j % 2 == 1) - 1.0 * (i == j + 1) * (j % 2 == 0)
    s, t = i % 64, j % 64
    c[:, C_RWKV:C_RWKV + P] = np.where(j < 64, s < t, s <= t)
    c[:, C_RWKV + P:C_RWKV + 2 * P] = np.where(j < 64, s > t, s >= t)
    same = i // 64 == j // 64
    c[:, C_HGRN:C_HGRN + P] = same & (i <= j)
    c[:, C_HGRN + P:C_HGRN + 2 * P] = same & (i >= j)
    c[:, C_SEL:C_SEL + 2] = i % 32 == np.arange(2)[None, :]
    c[:, C_SCAN:] = np.arange(T + 1)[None, :] % CH != 0
    return c


def rope_tables():
    tok = np.arange(NS)
    inv = (np.float32(10000.0) ** (-np.arange(0, 32, 2, dtype=np.float32) / np.float32(32))).astype(np.float32)
    ang = np.concatenate([(tok // 64).astype(np.float32)[:, None] * inv,
                          (tok % 64).astype(np.float32)[:, None] * inv], axis=-1)
    both = np.stack([np.cos(ang), np.sin(ang)]).astype(np.float32)
    both = np.repeat(both, 2, axis=2)
    both = np.concatenate([both, both], axis=2)
    return np.ascontiguousarray(both.transpose(2, 0, 1)).reshape(P, 2 * NS)


R_ADAB, R_N1, R_N2 = 0, 96, 112
R_MIX, R_W0, R_A0, R_KK, R_KA, R_RK, R_LNW, R_LNB, R1 = 0, 48, 64, 80, 88, 96, 104, 112, 120
R_C, R_LB, R_QN, R_KN, R_GN, R2 = 0, 16, 24, 25, 26, 27

U_X, U_H = 0, 8
U_Q, U_K, U_VA, U_QB, U_F, U_VB, U_GB = 16, 20, 21, 22, 26, 34, 38
U_MIX = 42
U_S = 50
U_R, U_RK, U_RV, U_MID, U_XI = 16, 24, 32, 40, 43
RING = 65 * T
SLOT = 4096
ARENA = RING + 2 * SLOT
SBUF_TOP = 229344

HIDT = DFF // 2 // P
WB = 2048
M_NH = 8 * T
M_NL = M_NH + KT * NS
M_NP = M_NL + KT * NS
M_HH = M_NP + KT * NP_
M_HL = M_HH + HIDT * NS
M_HP = M_HL + HIDT * NS
M_TMP = M_HP + HIDT * NP_
M_RAW = ARENA - 7 * WB
M_WH = M_RAW + 3 * WB
M_WL = M_WH + 2 * WB


def program(nc, a, o):
    with ExitStack() as ctx:
        def sb(name, shape):
            return ctx.enter_context(nc.sbuf_tensor(name, shape, F32))

        def in_arena(name, offset, shape, dtype=F32):
            return nc.alloc_sbuf_tensor_at(name, shape, dtype, offset=SBUF_TOP - 4 * (ARENA - offset))

        AR = in_arena("arena", 0, [P, ARENA])[:, :]
        CON = sb("constants", [P, C_END + 1])[:, :]
        PC = sb("param_cols", [P, 3, P])
        ADAS = sb("ada", [P, LAYERS, 48, 2])
        SC = sb("silu_c", [P, 2, KT])[:, :, :]
        SCW = sb("silu_c_rows", [P, KT, 32])[:, :, :]
        GAIN = sb("gain", [P, 2 * LAYERS, KT, 2])
        LB = sb("lower_bound", [P, 6, 4])
        SML = sb("small", [P, 32])
        EPSC = sb("eps_cols", [P, 4])
        DONE = sb("done", [P, 1])[:, :]
        PS = ctx.enter_context(nc.psum_tensor("psum", [P, 8, 512], F32))

        sems = {}

        def S(name):
            if name not in sems:
                sems[name] = ctx.enter_context(nc.semaphore(name))
            return sems[name]

        def unit(u, n=1):
            return AR[:, u * T:(u + n) * T] if n == 1 else AR[:, u * T:(u + n) * T].rearrange("p (u t) -> p u t", u=n)

        def flat(off, n):
            return AR[:, off:off + n]

        def pair(b, n=T):
            return PS[:, b:b + 2, :].rearrange("p b n -> p (b n)")[:, 0:n]

        def con(c, n=P):
            return CON[:, c:c + n]

        ident = con(C_ID)
        bd64 = con(C_BD64)
        GROUPS = ((0, NS), (NS, NP_))

        stage = {}

        def stage_end(eng, key):
            eng.drain().then_inc(S("stage_done"), 1)
            stage[key] = stage.get(key, 0) + 1
            eng.wait_ge(S("stage_done"), 4 * stage[key])

        def mm(out, lhsT, rhs, start=True, stop=True):
            return nc.tensor.matmul(out, lhsT, rhs, start=start, stop=stop)

        class Steps:

            def __init__(self, eng, name):
                self.eng, self.sem, self.n = eng, S(name), 0

            def __call__(self, ins):
                self.n += 1
                ins.then_inc(self.sem, 1)
                self.eng.wait_ge(self.sem, self.n)

        V, A, G = nc.vector, nc.scalar, nc.gpsimd

        def cols(w, c0, n):
            return w[:, c0:c0 + n].rearrange("(k p) n -> p k n", p=P)

        def cm_tiles(m0, n):
            return [("cm", j, m0 + j) for j in range(n)]

        stages = {}
        order = []

        def add_stage(name, blocks):
            stages[name] = blocks
            order.append(name)

        def ada_stage(l):
            add_stage(f"ada{l}", [(cols(a["ada_w"][l], 512 * b, 512), 8, 512, [("ada", 0, b)]) for b in range(12)])

        for l in range(LAYERS):
            if l == 0:
                ada_stage(0)
                w = a["ab_w_in"][0]
                tm = [("tm", 0, t) for t in range(TT_)]
                add_stage("in", [(cols(w, 0, 512), 8, 512, cm_tiles(U_Q, 4)),
                                 (cols(w, 512, 256), 8, 256, [("cm", 0, U_K)] + [("tmk", 1, t) for t in range(TT_)]),
                                 (cols(w, 768, 512), 8, 512, cm_tiles(U_QB, 4)),
                                 (cols(w, 1280, 512), 8, 512, cm_tiles(U_F, 4)),
                                 (cols(w, 1792, 512), 8, 512, cm_tiles(U_F + 4, 4)),
                                 (cols(w, 2304, 512), 8, 512, tm),
                                 (cols(w, 2816, 512), 8, 512, cm_tiles(U_GB, 4))])
                ada_stage(1)
                add_stage("out0", [(cols(a["ab_w_out"][0], 512 * b, 512), 8, 512, cm_tiles(4 * b, 4)) for b in range(2)])
            else:
                bl = []
                for u, n in ((U_R, "rwkv_wr"), (U_RK, "rwkv_wk")):
                    bl += [(cols(a[n][0], 512 * b, 512), 8, 512, cm_tiles(u + 4 * b, 4)) for b in range(2)]
                bl += [(cols(a["rwkv_wv"][0], 512 * b, 512), 8, 512, [("tm", b, t) for t in range(TT_)]) for b in range(2)]
                bl += [("lora_w1", 8, 128, cm_tiles(U_MID, 1)), ("lora_a1", 8, 128, cm_tiles(U_MID + 1, 1)),
                       (cols(a["rwkv_g1"][0], 0, 128), 8, 128, cm_tiles(U_MID + 2, 1))]
                add_stage("proj", bl)
                add_stage("out1", [(cols(a["rwkv_wo"][0], 512 * b, 512), 8, 512, cm_tiles(4 * b, 4)) for b in range(2)])

        first_block, first_tile, tiles_upto, nb, nt = {}, {}, [0], 0, 0
        for name in order:
            first_block[name], first_tile[name] = nb, nt
            for b in stages[name]:
                nb, nt = nb + 1, nt + len(b[3])
                tiles_upto.append(nt)

        def slot(b, kt, n):
            s = RING + (b % 2) * SLOT
            return flat(s, kt * n).rearrange("p (k n) -> p k n", k=kt)

        loads = [0, 0]
        loaded_at = {}

        def load_blocks(sp, name):
            for i, (w, kt, n, _) in enumerate(stages[name]):
                b = first_block[name] + i
                if b >= 2:
                    sp.wait_ge(S("tile_product"), tiles_upto[b - 1])
                dst = slot(b, kt, n)
                if w in ("lora_w1", "lora_a1"):
                    src = a["rwkv_w1" if w == "lora_w1" else "rwkv_a1"][0]
                    parts = [(dst[:, :, 64 * d:64 * d + 64], src[d].rearrange("(k p) n -> p k n", p=P)) for d in range(2)]
                else:
                    parts = [(dst, w)]
                for x, y in parts:
                    sp.dma_start(x, y).then_inc(S(f"ring_loaded{b % 2}"), 16)

        per = [0, 0]
        b = 0
        for name in order:
            for blk in stages[name]:
                per[b % 2] += 2 if isinstance(blk[0], str) else 1
                loaded_at[b] = 16 * per[b % 2]
                b += 1

        def products(pe, name, act, each=None):
            n = first_tile[name]
            for i, (_, kt, cn, tiles) in enumerate(stages[name]):
                b = first_block[name] + i
                pe.wait_ge(S(f"ring_loaded{b % 2}"), loaded_at[b])
                w = slot(b, kt, cn)
                for kind, j, _x in tiles:
                    pb = 2 * (n % 2)
                    if n - first_tile[name] >= 2:
                        pe.wait_ge(S("tile_evacuated"), n - 1)
                    for k in range(kt):
                        if each and (kind, j, _x) == tiles[0]:
                            each(i, k)
                        se = dict(start=k == 0, stop=k == kt - 1)
                        if kind == "cm":
                            lw = w[:, k, 128 * j:128 * j + 128]
                            mm(PS[:, pb, 0:NS], lw, act(i, k)[:, 0:NS], **se)
                            last = mm(PS[:, pb + 1, 0:NP_], lw, act(i, k)[:, NS:T], **se)
                        elif kind == "tm":
                            last = mm(PS[:, pb, 0:cn], act(i, k)[:, 128 * _x:128 * _x + 128], w[:, k, :], **se)
                        else:
                            last = mm(PS[:, pb, 0:128], act(i, k)[:, 128 * _x:128 * _x + 128], w[:, k, 128:256], **se)
                    last.then_inc(S("tile_product"), 1)
                    n += 1

        def tile_list(name):
            n = first_tile[name]
            for i, (_, kt, cn, tiles) in enumerate(stages[name]):
                for t in tiles:
                    yield n, i, t
                    n += 1

        AROW = flat(U_S * T, 1024).rearrange("p (s n) -> p s n", s=2)
        def ada_bank(l, b):
            return 7 if l else 6 + b % 2

        def ada_rows_pe(pe, l, b):
            i = first_block[f"ada{l}"] + b
            pe.wait_ge(S(f"ring_loaded{i % 2}"), loaded_at[i])
            if b >= 2 - l:
                pe.wait_ge(S("ada_cols"), 12 * l + b - 1 + l)
            w = slot(i, 8, 512)
            for k in range(KT):
                st = 32 * (k % 4)
                last = mm(PS[st:st + 32, ada_bank(l, b), :], SCW[:, k, :], w[:, k, :], start=k < 4, stop=k >= 4)
            last.then_inc(S("tile_product"), 1)

        def ada_turn_pe(pe, l, b):
            pe.wait_ge(S("ada_rows"), 12 * l + b + 1)
            for j in range(4):
                ins = mm(PS[:, ada_bank(l, b), 2 * j:2 * j + 2], AROW[:, b % 2, 128 * j:128 * j + 128], con(C_SEL, 2))
            ins.then_inc(S("ada_turned"), 1)

        def ada_act(act, l, b):
            act.wait_ge(S("tile_product"), first_tile[f"ada{l}"] + b + 1)
            if b >= 2:
                act.wait_ge(S("ada_turned"), 12 * l + b - 1)
            A.activation(AROW[:, b % 2, :], PS[:, ada_bank(l, b), :], ACT.Copy).then_inc(S("ada_rows"), 1)

        def ada_cols_act(act, l, b):
            act.wait_ge(S("ada_turned"), 12 * l + b + 1)
            A.activation(ADAS[:, l, 4 * b:4 * b + 4, :].rearrange("p m g -> p (m g)"), PS[:, ada_bank(l, b), 0:8],
                         ACT.Copy).then_inc(S("ada_cols"), 1)

        def ada_pe(pe, l):
            for b in range(12):
                ada_rows_pe(pe, l, b)
                if b:
                    ada_turn_pe(pe, l, b - 1)
            ada_turn_pe(pe, l, 11)

        def ada_dve(dve, step, l):
            ADA = ADAS[:, l, :, :]
            dve.wait_ge(S("ada_cols"), 12 * l + 12)
            bias = PC[:, 0, R_ADAB + 48 * l:R_ADAB + 48 * l + 48]
            for g in range(2):
                step(V.tensor_tensor(ADA[:, :, g], ADA[:, :, g], bias, ALU.add))
            for w, (row, q) in enumerate(((R_N1, 8), (R_N2, 32))):
                for g in range(2):
                    step(V.scalar_tensor_tensor(GAIN[:, 2 * l + w, :, g], ADA[:, q:q + 8, g], 1.0,
                                                PC[:, 0, row + 8 * l:row + 8 * l + 8], ALU.add, ALU.mult))
            V.memset(SML[:, 20:21], 0.0).then_inc(S("tile_evacuated"), 12)

        norms = [0]

        def norm_act(act, step, i, w):
            X = unit(U_X, 8)
            for k in range(KT):
                if k >= 2:
                    act.wait_ge(S("norm_sum"), 8 * i + k - 1)
                A.activation(unit(U_S + k % 2), X[:, k, :], ACT.Square).then_inc(S("norm_square"), 1)
            act.wait_ge(S("norm_sum"), 8 * i + 8)
            r = unit(U_S + 2)
            step(A.activation(r, pair(0), ACT.Ln, bias=EPSC[:, 0:1]))
            A.activation(r, r, ACT.Exp, scale=-0.5).then_inc(S("norm_rms"), 1)
            H = unit(U_H, 8)
            sh = 0 if w == 0 else 24
            for k in range(KT):
                act.wait_ge(S("norm_scaled"), 8 * i + k + 1)
                if w == 1 and k >= 2:
                    act.wait_ge(S("norm_split"), 8 * (i // 2) + k - 1)
                for g, (t0, n) in enumerate(GROUPS):
                    if w == 0:
                        dst = H[:, k, t0:t0 + n]
                    else:
                        dst = NPR[:, k, :] if g else NTMP[:, k % 2, :]
                    ins = A.activation(dst, unit(U_S + 3 + k % 2)[:, t0:t0 + n], ACT.Identity,
                                       scale=GAIN[:, i, k, g:g + 1], bias=ADAS[:, i // 2, sh + k, g:g + 1])
                ins.then_inc(S("norm_out"), 1)

        def norm_pe(pe, i):
            for k in range(KT):
                pe.wait_ge(S("norm_square"), 8 * i + k + 1)
                sq = unit(U_S + k % 2)
                mm(PS[:, 0, 0:NS], con(C_MEAN), sq[:, 0:NS], start=k == 0, stop=k == 7)
                mm(PS[:, 1, 0:NP_], con(C_MEAN), sq[:, NS:T], start=k == 0, stop=k == 7).then_inc(S("norm_sum"), 1)

        def norm_dve(dve, i):
            X = unit(U_X, 8)
            dve.wait_ge(S("norm_rms"), i + 1)
            for k in range(KT):
                if k >= 2:
                    dve.wait_ge(S("norm_out"), 8 * i + k - 1)
                V.tensor_tensor(unit(U_S + 3 + k % 2), X[:, k, :], unit(U_S + 2), ALU.mult).then_inc(S("norm_scaled"), 1)
                if i % 2 and k:
                    norm_split(dve, i, k - 1)
            if i % 2:
                norm_split(dve, i, KT - 1)

        def norm_split(dve, i, k):
            dve.wait_ge(S("norm_out"), 8 * i + k + 1)
            if i == 1 and k == 0:
                for q in range(2):
                    dve.wait_ge(S(f"hgrn_final_out{q}"), 2 * 32)
            split(dve, "norm_high", "norm_split", NTMP[:, k % 2, :], NH[:, k, :], NL[:, k, :])

        NH = in_arena("norm_high", M_NH, [P, KT, NS], F32R)[:, :, :]
        NL = in_arena("norm_low", M_NL, [P, KT, NS], F32R)[:, :, :]
        NPR = flat(M_NP, KT * NP_).rearrange("p (k t) -> p k t", k=KT)
        HH = in_arena("hidden_high", M_HH, [P, HIDT, NS], F32R)[:, :, :]
        HL = in_arena("hidden_low", M_HL, [P, HIDT, NS], F32R)[:, :, :]
        HPR = flat(M_HP, HIDT * NP_).rearrange("p (k t) -> p k t", k=HIDT)
        TMP = in_arena("relu", M_TMP, [P, 2, T])[:, :, :]
        WRAW = in_arena("weights", M_RAW, [P, 3, WB])[:, :, :]
        NTMP = in_arena("norm_whole", M_HH, [P, 2, NS])[:, :, :]
        WHI = in_arena("weights_high", M_WH, [P, 2, WB], F32R)[:, :, :]
        WLO = in_arena("weights_low", M_WL, [P, 2, WB], F32R)[:, :, :]
        BLOCKS = [(half, kind, b) for half in range(2) for kind in ("up", "down") for b in range(8)]
        NBLK = len(BLOCKS)
        tiles_before = [0]
        for _, kind, _b in BLOCKS:
            tiles_before.append(tiles_before[-1] + (2 if kind == "up" else 1))
        NTILE = tiles_before[-1]

        split_n = {}

        def split(dve, high_sem, low_sem, x, high, low):
            split_n[high_sem] = split_n.get(high_sem, 0) + 1
            V.tensor_copy(high, x).then_inc(S(high_sem), 1)
            dve.wait_ge(S(high_sem), split_n[high_sem])
            V.tensor_tensor(low, x, high, ALU.subtract).then_inc(S(low_sem), 1)

        def mlp_sp(sp, l):
            for n, (half, kind, b) in enumerate(BLOCKS):
                g = NBLK * l + n
                if n >= 3:
                    sp.wait_ge(S("mlp_product"), NTILE * l + tiles_before[n - 2])
                if kind == "up":
                    c = 2048 * half + 256 * b
                    src = a["mlp_w1"][l][:, c:c + 256]
                else:
                    src = a["mlp_w2"][l][2048 * half:2048 * half + 2048, 128 * b:128 * b + 128]
                k = KT if kind == "up" else HIDT
                sp.dma_start(WRAW[:, g % 3, :].rearrange("p (k n) -> p k n", k=k), src.rearrange("(k p) n -> p k n", p=P))\
                    .then_inc(S(f"mlp_loaded{g % 3}"), 16)

        def mlp_pe(pe, l):
            for n, (half, kind, b) in enumerate(BLOCKS):
                g, kt = NBLK * l + n, (KT if kind == "up" else HIDT)
                pe.wait_ge(S("mlp_weights_low"), g + 1)
                first = n == 0
                raw, wh, wl = (x.rearrange("p (k n) -> p k n", k=kt) for x in (WRAW[:, g % 3, :], WHI[:, g % 2, :], WLO[:, g % 2, :]))
                xh, xl, xp = (NH, NL, NPR) if kind == "up" else (HH, HL, HPR)
                for j in range(tiles_before[n + 1] - tiles_before[n]):
                    t = tiles_before[n] + j
                    if t >= 2:
                        wait_evacuated(pe, l, t - 2)
                    pb, c = 2 * (t % 2), slice(128 * j, 128 * j + 128)
                    for k in range(kt):
                        if kind == "down" and b == 0:
                            pe.wait_ge(S("hidden_split"), 2 * HIDT * l + HIDT * half + k + 1)
                        if first and j == 0:
                            pe.wait_ge(S("norm_split"), KT * l + k + 1)
                        mm(PS[:, pb, :], wh[:, k, c], xh[:, k, :], start=k == 0, stop=False)
                        mm(PS[:, pb, :], wh[:, k, c], xl[:, k, :], start=False, stop=False)
                        mm(PS[:, pb, :], wl[:, k, c], xh[:, k, :], start=False, stop=k == kt - 1)
                        ins = mm(PS[:, pb + 1, 0:NP_], raw[:, k, c], xp[:, k, :], start=k == 0, stop=k == kt - 1)
                    ins.then_inc(S("mlp_product"), 1)

        def wait_evacuated(pe, l, t):
            n = max(i for i in range(NBLK) if tiles_before[i] <= t)
            half, kind, b = BLOCKS[n]
            if kind == "up":
                pe.wait_ge(S("up_evacuated"), 2 * HIDT * l + HIDT * half + 2 * b + t - tiles_before[n] + 1)
            else:
                pe.wait_ge(S("down_evacuated"), 16 * l + 8 * half + b + 1)

        def mlp_high(act, g, n, l):
            act.wait_ge(S(f"mlp_loaded{g % 3}"), 16 * (g // 3 + 1))
            if n >= 2:
                act.wait_ge(S("mlp_product"), NTILE * l + tiles_before[n - 1])
            A.activation(WHI[:, g % 2, :], WRAW[:, g % 3, :], ACT.Copy).then_inc(S("mlp_weights_high"), 1)

        def mlp_low(dve, g, n, l):
            dve.wait_ge(S("mlp_weights_high"), g + 1)
            V.tensor_tensor(WLO[:, g % 2, :], WRAW[:, g % 3, :], WHI[:, g % 2, :], ALU.subtract)\
                .then_inc(S("mlp_weights_low"), 1)

        def mlp_first_block(dve, l):
            g = NBLK * l
            dve.wait_ge(S(f"mlp_loaded{g % 3}"), 16 * (g // 3 + 1))
            V.tensor_copy(WHI[:, g % 2, :], WRAW[:, g % 3, :]).then_inc(S("mlp_weights_high"), 1)
            mlp_low(dve, g, 0, l)

        def mlp_act(act, l):
            for n, (half, kind, b) in enumerate(BLOCKS):
                if n + 1 < NBLK:
                    mlp_high(act, NBLK * l + n + 1, n + 1, l)
                if kind == "up":
                    for j in range(2):
                        t = tiles_before[n] + j
                        u = 2 * HIDT * l + HIDT * half + 2 * b + j
                        act.wait_ge(S("mlp_product"), NTILE * l + t + 1)
                        if u % (2 * HIDT) >= 2:
                            act.wait_ge(S("hidden_split"), u - 1)
                        A.activation(TMP[:, u % 2, :], pair(2 * (t % 2)), ACT.Relu).then_inc(S("up_evacuated"), 1)

        def mlp_dve(dve, step, l):
            X = unit(U_X, 8)
            for n, (half, kind, b) in enumerate(BLOCKS):
                if n + 1 < NBLK:
                    mlp_low(dve, NBLK * l + n + 1, n + 1, l)
                if kind == "up":
                    for j in range(2):
                        k = 2 * b + j
                        u = 2 * HIDT * l + HIDT * half + k
                        dve.wait_ge(S("up_evacuated"), u + 1)
                        x = TMP[:, u % 2, :]
                        V.tensor_tensor(HPR[:, k, :], x[:, NS:T], x[:, NS:T], ALU.mult)
                        step(V.tensor_tensor(x[:, 0:NS], x[:, 0:NS], x[:, 0:NS], ALU.mult))
                        split(dve, "hidden_high", "hidden_split", x[:, 0:NS], HH[:, k, :], HL[:, k, :])
                else:
                    t = tiles_before[n]
                    dve.wait_ge(S("mlp_product"), NTILE * l + t + 1)
                    for g, (t0, c) in enumerate(GROUPS):
                        x = X[:, b, t0:t0 + c]
                        ins = V.scalar_tensor_tensor(x, PS[:, 2 * (t % 2) + g, 0:c], ADAS[:, l, 40 + b, g:g + 1], x, ALU.mult, ALU.add)
                    ins.then_inc(S("down_evacuated"), 1)
                    if half == 0:
                        dve.wait_ge(S("down_evacuated"), 16 * l + b + 1)

        def residual_dve(dve, name, gate):
            ADA = ADAS[:, int(name[-1]), :, :]
            X = unit(U_X, 8)
            for n, _, (_, j, m) in tile_list(name):
                dve.wait_ge(S("tile_product"), n + 1)
                pb = 2 * (n % 2)
                for g, (t0, c) in enumerate(GROUPS):
                    x = X[:, m, t0:t0 + c]
                    ins = V.scalar_tensor_tensor(x, PS[:, pb + g, 0:c], ADA[:, gate + m, g:g + 1], x, ALU.mult, ALU.add)
                ins.then_inc(S("tile_evacuated"), 1)

        def evac_act(act, name, func, tm_dst):
            for n, i, (kind, j, x) in tile_list(name):
                act.wait_ge(S("tile_product"), n + 1)
                pb = 2 * (n % 2)
                if kind == "cm":
                    ins = A.activation(unit(x), pair(pb), func(x))
                else:
                    dst, c = tm_dst(kind, j, x)
                    ins = A.activation(dst, PS[:, pb, 0:c], ACT.Copy)
                ins.then_inc(S("tile_evacuated"), 1)

        VA = unit(U_VA).rearrange("p (t c) -> p t c", t=TT_)
        COS = flat((U_S + 4) * T, NS)
        SIN = flat((U_S + 4) * T + NS, NS)
        KD = flat((U_S + 6) * T, 2 * 768).rearrange("p (k t) -> p k t", k=2)
        CK = flat((U_S + 9) * T, 256).rearrange("p (a c) -> p a c", a=2)
        KOUT = flat((U_S + 9) * T + 256, 128)
        PR = unit(U_S + 10, 2)
        PT = unit(U_S + 12, 2)

        def attn_prep_act(act, step):
            for t in range(5):
                u = unit(U_Q + t)
                if t >= 2:
                    act.wait_ge(S("qk_sum"), t - 1)
                A.activation(unit(U_S + t % 2), u, ACT.Square).then_inc(S("qk_square"), 1)
                act.wait_ge(S("qk_sum"), t + 1)
                r = unit(U_S + 2 + t % 2)
                if t >= 2:
                    act.wait_ge(S("qk_normed"), t - 1)
                step(A.activation(r, pair(2 * (t % 2)), ACT.Ln, bias=EPSC[:, 0:1]))
                A.activation(r, r, ACT.Exp, scale=-0.5).then_inc(S("qk_rms"), 1)
            act.wait_ge(S("key_out_psum"), 1)
            A.activation(KOUT, PS[:, 6, 0:128], ACT.Copy).then_inc(S("key_out"), 1)
            act.wait_ge(S("qk_roped"), 5)
            act.wait_ge(S("cache_key"), 1)
            K = unit(U_K)
            for kv in range(2):
                r0 = 64 * kv
                for half in range(2):
                    h = slice(64 * half, 64 * half + 64)
                    A.activation(KD[h, kv, 0:NS], K[r0:r0 + 64, 0:NS], ACT.Copy)
                    A.activation(KD[h, kv, NS:T], PS[r0:r0 + 64, 7, 0:128], ACT.Copy)
                    A.activation(KD[h, kv, T:768], K[r0:r0 + 64, NS:T], ACT.Copy)

        def attn_prep_pe(pe):
            for t in range(5):
                pe.wait_ge(S("qk_square"), t + 1)
                if t >= 2:
                    pe.wait_ge(S("qk_rms"), t - 1)
                sq, b = unit(U_S + t % 2), 2 * (t % 2)
                mm(PS[:, b, 0:NS], bd64, sq[:, 0:NS])
                mm(PS[:, b + 1, 0:NP_], bd64, sq[:, NS:T]).then_inc(S("qk_sum"), 1)
                if t >= 1:
                    rope_pe(pe, t - 1)
            rope_pe(pe, 4)
            nc.tensor.transpose(PS[:, 6, 0:128], unit(U_K)[:, NS:T], ident).then_inc(S("key_out_psum"), 1)
            pe.wait_ge(S("cache_loaded"), 32)
            nc.tensor.transpose(PS[:, 7, 0:128], CK[:, 0, :], ident).then_inc(S("cache_key"), 1)

        def rope_pe(pe, t):
            pe.wait_ge(S("qk_normed"), t + 1)
            if t >= 2:
                pe.wait_ge(S("qk_roped"), t - 1)
            mm(PS[:, 4 + t % 2, 0:NS], con(C_ROPE), unit(U_Q + t)[:, 0:NS]).then_inc(S("qk_swapped"), 1)

        def attn_prep_dve(dve, step):
            dve.wait_ge(S("rope_loaded"), 16)
            for t in range(5):
                u = unit(U_Q + t)
                col = PC[:, 2, R_QN:R_QN + 1] if t < 4 else PC[:, 2, R_KN:R_KN + 1]
                dve.wait_ge(S("qk_rms"), t + 1)
                V.scalar_tensor_tensor(u, u, col, unit(U_S + 2 + t % 2), ALU.mult, ALU.mult).then_inc(S("qk_normed"), 1)
                dve.wait_ge(S("qk_swapped"), t + 1)
                tmp = unit(U_S + 14)[:, 0:NS]
                step(V.tensor_tensor(tmp, PS[:, 4 + t % 2, 0:NS], SIN, ALU.mult))
                step(V.tensor_tensor(u[:, 0:NS], u[:, 0:NS], COS, ALU.mult))
                V.tensor_tensor(u[:, 0:NS], u[:, 0:NS], tmp, ALU.add).then_inc(S("qk_roped"), 1)
                dve.wait_ge(S("qk_roped"), t + 1)

        ATT = [(h, t) for h in range(8) for t in range(TT_)]
        NA = len(ATT)

        def keys_of(t):
            return T if t < 4 else 128

        def att_scores(n):
            h, t = ATT[n]
            r = slice(64 * (h % 2), 64 * (h % 2) + 64)
            q = unit(U_Q + h // 2)[r, 128 * t:128 * t + 128]
            kd = KD[r, h // 4, :]
            b = 2 * (n % 2)
            if t < 4:
                mm(PS[:, b, 0:NS], q, kd[:, 0:NS])
                return mm(PS[:, b + 1, 0:128], q, kd[:, NS:T])
            return mm(PS[:, b, 0:128], q, kd[:, T:768])

        def attn_pe(pe):
            def scores(n):
                if n >= 2:
                    pe.wait_ge(S("att_exp"), n - 1)
                att_scores(n).then_inc(S("att_scores"), 1)

            def turn(n):
                pe.wait_ge(S("att_probs"), n + 1)
                if n >= 1:
                    pe.wait_ge(S("att_pt"), n)
                for j in range(keys_of(ATT[n][1]) // 128):
                    ins = nc.tensor.transpose(pair(4)[:, 128 * j:128 * j + 128], PR[:, n % 2, 128 * j:128 * j + 128], ident)
                ins.then_inc(S("att_turned"), 1)

            def values(n):
                h, t = ATT[n]
                kt = keys_of(t) // 128
                pe.wait_ge(S("att_pt"), n + 1)
                if n:
                    pe.wait_ge(S("att_out"), n)
                r = slice(64 * (h % 2), 64 * (h % 2) + 64)
                vc = slice(64 * (h // 4), 64 * (h // 4) + 64)
                for j in range(kt):
                    v = VA[:, 4, vc] if t == 4 else (VA[:, j, vc] if j < 4 else CK[:, 1, vc])
                    ins = mm(att_out(n)[r, :], v, PT[:, n % 2, 128 * j:128 * j + 128], start=j == 0, stop=j == kt - 1)
                ins.then_inc(S("att_values"), 1)

            scores(0)
            for n in range(NA):
                if n + 1 < NA:
                    scores(n + 1)
                if n % 3 == 1 and n // 3 < 12:
                    ada_rows_pe(pe, 1, n // 3)
                turn(n)
                if n % 3 == 2 and n // 3 < 12:
                    ada_turn_pe(pe, 1, n // 3)
                if n:
                    values(n - 1)
            values(NA - 1)

        def att_out(n):
            return PS[:, 6, 0:128]

        def attn_dve(dve, step):
            def row_max(n):
                k = keys_of(ATT[n][1])
                dve.wait_ge(S("att_scores"), n + 1)
                if n >= 2:
                    dve.wait_ge(S("att_exp"), n - 1)
                st = SML[:, 4 * (n % 2):4 * (n % 2) + 4]
                step(V.tensor_reduce(st[:, 0:1], pair(2 * (n % 2), k), AXX, ALU.max))
                V.tensor_scalar(st[:, 1:2], st[:, 0:1], -ATTN_SCALE, None, ALU.mult).then_inc(S("att_max"), 1)

            row_max(0)
            for n in range(NA):
                k = keys_of(ATT[n][1])
                st = SML[:, 4 * (n % 2):4 * (n % 2) + 4]
                dve.wait_ge(S("att_exp"), n + 1)
                step(V.reciprocal(st[:, 3:4], st[:, 2:3]))
                V.tensor_scalar(PR[:, n % 2, 0:k], PR[:, n % 2, 0:k], st[:, 3:4], None, ALU.mult).then_inc(S("att_probs"), 1)
                if n + 1 < NA:
                    row_max(n + 1)
                dve.wait_ge(S("att_turned"), n + 1)
                if n >= 2:
                    dve.wait_ge(S("att_values"), n - 1)
                V.tensor_copy(PT[:, n % 2, 0:k], pair(4, k)).then_inc(S("att_pt"), 1)
            ada_dve(dve, step, 1)

        def attn_act(act):
            def head_out(n):
                h, t = ATT[n]
                r = slice(64 * (h % 2), 64 * (h % 2) + 64)
                act.wait_ge(S("att_values"), n + 1)
                A.activation(unit(U_MIX + h // 2)[r, 128 * t:128 * t + 128], att_out(n)[r, :],
                             ACT.Copy).then_inc(S("att_out"), 1)

            def exps(n):
                k = keys_of(ATT[n][1])
                st = SML[:, 4 * (n % 2):4 * (n % 2) + 4]
                act.wait_ge(S("att_max"), n + 1)
                if n >= 2:
                    act.wait_ge(S("att_turned"), n - 1)
                A.activation(PR[:, n % 2, 0:k], pair(2 * (n % 2), k), ACT.Exp, scale=ATTN_SCALE, bias=st[:, 1:2],
                             accum_out=st[:, 2:3]).then_inc(S("att_exp"), 1)

            exps(0)
            for n in range(NA):
                if n + 1 < NA:
                    exps(n + 1)
                if n % 3 == 1 and n // 3 < 12:
                    ada_act(act, 1, n // 3)
                if n % 3 == 2 and n // 3 < 12:
                    ada_cols_act(act, 1, n // 3)
                if n:
                    head_out(n - 1)
            head_out(NA - 1)

        VB = unit(U_VB, 4).rearrange("p u t -> p (u t)").rearrange("p (t c) -> p t c", t=TT_)
        EB, OD, HT, ON = unit(U_S, 2), unit(U_S + 6, 2), unit(U_S + 8, 2), unit(U_S + 10, 2)
        QDS = [unit(U_S + 2, 2), unit(U_S + 4, 2)]
        h0 = U_H * T
        HGM = flat(h0, 1024).rearrange("p (s d h c) -> p s d h c", s=2, d=2, h=2)
        HKT = flat(h0 + 1024, 512).rearrange("p (s d c) -> p s d c", s=2, d=2)
        HS = flat(h0 + 1536, 2 * 2 * 11 * 64).rearrange("p (s d x v) -> p s d x v", s=2, d=2, x=11)
        HS2 = flat(h0 + 1536 + 2816, 128).rearrange("p (d v) -> p d v", d=2)
        HDEC = flat(h0 + 1536 + 2944, 40).rearrange("p (s d c) -> p s d c", s=2, d=2)
        NH_ = 20

        def tile_of(i, d):
            return 4 if i == 4 else (i if d == 0 else 3 - i)

        def h_key(p, d):
            return unit(U_F + 4 * d + p)

        def hgrn_pe(pe):
            def scores(m):
                p, i = divmod(m, 5)
                pe.wait_ge(S("hgrn_staged"), p + 1)
                if m:
                    pe.wait_ge(S("hgrn_masked"), m)
                for d in range(2):
                    t = tile_of(i, d)
                    for h in range(2):
                        r = slice(64 * h, 64 * h + 64)
                        ins = mm(PS[:, h, 128 * d:128 * d + 128], h_key(p, d)[r, 128 * t:128 * t + 128],
                                 QDS[p % 2][r, d, 128 * t:128 * t + 128])
                ins.then_inc(S("hgrn_scores"), 1)
                if m:
                    pe.wait_ge(S("hgrn_key_rows"), m)
                for d in range(2):
                    t = tile_of(i, d)
                    ins = nc.tensor.transpose(PS[:, 2, 128 * d:128 * d + 128], h_key(p, d)[:, 128 * t:128 * t + 128], ident)
                ins.then_inc(S("hgrn_turned"), 1)

            def increments(m):
                p, i = divmod(m, 5)
                pe.wait_ge(S("hgrn_key_rows"), m + 1)
                if m:
                    pe.wait_ge(S("hgrn_state"), m)
                if i == 2 and p:
                    pe.wait_ge(S("hgrn_o_rms"), p)
                for d in range(2):
                    t = tile_of(i, d)
                    for x in range(2):
                        c = x if d == 0 else 1 - x
                        cr = slice(64 * c, 64 * c + 64)
                        for h in range(2):
                            r = slice(64 * h, 64 * h + 64)
                            ins = mm(PS[r, 5 + c, 128 * d + 64 * x:128 * d + 64 * x + 64], HKT[cr, m % 2, d, 64 * h:64 * h + 64],
                                     VB[cr, t, 128 * p + 64 * h:128 * p + 64 * h + 64])
                ins.then_inc(S("hgrn_ds"), 1)

            def outputs(m):
                p, i = divmod(m, 5)
                pe.wait_ge(S("hgrn_masked"), m + 1)
                pe.wait_ge(S("hgrn_state"), m + 1)
                pe.wait_ge(S(f"hgrn_state_load{p % 2}"), 32 * (p // 2 + 1))
                if m:
                    pe.wait_ge(S("hgrn_out_a"), 2 * m)
                    pe.wait_ge(S("hgrn_out_b"), 2 * m)
                for d in range(2):
                    t = tile_of(i, d)
                    for h in range(2):
                        r = slice(64 * h, 64 * h + 64)
                        mm(PS[r, 3 + h, 128 * d:128 * d + 128], VB[:, t, 128 * p + 64 * h:128 * p + 64 * h + 64],
                           HGM[:, m % 2, d, h, :], start=True, stop=False)
                    for x in range(2):
                        c = x if d == 0 else 1 - x
                        for h in range(2):
                            r = slice(64 * h, 64 * h + 64)
                            ins = mm(PS[r, 3 + h, 128 * d + 64 * c:128 * d + 64 * c + 64], HS[r, p % 2, d, 2 * i + x, :],
                                     QDS[p % 2][r, d, 128 * t + 64 * c:128 * t + 64 * c + 64], start=False, stop=x == 1)
                ins.then_inc(S("hgrn_out_psum"), 1)

            def norm(p):
                pe.wait_ge(S("hgrn_o_square"), p + 1)
                pe.wait_ge(S("hgrn_state"), min(5 * p + 7, NH_))
                mm(PS[:, 6, 0:NS], bd64, ON[:, 1, 0:NS])
                mm(PS[:, 7, 0:NP_], bd64, ON[:, 1, NS:T]).then_inc(S("hgrn_o_sum"), 1)

            scores(0)
            increments(0)
            for m in range(NH_):
                if m + 1 < NH_:
                    scores(m + 1)
                outputs(m)
                if m + 1 < NH_:
                    increments(m + 1)
                if m % 5 == 0 and m:
                    norm(m // 5 - 1)
            norm(3)

        def hgrn_dve(dve, step):
            lb, oml = LB[:, 4, :], LB[:, 5, :]

            def gates(p):
                q, g = unit(U_QB + p), unit(U_GB + p)
                dve.wait_ge(S("hgrn_sig"), 2 * p + 2)
                V.tensor_tensor(q, q, HT[:, 0, :], ALU.mult)
                step(V.tensor_tensor(g, g, HT[:, 1, :], ALU.mult))
                for d in range(2):
                    f = h_key(p, d)
                    V.tensor_scalar(f, f, oml[:, p:p + 1], lb[:, p:p + 1], ALU.mult, ALU.add).then_inc(S("hgrn_f"), 1)

            def cumulate(p):
                for d in range(2):
                    f = h_key(p, d)
                    dve.wait_ge(S("hgrn_log"), 2 * p + d + 1)
                    if p and d == 0:
                        dve.wait_ge(S("hgrn_staged"), p)
                    m = CON[:, C_SCAN:C_SCAN + T] if d == 0 else CON[:, C_SCAN + T:C_SCAN:-1]
                    x = HT[:, d, :] if d == 0 else HT[:, d, ::-1]
                    V.tensor_tensor_scan(EB[:, d, :] if d == 0 else EB[:, d, ::-1], m, x, 0.0,
                                         ALU.mult, ALU.add).then_inc(S("hgrn_cum"), 1)
                    step(V.tensor_scalar(f, f, -1.0, 1.0, ALU.mult, ALU.add))

            def scale(p):
                q = unit(U_QB + p)
                if p >= 2:
                    dve.wait_ge(S("hgrn_out_psum"), 5 * (p - 1))
                for d in range(2):
                    dve.wait_ge(S("hgrn_decay"), 2 * p + d + 1)
                    V.tensor_copy(HDEC[:, p % 2, d, :], EB[:, d, (63 if d == 0 else 0)::64])
                    V.tensor_tensor(QDS[p % 2][:, d, :], q, EB[:, d, :], ALU.mult)
                    ins = V.tensor_tensor(h_key(p, d), h_key(p, d), HT[:, d, :], ALU.mult)
                ins.then_inc(S("hgrn_staged"), 1)
                dve.wait_ge(S("hgrn_staged"), p + 1)

            def mask(m):
                dve.wait_ge(S("hgrn_scores"), m + 1)
                if m >= 2:
                    dve.wait_ge(S("hgrn_out_psum"), m - 1)
                for d in range(2):
                    ins = V.tensor_tensor(HGM[:, m % 2, d, :, :], PS[:, 0:2, 128 * d:128 * d + 128],
                                          con(C_HGRN + 128 * d).unsqueeze(1).broadcast_to([P, 2, 128]), ALU.mult)
                ins.then_inc(S("hgrn_masked"), 1)

            def states(m):
                p, i = divmod(m, 5)
                dve.wait_ge(S(f"hgrn_state_load{p % 2}"), 32 * (p // 2 + 1))
                dve.wait_ge(S("hgrn_state_init"), 4)
                if i == 4 and p >= 2:
                    dve.wait_ge(S(f"hgrn_final_out{p % 2}"), 32 * (p // 2))
                if m:
                    dve.wait_ge(S("hgrn_state"), m)
                dve.wait_ge(S("hgrn_ds"), m + 1)
                for x in range(2):
                    if 2 * i + x == 7:
                        continue
                    for d in range(2):
                        c = 2 * tile_of(i, d) + (x if d == 0 else 1 - x)
                        ins = V.tensor_scalar(HS2[:, d, :], HS[:, p % 2, d, 2 * i + x, :], HDEC[:, p % 2, d, c:c + 1], None, ALU.mult)
                    step(ins)
                    for d in range(2):
                        c = 2 * tile_of(i, d) + (x if d == 0 else 1 - x)
                        ins = V.scalar_tensor_tensor(HS[:, p % 2, d, 2 * i + x + 1, :], PS[:, 5 + c % 2, 128 * d + 64 * x:128 * d + 64 * x + 64],
                                                     HDEC[:, p % 2, d, c:c + 1], HS2[:, d, :], ALU.mult, ALU.add)
                    step(ins)
                V.memset(SML[:, 21:22], 0.0).then_inc(S("hgrn_state"), 1)

            def out_b(m):
                p, i = divmod(m, 5)
                dve.wait_ge(S("hgrn_out_psum"), m + 1)
                for d in range(2):
                    t = tile_of(i, d)
                    V.tensor_copy(OD[64:128, d, 128 * t:128 * t + 128], PS[64:128, 4, 128 * d:128 * d + 128]).then_inc(S("hgrn_out_b"), 1)

            def add_up(p):
                dve.wait_ge(S("hgrn_out_a"), 2 * 5 * (p + 1))
                dve.wait_ge(S("hgrn_out_b"), 2 * 5 * (p + 1))
                V.tensor_tensor(ON[:, 0, :], OD[:, 0, :], OD[:, 1, :], ALU.add).then_inc(S("hgrn_o"), 1)
                dve.wait_ge(S("hgrn_o"), p + 1)

            def norm_gate(p):
                dve.wait_ge(S("hgrn_o_rms"), p + 1)
                step(V.scalar_tensor_tensor(ON[:, 0, :], ON[:, 0, :], PC[:, 2, R_GN:R_GN + 1], ON[:, 1, :], ALU.mult, ALU.mult))
                V.tensor_tensor(unit(U_MIX + 4 + p), ON[:, 0, :], unit(U_GB + p), ALU.mult).then_inc(S("hgrn_pair_done"), 1)
                dve.wait_ge(S("hgrn_pair_done"), p + 1)

            gates(0)
            cumulate(0)
            scale(0)
            mask(0)
            states(0)
            for m in range(NH_):
                p, i = divmod(m, 5)
                if i == 0 and p:
                    add_up(p - 1)
                if m + 1 < NH_:
                    mask(m + 1)
                out_b(m)
                if m + 1 < NH_:
                    states(m + 1)
                if i == 1 and p < 3:
                    gates(p + 1)
                if i == 2:
                    if p:
                        norm_gate(p - 1)
                    if p < 3:
                        cumulate(p + 1)
                if i == 3 and p < 3:
                    scale(p + 1)
            add_up(3)
            norm_gate(3)

        def hgrn_act(act, step):
            act.wait_ge(S("kv_stored"), 32)

            def sigmoids(p):
                if p:
                    act.wait_ge(S("hgrn_staged"), p)
                A.activation(HT[:, 0, :], unit(U_QB + p), ACT.Sigmoid).then_inc(S("hgrn_sig"), 1)
                A.activation(HT[:, 1, :], unit(U_GB + p), ACT.Sigmoid).then_inc(S("hgrn_sig"), 1)

            def logs(p):
                for d in range(2):
                    act.wait_ge(S("hgrn_f"), 2 * p + d + 1)
                    A.activation(HT[:, d, :], h_key(p, d), ACT.Ln).then_inc(S("hgrn_log"), 1)

            def decays(p):
                for d in range(2):
                    act.wait_ge(S("hgrn_cum"), 2 * p + d + 1)
                    A.activation(HT[:, d, :], EB[:, d, :], ACT.Exp, scale=-1.0)
                    A.activation(EB[:, d, :], EB[:, d, :], ACT.Exp).then_inc(S("hgrn_decay"), 1)

            def key_rows(m):
                act.wait_ge(S("hgrn_turned"), m + 1)
                if m >= 2:
                    act.wait_ge(S("hgrn_ds"), m - 1)
                A.activation(HKT[:, m % 2, :, :].rearrange("p d c -> p (d c)"), PS[:, 2, 0:256], ACT.Copy).then_inc(S("hgrn_key_rows"), 1)

            def out_a(m):
                p, i = divmod(m, 5)
                act.wait_ge(S("hgrn_out_psum"), m + 1)
                for d in range(2):
                    t = tile_of(i, d)
                    A.activation(OD[0:64, d, 128 * t:128 * t + 128], PS[0:64, 3, 128 * d:128 * d + 128], ACT.Copy).then_inc(S("hgrn_out_a"), 1)

            def square(p):
                act.wait_ge(S("hgrn_o"), p + 1)
                A.activation(ON[:, 1, :], ON[:, 0, :], ACT.Square).then_inc(S("hgrn_o_square"), 1)

            def rms(p):
                act.wait_ge(S("hgrn_o_sum"), p + 1)
                step(A.activation(ON[:, 1, :], pair(6), ACT.Ln, bias=EPSC[:, 0:1]))
                A.activation(ON[:, 1, :], ON[:, 1, :], ACT.Exp, scale=-0.5).then_inc(S("hgrn_o_rms"), 1)

            sigmoids(0)
            logs(0)
            decays(0)
            key_rows(0)
            for m in range(NH_):
                p, i = divmod(m, 5)
                if m + 1 < NH_:
                    key_rows(m + 1)
                if i == 0 and p:
                    square(p - 1)
                if i == 1 and p:
                    rms(p - 1)
                out_a(m)
                if i == 0 and p < 3:
                    sigmoids(p + 1)
                if i == 1 and p < 3:
                    logs(p + 1)
                if i == 2 and p < 3:
                    decays(p + 1)
            square(3)
            rms(3)

        def hgrn_pool(pool):
            for q in range(2):
                for d in range(2):
                    G.memset(HS[:, q, d, 8, :], 0.0).then_inc(S("hgrn_state_init"), 1)

        def hgrn_sp(sp):
            def load(p):
                if p >= 2:
                    sp.wait_ge(S("hgrn_out_psum"), 5 * (p - 1))
                for d, n in enumerate(("state_hgrn_fwd", "state_hgrn_bwd")):
                    sp.dma_start(HS[:, p % 2, d, 0, :], a[n][0, 0, 2 * p:2 * p + 2].rearrange("h k v -> (h k) v"))\
                        .then_inc(S(f"hgrn_state_load{p % 2}"), 16)

            load(0)
            load(1)
            load_blocks(sp, "out0")
            for p in range(4):
                sp.wait_ge(S("hgrn_state"), 5 * (p + 1))
                for d in range(2):
                    sp.dma_start(o["hgrn"][d][0, 0, 2 * p:2 * p + 2].rearrange("h k v -> (h k) v"), HS[:, p % 2, d, 10, :])\
                        .then_inc(S(f"hgrn_final_out{p % 2}"), 16)
                if p < 2:
                    load(p + 2)

        spans = [[U_H * T, (U_H + 8) * T], [(U_MID + 3) * T, ARENA]]

        def take(n):
            for span in spans:
                if span[1] - span[0] >= n:
                    span[0] += n
                    return flat(span[0] - n, n)
            raise AssertionError("the arena is full")

        def sq4():
            return take(512).rearrange("p (u x) -> p u x", u=4)

        XI = [unit(U_XI, 8), unit(U_XI + 8, 8)]
        NSLOT = NCH
        ARD = [take(NSLOT * 128).rearrange("p (c x) -> p c x", c=NSLOT) for _ in range(2)]
        BKD = [take(NSLOT * 128).rearrange("p (c x) -> p c x", c=NSLOT) for _ in range(2)]
        SV = [take(2 * 11 * 64).rearrange("p (h c v) -> p h c v", h=2, c=11) for _ in range(2)]
        UV = [take(2 * 10 * 64).rearrange("p (h c v) -> p h c v", h=2, c=10) for _ in range(2)]
        YD = [take(T) for _ in range(2)]
        BN = take(T)
        SW = [take(T) for _ in range(2)]
        BC = [take(T) for _ in range(2)]
        AD = [take(T) for _ in range(2)]
        KKN, SQ, RT = take(T), take(T), take(T)
        YS, YC = BC
        STL = take(128).rearrange("p (d k) -> p d k", d=2)
        STO = take(128).rearrange("p (d k) -> p d k", d=2)
        LW = take(256).rearrange("p (w c) -> p w c", w=2)
        G2 = take(256).rearrange("p (s c) -> p s c", s=2)
        XS = take(128).rearrange("p (d v) -> p d v", d=2)
        S2 = take(128).rearrange("p (d v) -> p d v", d=2)
        PE_ = take(40).rearrange("p (s d c) -> p s d c", s=2, d=2)
        Qm, Qd, QdT, Q2, QT2, P1, P2 = (sq4() for _ in range(7))
        TTs, BTs = [sq4(), sq4()], [sq4(), sq4()]
        Ls = [take(512).rearrange("p (h u x) -> p h u x", h=2, u=4) for _ in range(2)]
        Rs = [take(512).rearrange("p (h u x) -> p h u x", h=2, u=4) for _ in range(2)]

        R, K = unit(U_R, 8), unit(U_RK, 8)
        RV = unit(U_RV, 8).rearrange("p u t -> p (u t)").rearrange("p (t c) -> p t c", t=TT_)
        MID = unit(U_MID, 3)

        MIXES = [(0, 0, 2), (2, 2, 4), (3, 4, 6), (1, 6, 7), (4, 7, 8), (5, 8, 9)]

        def stage_of_block(i):
            return next(s for s, (_, b0, b1) in enumerate(MIXES) if b0 <= i < b1)

        def proj_tiles_upto(s):
            return first_tile["proj"] + sum(len(b[3]) for b in stages["proj"][:MIXES[s][2]])

        def proj_dve(dve, step):
            H = unit(U_H, 8)
            for s, (mrow, _, _) in enumerate(MIXES):
                xi = XI[s % 2]
                if s >= 2:
                    dve.wait_ge(S("tile_product"), proj_tiles_upto(s - 2))
                mix = PC[:, 1, R_MIX + 8 * mrow:R_MIX + 8 * mrow + 8]
                omm = SML[:, 8:16]
                step(V.tensor_scalar(omm, mix, -1.0, 1.0, ALU.mult, ALU.add))
                for k in range(KT):
                    if s == 0:
                        dve.wait_ge(S("norm_out"), 2 * KT + k + 1)
                    step(V.tensor_scalar(xi[:, k, :], H[:, k, :], omm[:, k:k + 1], None, ALU.mult))
                    for g, (t0, n) in enumerate(GROUPS):
                        dst, src = (t0 + 1, t0) if k < 4 else (t0, t0 + 1)
                        ins = V.scalar_tensor_tensor(xi[:, k, dst:dst + n - 1], H[:, k, src:src + n - 1], mix[:, k:k + 1],
                                                     xi[:, k, dst:dst + n - 1], ALU.mult, ALU.add)
                        ins.then_inc(S("mixed_input"), 1) if g else step(ins)
                dve.wait_ge(S("mixed_input"), KT * (s + 1))

        NB = 40
        UNITS = [(d, h) for d in range(2) for h in range(2)]
        PR_ = {k: i + 1 for i, k in enumerate(("QT", "Q2", "QT2", "Q4", "QT4", "P2", "QT8", "P3", "D", "DT", "NT", "H1", "H2", "H3"))}
        VE_ = {k: i + 1 for i, k in enumerate(("QA", "QB", "Qd", "Qo", "QT2", "QT4", "P2", "P3", "D", "H1", "H2", "H3"))}
        SC_ = {k: i + 1 for i, k in enumerate(("QT", "Q2", "Q4", "QT8", "DT", "NT"))}
        PO_ = {k: i + 1 for i, k in enumerate(("P1", "IQ"))}

        def chunk(i, d, h):
            return 2 * tile_of(i, d) + h

        ORDER = ("gram", "m0", "item0", "a", "item1", "m1", "b", "item2", "m2", "c", "item3", "x0", "d", "m3", "u0",
                 "e", "s0", "m4", "f", "x1", "g", "u1", "h", "i", "s1")

        def run_iteration(n, inverse, walk, side, more={}):
            p, i = n // 5, n % 5
            items = aside(n) if n >= 0 else []
            for what in ORDER:
                if what in inverse:
                    if n + 1 < NB:
                        inverse[what](n + 1)
                elif what[0] == "m":
                    if n >= 0:
                        for f in more.get((i, what), ()):
                            f(p)
                elif what[:4] == "item":
                    if int(what[4]) < len(items) and items[int(what[4])]:
                        side(items[int(what[4])])
                elif n >= 0 and what[0] in walk:
                    walk[what[0]](n, int(what[1]))

        def steps_of(n, s):
            return [chunk(n % 5, 0, s), chunk(n % 5, 1, 1 - s)], [s, 3 - s]

        def aside(n):
            p, i = n // 5, n % 5
            last, this, nxt = p - 1, p, p + 1
            r = [[("final", last), None, ("mean", last), ("var", last)],
                 [("w0", nxt), ("gate", last), ("w1", nxt), ("k_sum", nxt)],
                 [("bonus", this), ("values", this), ("a0", nxt), ("a1", nxt)],
                 [("state", nxt)],
                 []][i]
            return [x if x and 0 <= x[1] < 8 else None for x in r]

        FIRST_ASIDE = [(x, 0) for x in ("w0", "w1", "a0", "a1", "k_sum", "state")]
        LAST_ASIDE = [(x, 7) for x in ("final", "mean", "var", "gate")]

        def evacuated(eng, item):
            kind, q = item
            sem, val = {"y": ("rwkv_y", 4 * q + 4), "final": ("rwkv_final", 2 * q + 2), "mean": ("rwkv_centred", q + 1),
                        "var": ("rwkv_y_rs", q + 1), "gate": ("rwkv_pair_done", q + 1), "w0": ("rwkv_sig", 4 * q + 1),
                        "w1": ("rwkv_sig", 4 * q + 2), "a0": ("rwkv_sig", 4 * q + 3), "a1": ("rwkv_sig", 4 * q + 4),
                        "bonus": ("rwkv_bonus", q + 1), "values": ("rwkv_bonus_v", q + 1),
                        "k_sum": ("rwkv_k_max", q + 1), "state": ("rwkv_state_in", 4 * q + 4)}[kind]
            eng.wait_ge(S(sem), val)

        def rwkv_pe(pe):
            before = [None]

            def wide(lhsT, rhs):
                mm(PS[:, 6, 0:NS], lhsT, rhs[:, 0:NS])
                return mm(PS[:, 7, 0:NP_], lhsT, rhs[:, NS:T])

            def side(item):
                kind, q = item
                if before[0]:
                    evacuated(pe, before[0])
                before[0] = item
                if kind in ("w0", "w1", "a0", "a1"):
                    w, d = "wa".index(kind[0]), int(kind[1])
                    pe.wait_ge(S("rwkv_weights"), 64 * (q + 1))
                    r = slice(64 * d, 64 * d + 64)
                    wide(LW[r, w, :], MID[r, w, :]).then_inc(S("rwkv_lora"), 1)
                elif kind == "k_sum":
                    pe.wait_ge(S("rwkv_k_square"), q + 1)
                    wide(bd64, SQ).then_inc(S("rwkv_k_sum"), 1)
                elif kind == "state":
                    for d in range(2):
                        for h in range(2):
                            r = slice(64 * h, 64 * h + 64)
                            ins = mm(PS[r, 6 + h, 64 * d:64 * d + 64], STL[r, d, :], CON[r, 64 * h:64 * h + 64])
                    ins.then_inc(S("rwkv_state_psum"), 1)
                elif kind == "final":
                    pe.wait_ge(S("rwkv_state"), 2 * (5 * q + 5))
                    for d in range(2):
                        for h in range(2):
                            r = slice(64 * h, 64 * h + 64)
                            ins = mm(PS[r, 6 + h, 64 * d:64 * d + 64], SV[d][r, h, 10, :], CON[r, 64 * h:64 * h + 64])
                    ins.then_inc(S("rwkv_final_psum"), 1)
                elif kind == "mean":
                    pe.wait_ge(S("rwkv_ysum"), q + 1)
                    wide(bd64, YS).then_inc(S("rwkv_mean"), 1)
                elif kind == "var":
                    pe.wait_ge(S("rwkv_yc_square"), q + 1)
                    wide(bd64, SQ).then_inc(S("rwkv_var"), 1)
                elif kind == "gate":
                    pe.wait_ge(S("rwkv_gate_weights"), 16 * (q + 1))
                    wide(G2[:, q % 2, :], MID[:, 2, :]).then_inc(S("rwkv_gate"), 1)
                elif kind == "bonus":
                    pe.wait_ge(S("rwkv_bonus_raw"), q + 1)
                    wide(bd64, BN).then_inc(S("rwkv_bonus_psum"), 1)
                elif kind == "values":
                    for t in range(TT_):
                        ins = nc.tensor.transpose(pair(6)[:, 128 * t:128 * t + 128], RV[:, t, 128 * q:128 * q + 128], ident)
                    ins.then_inc(S("rwkv_values_psum"), 1)

            def gram(n):
                pe.wait_ge(S("rwkv_staged"), n + 1)
                if n:
                    pe.wait_ge(S("inverse_vector"), 12 * n)
                for h in range(2):
                    r = slice(64 * h, 64 * h + 64)
                    for u, (d, hh) in enumerate(UNITS):
                        c = chunk(n % 5, d, hh)
                        ins = mm(PS[:, h, 128 * u:128 * u + 128], BKD[d][r, c, :], ARD[d][r, c, :])
                ins.then_inc(S("rwkv_gram"), 1)
                for u, (d, hh) in enumerate(UNITS):
                    ins = nc.tensor.transpose(PS[:, 2, 128 * u:128 * u + 128], BKD[d][:, chunk(n % 5, d, hh), :], ident)
                ins.then_inc(S("rwkv_bk_turned"), 1)

            def prod(name, bank, lhsT, rhs):
                for u in range(4):
                    ins = mm(PS[:, bank, 128 * u:128 * u + 128], lhsT[:, u, :], rhs[:, u, :])
                ins.then_inc(S("inverse_products"), 1)

            def need(n, ve=None, sc=None, po=None):
                if ve:
                    pe.wait_ge(S("inverse_vector"), 12 * n + VE_[ve])
                if sc:
                    pe.wait_ge(S("inverse_scalar"), 6 * n + SC_[sc])
                if po:
                    pe.wait_ge(S("inverse_pool"), 2 * n + PO_[po])

            def inv_a(n):
                need(n, ve="Qd")
                for u in range(4):
                    ins = nc.tensor.transpose(PS[:, 3, 128 * u:128 * u + 128], Qd[:, u, :], ident)
                ins.then_inc(S("inverse_products"), 1)

            def inv_b(n):
                need(n, sc="QT")
                pe.wait_ge(S("rwkv_bt"), n + 1)
                prod("Q2", 2, QdT, Qd)
                prod("QT2", 3, Qd, QdT)

            def inv_c(n):
                need(n, ve="QT2", sc="Q2")
                pe.wait_ge(S("rwkv_masked"), 4 * (n + 1))
                prod("Q4", 0, QT2, Q2)
                prod("QT4", 1, Q2, QT2)
                need(n, po="P1")
                prod("P2", 2, QT2, P1)

            def inv_d(n):
                need(n, ve="QT4", sc="Q4")
                prod("QT8", 3, Qd, QdT)
                need(n, ve="P2")
                prod("P3", 0, QdT, P2)

            def inv_e(n):
                need(n, ve="P3", sc="QT8")
                prod("D", 1, Q2, QT2)
                need(n, po="IQ")
                prod("DT", 2, QT2, P1)

            def inv_f(n):
                need(n, sc="DT")
                prod("NT", 3, Qm, QdT)

            def inv_g(n):
                need(n, sc="NT", ve="D")
                prod("H1", 0, Q2, Qd)

            def inv_h(n):
                need(n, ve="H1")
                prod("H2", 1, Q2, QT2)

            def inv_i(n):
                need(n, ve="H2")
                prod("H3", 2, Q2, P2)

            def walk_x(n, s):
                (cs, us), k = steps_of(n, s), 2 * n + s
                pe.wait_ge(S("rwkv_state"), k)
                if s == 0:
                    pe.wait_ge(S("rwkv_masked"), 4 * (n + 1))
                    pe.wait_ge(S("rwkv_alpha"), 4 * (n + 1))
                    pe.wait_ge(S("inverse_vector"), 12 * (n + 1))
                    pe.wait_ge(S("rwkv_state_in"), 4 * (n // 5 + 1))
                    pe.wait_ge(S("rwkv_values_staged"), 16 * (n // 5 + 1))
                    if n >= 0 and n % 5 == 4:
                        pe.wait_ge(S("rwkv_prompt_staged"), 8 * (n // 5 + 1))
                        pe.wait_ge(S("rwkv_prompt_zero"), 4 * (n // 5 + 1))
                for d in range(2):
                    for h in range(2):
                        ins = mm(PS[64 * h:64 * h + 64, 4, 64 * d:64 * d + 64], Ls[n % 2][:, h, us[d], :], SV[d][:, h, cs[d], :])
                ins.then_inc(S("rwkv_x_psum"), 1)

            def walk_u(n, s):
                (cs, us), k = steps_of(n, s), 2 * n + s
                pe.wait_ge(S("rwkv_x"), k + 1)
                for d in range(2):
                    ins = mm(PS[:, 5, 64 * d:64 * d + 64], TTs[n % 2][:, us[d], :], XS[:, d, :])
                ins.then_inc(S("rwkv_u_psum"), 1)

            def walk_s(n, s):
                (cs, us), k = steps_of(n, s), 2 * n + s
                pe.wait_ge(S("rwkv_u_a"), 2 * (k + 1))
                pe.wait_ge(S("rwkv_u_b"), 2 * (k + 1))
                for d in range(2):
                    for h in range(2):
                        ins = mm(PS[64 * h:64 * h + 64, 5, 128 + 64 * d:192 + 64 * d], BTs[n % 2][:, us[d], 64 * h:64 * h + 64],
                                 UV[d][:, h, cs[d], :])
                ins.then_inc(S("rwkv_s_psum"), 1)
                if s == 0 and before[0]:
                    evacuated(pe, before[0])
                for d in range(2):
                    for h in range(2):
                        r = slice(64 * h, 64 * h + 64)
                        out = PS[r, 6 + h, 64 * us[d]:64 * us[d] + 64]
                        mm(out, UV[d][:, h, cs[d], :], Rs[n % 2][:, h, us[d], :], start=True, stop=False)
                        ins = mm(out, SV[d][r, h, cs[d], :], ARD[d][r, cs[d], 64:128], start=False, stop=True)
                if s == 1:
                    ins.then_inc(S("rwkv_y_psum"), 1)
                    before[0] = ("y", n)

            for item in FIRST_ASIDE:
                side(item)
            inverse = dict(gram=gram, a=inv_a, b=inv_b, c=inv_c, d=inv_d, e=inv_e, f=inv_f, g=inv_g, h=inv_h, i=inv_i)
            for n in range(-1, NB):
                run_iteration(n, inverse, dict(x=walk_x, u=walk_u, s=walk_s), side)
            for item in LAST_ASIDE:
                side(item)

        def rwkv_act(act, step):
            def side(item):
                kind, q = item
                if kind in ("w0", "w1", "a0", "a1"):
                    w, d = "wa".index(kind[0]), int(kind[1])
                    if w == 1 and q:
                        act.wait_ge(S("rwkv_bonus_raw"), q)
                    if q:
                        act.wait_ge(S("rwkv_staged"), 5 * q)
                    act.wait_ge(S("rwkv_lora"), 4 * q + 2 * w + d + 1)
                    col = (R_W0, R_A0)[w] + 8 * d + q
                    A.activation((SW, AD)[w][d], pair(6), ACT.Sigmoid, bias=PC[:, 1, col:col + 1]).then_inc(S("rwkv_sig"), 1)
                elif kind == "k_sum":
                    k_square(q)
                    act.wait_ge(S("rwkv_k_max"), q + 1)
                    step(A.activation(RT, RT, ACT.Sqrt, scale=64.0))
                    step(A.activation(RT, RT, ACT.Ln))
                    A.activation(RT, RT, ACT.Exp, scale=-1.0).then_inc(S("rwkv_k_rs"), 1)
                elif kind == "state":
                    act.wait_ge(S("rwkv_state_psum"), q + 1)
                    for d in range(2):
                        for h in range(2):
                            r = slice(64 * h, 64 * h + 64)
                            A.activation(SV[d][r, h, 7 * d, :], PS[r, 6 + h, 64 * d:64 * d + 64], ACT.Copy)\
                                .then_inc(S("rwkv_state_in"), 1)
                elif kind == "final":
                    act.wait_ge(S("rwkv_final_psum"), q + 1)
                    if q:
                        act.wait_ge(S("rwkv_final_out"), 64 * q)
                    for h in range(2):
                        r = slice(64 * h, 64 * h + 64)
                        A.activation(STO[r, :, :].rearrange("p d k -> p (d k)"), PS[r, 6 + h, 0:128], ACT.Copy)\
                            .then_inc(S("rwkv_final"), 1)
                elif kind == "mean":
                    act.wait_ge(S("rwkv_centred"), q + 1)
                    A.activation(SQ, YC, ACT.Square).then_inc(S("rwkv_yc_square"), 1)
                elif kind == "var":
                    act.wait_ge(S("rwkv_var"), q + 1)
                    step(A.activation(RT, pair(6), ACT.Ln, bias=EPSC[:, 1:2]))
                    A.activation(RT, RT, ACT.Exp, scale=-0.5).then_inc(S("rwkv_y_rs"), 1)

            def k_square(q):
                act.wait_ge(S("rwkv_k_raw"), q + 1)
                A.activation(SQ, KKN, ACT.Square).then_inc(S("rwkv_k_square"), 1)

            def decays(q, i):
                act.wait_ge(S("rwkv_cum"), 2 * q + 2)
                if q:
                    act.wait_ge(S("rwkv_y_psum"), 5 * (q - 1) + i + 1)
                for d in range(2):
                    c = 2 * tile_of(i, d)
                    e = 63 if d == 0 else 0
                    for x0, src in ((0, SW[d]), (64, BC[d])):
                        ins = A.activation(ARD[d][:, c:c + 2, x0:x0 + 64], src.rearrange("p (c x) -> p c x", c=NCH)[:, c:c + 2, :],
                                           ACT.Exp, scale=-DECAY)
                    step(ins)
                    A.activation(PE_[:, q % 2, d, c:c + 2], ARD[d][:, c:c + 2, 64 + e], ACT.Copy)
                    x = BC[d][:, 64 * c:64 * c + 128]
                    step(A.activation(x, x, ACT.Exp, scale=DECAY))
                A.activation(DONE, EPSC[:, 0:1], ACT.Copy).then_inc(S("rwkv_decays"), 1)

            def values(q, part):
                for d, h, par in [(d, h, par) for d in range(2) for h in range(2) for par in range(2)][2 * part:2 * part + 2]:
                    src = RV[64 * par:64 * par + 64, 0:4, 128 * q + 64 * h:128 * q + 64 * h + 64]
                    row = slice(64, 128) if h == 0 else slice(0, 64)
                    A.activation(SV[d][row, h, par:8:2, :], src, ACT.Copy).then_inc(S("rwkv_values_staged"), 1)
                    A.activation(UV[d][64:128, h, par:8:2, :], src, ACT.Copy).then_inc(S("rwkv_values_staged"), 1)

            def prompt_values(q, part):
                if q:
                    act.wait_ge(S("rwkv_y_psum"), 5 * q)
                for h in (part,):
                    row = slice(64, 128) if h == 0 else slice(0, 64)
                    for par in range(2):
                        src = RV[64 * par:64 * par + 64, 4, 128 * q + 64 * h:128 * q + 64 * h + 64]
                        for d in range(2):
                            A.activation(SV[d][row, h, 8 + par, :], src, ACT.Copy)
                            A.activation(UV[d][64:128, h, 8 + par, :], src, ACT.Copy).then_inc(S("rwkv_prompt_staged"), 1)

            def ev(n, name, bank, dst):
                act.wait_ge(S("inverse_products"), 14 * n + PR_[name])
                A.activation(dst.rearrange("p u x -> p (u x)"), PS[:, bank, :], ACT.Copy).then_inc(S("inverse_scalar"), 1)

            def bt(n):
                act.wait_ge(S("rwkv_bk_turned"), n + 1)
                if n >= 2:
                    act.wait_ge(S("rwkv_s_psum"), 2 * (n - 1))
                A.activation(BTs[n % 2].rearrange("p u x -> p (u x)"), PS[:, 2, :], ACT.Copy).then_inc(S("rwkv_bt"), 1)

            def inv_c(n):
                act.wait_ge(S("inverse_pool"), 2 * n + PO_["P1"])
                ev(n, "Q4", 0, Qd)

            def inv_d(n):
                act.wait_ge(S("inverse_products"), 14 * n + PR_["P2"])
                ev(n, "QT8", 3, Q2)

            def walk_x(n, s):
                k = 2 * n + s
                act.wait_ge(S("rwkv_x_psum"), k + 1)
                A.activation(XS.rearrange("p d v -> p (d v)"), PS[:, 4, 0:128], ACT.Copy).then_inc(S("rwkv_x"), 1)

            def walk_u(n, s):
                (cs, us), k = steps_of(n, s), 2 * n + s
                act.wait_ge(S("rwkv_u_psum"), k + 1)
                for d in range(2):
                    A.activation(UV[d][0:64, 0, cs[d], :], PS[0:64, 5, 64 * d:64 * d + 64], ACT.Copy).then_inc(S("rwkv_u_a"), 1)

            def walk_y(n, s):
                if s == 0:
                    return
                act.wait_ge(S("rwkv_y_psum"), n + 1)
                if n >= 5:
                    act.wait_ge(S("rwkv_ysum"), n // 5)
                for d in range(2):
                    t = tile_of(n % 5, d)
                    for h in range(2):
                        r = slice(64 * h, 64 * h + 64)
                        A.activation(YD[d][r, 128 * t:128 * t + 128], PS[r, 6 + h, 128 * d:128 * d + 128], ACT.Copy)\
                            .then_inc(S("rwkv_y"), 1)

            for item in FIRST_ASIDE:
                side(item)
            for i in range(4):
                decays(0, i)
            for part in range(4):
                values(0, part)
            inverse = dict(gram=bt, a=lambda m: ev(m, "QT", 3, QdT), b=lambda m: ev(m, "Q2", 2, Q2), c=inv_c, d=inv_d,
                           e=lambda m: ev(m, "DT", 2, QdT), f=lambda m: ev(m, "NT", 3, Q2))
            def inner(f, *args):
                return lambda p: f(p + 1, *args) if p < 7 else None

            more = {(0, "m0"): [lambda p: decays(p, 4)],
                    (1, "m2"): [lambda p: prompt_values(p, 0)], (1, "m3"): [lambda p: prompt_values(p, 1)],
                    (3, "m2"): [inner(decays, 0)],
                    (4, "m1"): [inner(decays, 1)], (4, "m2"): [inner(decays, 2)], (4, "m3"): [inner(decays, 3)],
                    (4, "m4"): [lambda p: act.wait_ge(S("rwkv_y_psum"), 5 * p + 4),
                                inner(values, 0), inner(values, 1), inner(values, 2), inner(values, 3)]}
            for n in range(-1, NB):
                run_iteration(n, inverse, dict(x=walk_x, u=walk_u, s=walk_y), side, more)
            for item in LAST_ASIDE:
                side(item)

        def rwkv_dve(dve, step):
            inv = S("inverse_vector")
            lo, hi, al = slice(0, 64), slice(64, 128), slice(0, 128)
            f = lambda x: x.rearrange("p u x -> p (u x)")
            bd = con(C_BD16).unsqueeze(1).broadcast_to([P, 4, 128])
            oka = SML[:, 16:17]

            def pcol(row, q):
                return PC[:, 1, row + q:row + q + 1]

            def cum(q, d):
                dve.wait_ge(S("rwkv_sig"), 4 * q + d + 1)
                m = CON[:, C_SCAN:C_SCAN + T] if d == 0 else CON[:, C_SCAN + T:C_SCAN:-1]
                x, y = (SW[d], BC[d]) if d == 0 else (SW[d][:, ::-1], BC[d][:, ::-1])
                step(V.tensor_tensor_scan(y, m, x, 0.0, ALU.mult, ALU.add))
                V.tensor_tensor(SW[d], BC[d], SW[d], ALU.subtract).then_inc(S("rwkv_cum"), 1)

            def k_raw(q):
                if q:
                    dve.wait_ge(S("rwkv_staged"), 5 * q)
                V.tensor_scalar(KKN, K[:, q, :], pcol(R_KK, q), None, ALU.mult).then_inc(S("rwkv_k_raw"), 1)

            def k_max(q):
                dve.wait_ge(S("rwkv_k_sum"), q + 1)
                V.tensor_scalar(RT, pair(6), 1e-24 / 64, None, ALU.max).then_inc(S("rwkv_k_max"), 1)

            def keys(q, part):
                if part == 0:
                    step(V.tensor_scalar(oka, pcol(R_KA, q), -1.0, 1.0, ALU.mult, ALU.add))
                    dve.wait_ge(S("rwkv_k_rs"), q + 1)
                    step(V.tensor_tensor(KKN, KKN, RT, ALU.mult))
                    dve.wait_ge(S("rwkv_sig"), 4 * q + 4)
                    for d in range(2):
                        V.tensor_tensor((SQ, RT)[d], KKN, AD[d], ALU.mult)
                else:
                    for d in range(2):
                        step(V.tensor_scalar(AD[d], AD[d], pcol(R_KA, q), oka, ALU.mult, ALU.add))
                    for d in range(2):
                        step(V.tensor_tensor(AD[d], AD[d], K[:, q, :], ALU.mult))

            def staging(q, i):
                dve.wait_ge(S("rwkv_decays"), 5 * q + i + 1)
                for d in range(2):
                    c = 2 * tile_of(i, d)
                    sl, t = slice(c, c + 2), slice(64 * c, 64 * c + 128)
                    v3 = lambda x: x[:, t].rearrange("p (c x) -> p c x", c=2)
                    rr, aa = ARD[d][:, sl, 64:128], ARD[d][:, sl, 0:64]
                    V.tensor_tensor(rr, rr, v3(R[:, q, :]), ALU.mult)
                    V.scalar_tensor_tensor(aa, aa, -1.0, v3(KKN), ALU.mult, ALU.mult)
                    V.tensor_tensor(BKD[d][:, sl, 0:64], v3((SQ, RT)[d]), v3(BC[d]), ALU.mult)
                    ins = V.tensor_tensor(BKD[d][:, sl, 64:128], v3(AD[d]), v3(BC[d]), ALU.mult)
                ins.then_inc(S("rwkv_staged"), 1)

            def gram(n):
                dve.wait_ge(S("rwkv_gram"), n + 1)
                if n:
                    dve.wait_ge(S("inverse_products"), 14 * n)
                V.tensor_tensor(o4(Qm[lo, :, 0:64]), g4(0, lo, 0), m4(lo, 0), ALU.mult).then_inc(inv, 1)
                V.tensor_tensor(o4(Qm[hi, :, 64:128]), g4(1, lo, 0), m4(lo, 0), ALU.mult).then_inc(inv, 1)
                dve.wait_ge(inv, 12 * n + VE_["QB"])
                V.tensor_tensor(Qd, Qm, bd, ALU.mult).then_inc(inv, 1)
                dve.wait_ge(inv, 12 * n + VE_["Qd"])
                V.tensor_tensor(Qm, Qm, Qd, ALU.subtract).then_inc(inv, 1)

            def g4(bank, rows, c0):
                x = PS[rows, bank, :].rearrange("p (d h x) -> p d h x", d=2, h=2)
                return x[:, :, :, c0:c0 + 64]

            def m4(rows, c0):
                x = CON[rows, C_RWKV:C_RWKV + 256].rearrange("p (d x) -> p d x", d=2)[:, :, c0:c0 + 64]
                return x.unsqueeze(2).broadcast_to([rows.stop - rows.start, 2, 2, 64])

            def o4(x):
                return x.rearrange("p (d h) x -> p d h x", d=2)

            def masks(n):
                Lm, Rm, msk = Ls[n % 2], Rs[n % 2], S("rwkv_masked")
                if n >= 2:
                    dve.wait_ge(S("rwkv_y_psum"), n - 1)
                V.tensor_tensor(o4(Lm[hi, 0, :, :]), g4(0, hi, 0), m4(hi, 0), ALU.mult).then_inc(msk, 1)
                V.tensor_tensor(o4(Lm[lo, 1, :, :]), g4(1, hi, 0), m4(hi, 0), ALU.mult).then_inc(msk, 1)
                V.tensor_tensor(o4(Rm[:, 0, :, :]), g4(0, al, 64), m4(al, 64), ALU.mult).then_inc(msk, 1)
                V.tensor_tensor(o4(Rm[:, 1, :, :]), g4(1, al, 64), m4(al, 64), ALU.mult).then_inc(msk, 1)

            def ev(n, name, bank, dst, plus=None, mine=None):
                dve.wait_ge(S("inverse_products"), 14 * n + PR_[name])
                if mine:
                    dve.wait_ge(inv, 12 * n + VE_[mine])
                if plus is None:
                    ins = V.tensor_copy(f(dst), PS[:, bank, :])
                else:
                    ins = V.tensor_tensor(f(dst), PS[:, bank, :], f(plus), ALU.add)
                ins.then_inc(inv, 1)

            def inv_b(n):
                ev(n, "QT2", 3, QT2)

            def inv_c(n):
                ev(n, "QT4", 1, QdT)
                dve.wait_ge(S("inverse_pool"), 2 * n + PO_["P1"])
                ev(n, "P2", 2, P2, P1)

            def inv_d(n):
                ev(n, "P3", 0, QT2, P2, "P2")

            def inv_e(n):
                ev(n, "D", 1, Qd, QT2, "P3")

            def inv_g(n):
                dve.wait_ge(S("inverse_products"), 14 * n + PR_["DT"])
                ev(n, "H1", 0, QT2, Qd, "D")

            def inv_h(n):
                ev(n, "H2", 1, P2, Qd)

            def inv_i(n):
                ev(n, "H3", 2, TTs[n % 2], Qd)

            def walk_u(n, s):
                (cs, us), k = steps_of(n, s), 2 * n + s
                dve.wait_ge(S("rwkv_u_psum"), k + 1)
                for d in range(2):
                    V.tensor_copy(UV[d][0:64, 1, cs[d], :], PS[64:128, 5, 64 * d:64 * d + 64]).then_inc(S("rwkv_u_b"), 1)

            def walk_s(n, s):
                (cs, us), k = steps_of(n, s), 2 * n + s
                dve.wait_ge(S("rwkv_s_psum"), k + 1)
                dve.wait_ge(S("rwkv_s2"), 4 * (k + 1))
                for d in range(2):
                    nxt = {7: None, 9: 10}.get(cs[d], cs[d] + 1) if d == 0 else {0: None, 8: 10}.get(cs[d], cs[d] - 1)
                    for h in range(2):
                        r = slice(64 * h, 64 * h + 64)
                        if nxt is None:
                            continue
                        V.scalar_tensor_tensor(SV[d][r, h, nxt, :], PS[r, 5, 128 + 64 * d:192 + 64 * d],
                                               PE_[r, (n // 5) % 2, d, cs[d]:cs[d] + 1], S2[r, d, :], ALU.mult, ALU.add)
                V.memset(SML[:, 18:19], 0.0).then_inc(S("rwkv_state"), 1)

            def side(item):
                kind, q = item
                if kind == "k_sum":
                    k_max(q)
                elif kind == "mean":
                    dve.wait_ge(S("rwkv_mean"), q + 1)
                    V.tensor_tensor(YC, YS, pair(6), ALU.subtract).then_inc(S("rwkv_centred"), 1)
                elif kind == "gate":
                    dve.wait_ge(S("rwkv_gate"), q + 1)
                    V.tensor_tensor(R[:, q, :], YC, pair(6), ALU.mult).then_inc(S("rwkv_pair_done"), 1)
                elif kind == "bonus":
                    dve.wait_ge(S("rwkv_bonus_psum"), q + 1)
                    V.tensor_scalar(BN, pair(6), 64.0, None, ALU.mult).then_inc(S("rwkv_bonus"), 1)
                elif kind == "values":
                    dve.wait_ge(S("rwkv_bonus"), q + 1)
                    dve.wait_ge(S("rwkv_values_psum"), q + 1)
                    V.tensor_tensor(BN, BN, pair(6), ALU.mult).then_inc(S("rwkv_bonus_v"), 1)

            def y_sum(q):
                dve.wait_ge(S("rwkv_y"), 4 * (5 * q + 5))
                if q < 7:
                    dve.wait_ge(S("rwkv_staged"), 5 * (q + 2))
                V.tensor_tensor(YS, YD[0], YD[1], ALU.add).then_inc(S("rwkv_ysum"), 1)
                dve.wait_ge(S("rwkv_ysum"), q + 1)

            def y_norm(q):
                dve.wait_ge(S("rwkv_y_rs"), q + 1)
                dve.wait_ge(S("rwkv_centred"), q + 1)
                step(V.tensor_tensor(YC, YC, RT, ALU.mult))
                step(V.tensor_scalar(YC, YC, pcol(R_LNW, q), pcol(R_LNB, q), ALU.mult, ALU.add))
                dve.wait_ge(S("rwkv_bonus_v"), q + 1)
                step(V.tensor_tensor(YC, YC, BN, ALU.add))

            def bonus_raw(q):
                step(V.tensor_tensor(BN, AD[0], AD[1], ALU.add))
                V.scalar_tensor_tensor(BN, BN, pcol(R_RK, q), R[:, q, :], ALU.mult, ALU.mult).then_inc(S("rwkv_bonus_raw"), 1)

            step(V.memset(Qm, 0.0))
            k_raw(0)
            cum(0, 0)
            cum(0, 1)
            k_max(0)
            keys(0, 0)
            keys(0, 1)
            for i in range(4):
                staging(0, i)
            inverse = dict(gram=gram, a=masks, b=inv_b, c=inv_c, d=inv_d, e=inv_e, g=inv_g, h=inv_h, i=inv_i)
            def inner(f, *args):
                return lambda p: f(p + 1, *args) if p < 7 else None

            more = {(0, "m1"): [lambda p: staging(p, 4), lambda p: y_sum(p - 1) if p else None],
                    (1, "m0"): [lambda p: y_norm(p - 1) if p else None],
                    (1, "m1"): [inner(k_raw)], (1, "m3"): [bonus_raw],
                    (2, "m1"): [inner(cum, 0)], (2, "m2"): [inner(cum, 1)],
                    (3, "m1"): [inner(keys, 0)], (3, "m2"): [inner(keys, 1)], (3, "m3"): [inner(staging, 0)],
                    (4, "m1"): [inner(staging, 1)], (4, "m2"): [inner(staging, 2)], (4, "m3"): [inner(staging, 3)]}
            for n in range(-1, NB):
                run_iteration(n, inverse, dict(u=walk_u, s=walk_s), side, more)
            y_sum(7)
            side(("mean", 7))
            y_norm(7)
            side(("gate", 7))

        def rwkv_pool(pool, step):
            idb = ident.unsqueeze(1).broadcast_to([P, 4, 128])

            def prompt_zero(q):
                if q:
                    pool.wait_ge(S("rwkv_y_psum"), 5 * q)
                for d in range(2):
                    for h in range(2):
                        G.memset(SV[d][64 * h:64 * h + 64, h, 8 + d, :], 0.0).then_inc(S("rwkv_prompt_zero"), 1)
                        pool.wait_ge(S("rwkv_prompt_zero"), 4 * q + 2 * d + h + 1)

            def s2(n, s):
                (cs, us), k = steps_of(n, s), 2 * n + s
                pool.wait_ge(S("rwkv_state"), k)
                pool.wait_ge(S("rwkv_state_in"), 4 * (n // 5 + 1))
                if n % 5 == 4:
                    pool.wait_ge(S("rwkv_prompt_zero"), 4 * (n // 5 + 1))
                for d in range(2):
                    for h in range(2):
                        r = slice(64 * h, 64 * h + 64)
                        G.tensor_scalar(S2[r, d, :], SV[d][r, h, cs[d], :], PE_[r, (n // 5) % 2, d, cs[d]:cs[d] + 1], None, ALU.mult)\
                            .then_inc(S("rwkv_s2"), 1)
                        pool.wait_ge(S("rwkv_s2"), 4 * k + 2 * d + h + 1)

            def start(n):
                pool.wait_ge(S("inverse_vector"), 12 * n + VE_["Qd"])
                if n:
                    pool.wait_ge(S("inverse_products"), 14 * n)
                G.tensor_tensor(P1, Qd, idb, ALU.add).then_inc(S("inverse_pool"), 1)
                pool.wait_ge(S("inverse_pool"), 2 * n + 1)
                for d in range(2):
                    c = 2 * tile_of(n % 5, d)
                    for h in range(2):
                        r = slice(64 * h, 64 * h + 64)
                        G.tensor_copy(Ls[n % 2][r, h, 2 * d:2 * d + 2, :], ARD[d][r, c:c + 2, 0:64]).then_inc(S("rwkv_alpha"), 1)
                        pool.wait_ge(S("rwkv_alpha"), 4 * n + 2 * d + h + 1)

            def iq(n):
                pool.wait_ge(S("inverse_scalar"), 6 * n + SC_["QT8"])
                pool.wait_ge(S("inverse_vector"), 12 * n + VE_["P2"])
                G.tensor_tensor(P1, Q2, idb, ALU.add).then_inc(S("inverse_pool"), 1)
                pool.wait_ge(S("inverse_pool"), 2 * n + 2)

            prompt_zero(0)
            for n in range(-1, NB):
                p, i = n // 5, n % 5
                if i == 1 and p > 0:
                    prompt_zero(p)
                run_iteration(n, dict(gram=start, e=iq), dict(x=s2), None if n < 0 else (lambda item: None))

        def rwkv_sp(sp):
            for q in range(10):
                c = slice(128 * q, 128 * q + 128)
                if q < 8:
                    if q:
                        sp.wait_ge(S("rwkv_sig"), 4 * q)
                        sp.wait_ge(S("rwkv_state_psum"), q)
                    for w, n in enumerate(("rwkv_w2", "rwkv_a2")):
                        sp.dma_start(LW[:, w, :], a[n][0, :, :, c].rearrange("d k n -> (d k) n")).then_inc(S("rwkv_weights"), 16)
                    for d, n in enumerate(("state_rwkv_fwd", "state_rwkv_bwd")):
                        sp.dma_start(STL[:, d, :], a[n][0, 0, 2 * q:2 * q + 2].rearrange("h v k -> (h v) k"))\
                            .then_inc(S("rwkv_weights"), 16)
                if q >= 2:
                    p = q - 2
                    sp.wait_ge(S("rwkv_final"), 2 * (p + 1))
                    for d in range(2):
                        for h in range(2):
                            r = slice(64 * h, 64 * h + 64)
                            sp.dma_start(o["rwkv"][d][0, 0, 2 * p + h], STO[r, d, :]).then_inc(S("rwkv_final_out"), 16)
                if q < 8:
                    if q >= 2:
                        sp.wait_ge(S("rwkv_pair_done"), q - 1)
                    sp.dma_start(G2[:, q % 2, :], a["rwkv_g2"][0, :, c]).then_inc(S("rwkv_gate_weights"), 16)

        XROWS = flat(16 * T, TT_ * D).rearrange("p (t d) -> p t d", t=TT_)
        PROWS = flat(U_S * T, 3 * 128).rearrange("p (w c) -> p w c", w=3)

        def load_all(sp):
            sp.dma_start(con(0, C_END), a["constants"]).then_inc(S("const_loaded"), 16)
            rows = [(0, R_ADAB, a["ada_b"].rearrange("l (r p) -> (l r) p", p=P), 96),
                    (0, R_N1, a["norm1_w"].rearrange("l (r p) -> (l r) p", p=P), 16),
                    (0, R_N2, a["norm2_w"].rearrange("l (r p) -> (l r) p", p=P), 16),
                    (1, R_MIX, a["rwkv_mix"].rearrange("o i (r p) -> (o i r) p", p=P), 48),
                    (1, R_W0, a["rwkv_w0"].rearrange("o i (r p) -> (o i r) p", p=P), 16),
                    (1, R_A0, a["rwkv_a0"].rearrange("o i (r p) -> (o i r) p", p=P), 16),
                    (1, R_KK, a["rwkv_k_k"].rearrange("o (r p) -> (o r) p", p=P), 8),
                    (1, R_KA, a["rwkv_k_a"].rearrange("o (r p) -> (o r) p", p=P), 8),
                    (1, R_RK, a["rwkv_r_k"].rearrange("o (r h) n -> (o r) (h n)", h=2), 8),
                    (1, R_LNW, a["rwkv_ln_w"].rearrange("o (r p) -> (o r) p", p=P), 8),
                    (1, R_LNB, a["rwkv_ln_b"].rearrange("o (r p) -> (o r) p", p=P), 8),
                    (2, R_C, a["c"].rearrange("o (r p) -> (o r) p", p=P), 8),
                    (2, R_C + 8, a["c_ctx"].rearrange("(r p) -> r p", p=P), 8),
                    (2, R_LB, a["hgrn_lb"].rearrange("o (r p) -> (o r) p", p=P), 8)]
            for w, r, src, n in rows:
                sp.dma_start(PROWS[r:r + n, w, :], src).then_inc(S("rows_loaded"), 16)
            for r, name in ((R_QN, "attn_q_norm"), (R_KN, "attn_k_norm"), (R_GN, "hgrn_g_norm")):
                for h in range(2):
                    sp.dma_start(PROWS[r:r + 1, 2, 64 * h:64 * h + 64], a[name]).then_inc(S("rows_loaded"), 16)
            sp.dma_start(XROWS[:, 0:4, :], a["x_sample"][0].rearrange("(t p) d -> p t d", p=P)).then_inc(S("x_loaded"), 16)
            sp.dma_start(XROWS[:, 4, :], a["x_prompt"][0]).then_inc(S("x_loaded"), 16)
        ROWS = 16 * 20

        def setup_pe(pe):
            pe.wait_ge(S("const_loaded"), 16)
            pe.wait_ge(S("rows_loaded"), ROWS)
            for w, n in enumerate((P, R1, R2)):
                ins = nc.tensor.transpose(PS[:, 7, 128 * w:128 * w + n], PROWS[0:n, w, :], ident[0:n, 0:n])
            ins.then_inc(S("params_psum"), 1)
            pe.wait_ge(S("x_loaded"), 32)
            for k in range(KT):
                b = 2 * (k % 2)
                if k >= 2:
                    pe.wait_ge(S("x_in"), k - 1)
                for t in range(TT_):
                    ins = nc.tensor.transpose(pair(b)[:, 128 * t:128 * t + 128], XROWS[:, t, 128 * k:128 * k + 128], ident)
                ins.then_inc(S("x_turned"), 1)

        def setup_act(act, step):
            act.wait_ge(S("params"), 3)
            c = PC[:, 2, R_C:R_C + 16].rearrange("p (g k) -> p g k", g=2)
            A.activation(SC, c, ACT.Sigmoid).then_inc(S("sig_c"), 1)
            act.wait_ge(S("lb_max"), 1)
            step(A.activation(LB[:, 0, :], LB[:, 2, :], ACT.Exp))
            A.activation(LB[:, 1, :], LB[:, 3, :], ACT.Exp).then_inc(S("lb_exp"), 1)
            for k in range(KT):
                act.wait_ge(S("x_turned"), k + 1)
                A.activation(unit(U_X + k), pair(2 * (k % 2)), ACT.Copy).then_inc(S("x_in"), 1)

        def setup_dve(dve, step):
            step(V.memset(EPSC[:, 0:1], EPS))
            step(V.memset(EPSC[:, 1:2], LN_X_EPS))
            dve.wait_ge(S("params_psum"), 1)
            for w, n in enumerate((P, R1, R2)):
                V.tensor_copy(PC[:, w, 0:n], PS[:, 7, 128 * w:128 * w + n]).then_inc(S("params"), 1)
            dve.wait_ge(S("params"), 3)
            l0, l1 = PC[:, 2, R_LB:R_LB + 4], PC[:, 2, R_LB + 4:R_LB + 8]
            step(V.tensor_tensor(LB[:, 4, :], l0, l1, ALU.max))
            V.tensor_tensor(LB[:, 2, :], l0, LB[:, 4, :], ALU.subtract)
            V.tensor_tensor(LB[:, 3, :], l1, LB[:, 4, :], ALU.subtract).then_inc(S("lb_max"), 1)
            dve.wait_ge(S("sig_c"), 1)
            c = PC[:, 2, R_C:R_C + 16].rearrange("p (g k) -> p g k", g=2)
            step(V.memset(SCW, 0.0))
            step(V.tensor_tensor(SCW[:, :, 0:2].rearrange("p k g -> p g k"), SC, c, ALU.mult))
            dve.wait_ge(S("lb_exp"), 1)
            step(V.tensor_tensor(LB[:, 1, :], LB[:, 0, :], LB[:, 1, :], ALU.add))
            step(V.reciprocal(LB[:, 1, :], LB[:, 1, :]))
            step(V.tensor_tensor(LB[:, 4, :], LB[:, 0, :], LB[:, 1, :], ALU.mult))
            step(V.tensor_scalar(LB[:, 5, :], LB[:, 4, :], -1.0, 1.0, ALU.mult, ALU.add))

        def out_pe(pe):
            for t in range(TT_):
                for b in range(2):
                    i = 2 * t + b
                    if i >= 2:
                        pe.wait_ge(S("rows_out"), i - 1)
                    for k in range(4):
                        ins = nc.tensor.transpose(PS[:, b, 128 * k:128 * k + 128],
                                                  unit(U_X + 4 * b + k)[:, 128 * t:128 * t + 128], ident)
                    ins.then_inc(S("rows_turned"), 1)

        def out_act(act):
            for i in range(2 * TT_):
                act.wait_ge(S("rows_turned"), i + 1)
                A.activation(XROWS[:, i // 2, 512 * (i % 2):512 * (i % 2) + 512], PS[:, i % 2, :], ACT.Copy)\
                    .then_inc(S("rows_out"), 1)

        def out_sp(sp):
            for t in range(TT_):
                sp.wait_ge(S("rows_out"), 2 * t + 2)
                dst = o["y_sample"][0, 128 * t:128 * t + 128] if t < 4 else o["y_prompt"][0]
                sp.dma_start(dst, XROWS[:, t, :]).then_inc(S("y_stored"), 16)
            sp.wait_ge(S("y_stored"), 16 * TT_)
            for q in range(2):
                sp.wait_ge(S(f"hgrn_final_out{q}"), 2 * 32)
            sp.wait_ge(S("rwkv_final_out"), 8 * 64)
            sp.wait_ge(S("kv_stored"), 32)

        block = ctx.enter_context(nc.Block())

        @block.sync
        def _(sp):
            load_all(sp)
            load_blocks(sp, "ada0")
            load_blocks(sp, "in")
            sp.wait_ge(S("stage_done"), 4 * 3)
            sp.dma_start(flat((U_S + 4) * T, 2 * NS), a["rope"]).then_inc(S("rope_loaded"), 16)
            sp.dma_start(CK[:, 0, :], a["cache_attn_k"][0, 0].rearrange("t h c -> t (h c)")).then_inc(S("cache_loaded"), 16)
            sp.dma_start(CK[:, 1, :], a["cache_attn_v"][0, 0].rearrange("t h c -> t (h c)")).then_inc(S("cache_loaded"), 16)
            sp.wait_ge(S("key_out"), 1)
            sp.dma_start(o["k"][0, 0].rearrange("t h c -> t (h c)"), KOUT).then_inc(S("kv_stored"), 16)
            sp.dma_start(o["v"][0, 0].rearrange("t h c -> t (h c)"), VA[:, 4, :]).then_inc(S("kv_stored"), 16)
            load_blocks(sp, "ada1")
            sp.wait_ge(S("kv_stored"), 32)
            sp.wait_ge(S("stage_done"), 4 * 5)
            hgrn_sp(sp)
            sp.wait_ge(S("stage_done"), 4 * 6)
            mlp_sp(sp, 0)
            sp.wait_ge(S("stage_done"), 4 * 8)
            load_blocks(sp, "proj")
            sp.wait_ge(S("stage_done"), 4 * 9)
            rwkv_sp(sp)
            sp.wait_ge(S("stage_done"), 4 * 10)
            load_blocks(sp, "out1")
            sp.wait_ge(S("rwkv_final_out"), 8 * 64)
            mlp_sp(sp, 1)
            out_sp(sp)

        def act_h(i, k):
            return unit(U_H + k)

        @block.tensor
        def _(pe):
            setup_pe(pe)
            stage_end(pe, "pe")
            ada_pe(pe, 0)
            stage_end(pe, "pe")
            norm_pe(pe, 0)
            products(pe, "in", act_h, each=lambda i, k: pe.wait_ge(S("norm_out"), k + 1))
            stage_end(pe, "pe")
            attn_prep_pe(pe)
            stage_end(pe, "pe")
            attn_pe(pe)
            stage_end(pe, "pe")
            hgrn_pe(pe)
            stage_end(pe, "pe")
            products(pe, "out0", lambda i, k: unit(U_MIX + k))
            stage_end(pe, "pe")
            norm_pe(pe, 1)
            mlp_pe(pe, 0)
            stage_end(pe, "pe")
            norm_pe(pe, 2)
            products(pe, "proj", lambda i, k: XI[stage_of_block(i) % 2][:, k, :],
                     each=lambda i, k: pe.wait_ge(S("mixed_input"), KT * stage_of_block(i) + k + 1))
            stage_end(pe, "pe")
            rwkv_pe(pe)
            stage_end(pe, "pe")
            products(pe, "out1", lambda i, k: unit(U_R + k))
            stage_end(pe, "pe")
            norm_pe(pe, 3)
            mlp_pe(pe, 1)
            stage_end(pe, "pe")
            out_pe(pe)

        @block.vector
        def _(dve):
            step = Steps(dve, "vector_step")
            setup_dve(dve, step)
            stage_end(dve, "dve")
            ada_dve(dve, step, 0)
            stage_end(dve, "dve")
            norm_dve(dve, 0)
            stage_end(dve, "dve")
            attn_prep_dve(dve, step)
            stage_end(dve, "dve")
            attn_dve(dve, step)
            stage_end(dve, "dve")
            hgrn_dve(dve, step)
            stage_end(dve, "dve")
            residual_dve(dve, "out0", 16)
            stage_end(dve, "dve")
            mlp_first_block(dve, 0)
            norm_dve(dve, 1)
            mlp_dve(dve, step, 0)
            stage_end(dve, "dve")
            norm_dve(dve, 2)
            proj_dve(dve, step)
            stage_end(dve, "dve")
            rwkv_dve(dve, step)
            stage_end(dve, "dve")
            residual_dve(dve, "out1", 16)
            stage_end(dve, "dve")
            mlp_first_block(dve, 1)
            norm_dve(dve, 3)
            mlp_dve(dve, step, 1)
            stage_end(dve, "dve")

        @block.scalar
        def _(act):
            step = Steps(act, "scalar_step")
            setup_act(act, step)
            stage_end(act, "act")
            for b in range(12):
                ada_act(act, 0, b)
                if b:
                    ada_cols_act(act, 0, b - 1)
            ada_cols_act(act, 0, 11)
            stage_end(act, "act")
            norm_act(act, step, 0, 0)
            evac_act(act, "in", lambda u: ACT.Sigmoid if U_F <= u < U_F + 8 else ACT.Copy,
                     lambda kind, j, t: (VB[:, t, :], 512) if kind == "tm" else (VA[:, t, :], 128))
            stage_end(act, "act")
            attn_prep_act(act, step)
            stage_end(act, "act")
            attn_act(act)
            stage_end(act, "act")
            hgrn_act(act, step)
            stage_end(act, "act")
            stage_end(act, "act")
            norm_act(act, step, 1, 1)
            mlp_act(act, 0)
            stage_end(act, "act")
            norm_act(act, step, 2, 0)
            evac_act(act, "proj", lambda u: {U_MID: ACT.Tanh, U_MID + 2: ACT.Sigmoid}.get(u, ACT.Copy),
                     lambda kind, j, t: (RV[:, t, 512 * j:512 * j + 512], 512))
            stage_end(act, "act")
            rwkv_act(act, step)
            stage_end(act, "act")
            stage_end(act, "act")
            norm_act(act, step, 3, 1)
            mlp_act(act, 1)
            stage_end(act, "act")
            out_act(act)

        @block.gpsimd
        def _(pool):
            step = Steps(pool, "pool_step")
            for i in range(5):
                stage_end(pool, "pool")
            hgrn_pool(pool)
            for i in range(4):
                stage_end(pool, "pool")
            rwkv_pool(pool, step)
            for i in range(3):
                stage_end(pool, "pool")


_IN = ["x_prompt", "x_sample", "cache_attn_k", "cache_attn_v", "state_hgrn_fwd", "state_hgrn_bwd", "state_rwkv_fwd",
       "state_rwkv_bwd", "c", "c_ctx", "ada_w", "ada_b", "norm1_w", "norm2_w", "ab_w_in", "ab_w_out", "attn_q_norm",
       "attn_k_norm", "hgrn_lb", "hgrn_g_norm", "rwkv_mix", "rwkv_wr", "rwkv_wk", "rwkv_wv", "rwkv_wo", "rwkv_w0",
       "rwkv_w1", "rwkv_w2", "rwkv_a0", "rwkv_a1", "rwkv_a2", "rwkv_g1", "rwkv_g2", "rwkv_k_k", "rwkv_k_a", "rwkv_r_k",
       "rwkv_ln_w", "rwkv_ln_b", "mlp_w1", "mlp_w2"]
_OUT = [("y_prompt", (1, 128, 1024)), ("y_sample", (1, 512, 1024)), ("new_attn_k", (1, 1, 128, 2, 64)),
        ("new_attn_v", (1, 1, 128, 2, 64)), ("new_hgrn_fwd", (1, 1, 8, 64, 64)), ("new_hgrn_bwd", (1, 1, 8, 64, 64)),
        ("new_rwkv_fwd", (1, 1, 16, 64, 64)), ("new_rwkv_bwd", (1, 1, 16, 64, 64))]


def kernel(**inputs):
    import concourse.bacc as bacc
    from concourse.bass_utils import run_bass_kernel_spmd as run

    nc = bacc.Bacc("TRN2", target_bir_lowering=False, num_devices=1)
    arrays = {n: np.ascontiguousarray(inputs[n]) for n in _IN}
    arrays["constants"] = constants()
    arrays["rope"] = rope_tables()
    arrays = {"in_" + n: v for n, v in arrays.items()}
    a = {n[3:]: nc.dram_tensor(n, v.shape, F32, kind="ExternalInput").ap() for n, v in arrays.items()}
    outs = {n: nc.dram_tensor("out_" + n, s, F32, kind="ExternalOutput").ap() for n, s in _OUT}
    o = {"y_prompt": outs["y_prompt"], "y_sample": outs["y_sample"], "k": outs["new_attn_k"], "v": outs["new_attn_v"],
         "hgrn": (outs["new_hgrn_fwd"], outs["new_hgrn_bwd"]), "rwkv": (outs["new_rwkv_fwd"], outs["new_rwkv_bwd"])}
    program(nc, a, o)
    r = run(nc, [arrays], core_ids=[0])
    return tuple(r.results[0]["out_" + n] for n, _ in _OUT)
```
